# Optimizing a Trainium2 kernel written in Bass

```python
import jax, jax.numpy as jnp
from jax import lax
import numpy as np

D_MODEL = 1024
BATCH = 1
SEQ = 1024
DEPTH = 2
DEC_BATCH = 8
DEC_SEQ = 16
PAST_LEN = 1024

CHUNK = 64
EPS = 1e-6
N_EVEN = (DEPTH + 1) // 2
N_ODD = DEPTH // 2

A_HEADS = 4
A_EXPAND = 128
A_HEAD_DIM = D_MODEL // 8
A_KEY_WIDTH = A_HEADS * A_EXPAND
A_WIDTH = A_HEADS * A_HEAD_DIM
POOL_WINDOWS = (2, 4, 8, 16)
B_GROUPS = len(POOL_WINDOWS)
B_GROUP_DIM = D_MODEL // 8
B_WIDTH = B_GROUPS * B_GROUP_DIM
POOL_HIST = max(POOL_WINDOWS) - 1
AB_IN = 2 * A_KEY_WIDTH + 2 * A_WIDTH + B_WIDTH
AB_OUT = A_WIDTH + B_WIDTH
C_BLOCK = 128
C_GROUPS = 8
C_WIDTH = 2 * D_MODEL
C_GROUP_DIM = C_WIDTH // C_GROUPS
D_FF = 2816
CONV_W = 3

kernel_name = "hgrn2_pool_cmlp_streaming_step"

def rms_norm(x, gain):
    xf = x.astype(jnp.float32)
    y = xf * lax.rsqrt(jnp.mean(xf * xf, axis=-1, keepdims=True) + EPS)
    return (y * gain.astype(jnp.float32)).astype(x.dtype)

def layer_norm(x, gain, bias):
    xf = x.astype(jnp.float32)
    mu = jnp.mean(xf, axis=-1, keepdims=True)
    xc = xf - mu
    y = xc * lax.rsqrt(jnp.mean(xc * xc, axis=-1, keepdims=True) + EPS)
    return (y * gain.astype(jnp.float32) + bias.astype(jnp.float32)).astype(x.dtype)

def hgrn_lower_bounds(lb_logits):
    p = jax.nn.softmax(lb_logits.astype(jnp.float32), axis=0)
    c = jnp.cumsum(p, axis=0)
    return c - c[0:1]

def hgrn2_recurrence(q, k, log_f, v, s0):
    B, T, H, K = q.shape
    V = v.shape[-1]
    L = min(CHUNK, T)
    n = T // L

    def to_blocks(a):
        return a.astype(jnp.float32).reshape(B, n, L, H, a.shape[-1]).transpose(1, 0, 3, 2, 4)

    qc, kc, gc, vc = to_blocks(q), to_blocks(k), to_blocks(log_f), to_blocks(v)
    causal = jnp.tril(jnp.ones((L, L), dtype=bool))

    def step(S, inp):
        qb, kb, gb, vb = inp
        b = jnp.cumsum(gb, axis=2)
        rel = b[:, :, :, None, :] - b[:, :, None, :, :]
        decay = jnp.exp(jnp.where(causal[:, :, None], rel, -jnp.inf))
        scores = jnp.einsum('bhtk,bhsk,bhtsk->bhts', qb, kb, decay)
        o = (jnp.einsum('bhts,bhsv->bhtv', scores, vb)
             + jnp.einsum('bhtk,bhkv->bhtv', qb * jnp.exp(b), S))
        b_last = b[:, :, -1:, :]
        S_new = (jnp.exp(b_last[:, :, 0, :])[..., None] * S
                 + jnp.einsum('bhsk,bhsv->bhkv', kb * jnp.exp(b_last - b), vb))
        return S_new, o

    S_fin, oc = lax.scan(step, s0.astype(jnp.float32), (qc, kc, gc, vc))
    o = oc.transpose(1, 0, 3, 2, 4).reshape(B, T, H, V)
    return o, S_fin.astype(s0.dtype)

def multiscale_pool(p, hist, pos0, pool_w, pool_scale):
    B, T, _ = p.shape
    full = jnp.concatenate([hist.astype(p.dtype), p], axis=1).astype(jnp.float32)
    cs = jnp.concatenate([jnp.zeros((B, 1, B_WIDTH), jnp.float32), jnp.cumsum(full, axis=1)], axis=1)
    pos = pos0 + jnp.arange(T)
    cur = full[:, POOL_HIST:]
    outs = []
    for gi, w in enumerate(POOL_WINDOWS):
        sl = slice(gi * B_GROUP_DIM, (gi + 1) * B_GROUP_DIM)
        end = cs[:, POOL_HIST + 1:POOL_HIST + 1 + T, sl]
        start = cs[:, POOL_HIST + 1 - w:POOL_HIST + 1 - w + T, sl]
        cnt = jnp.minimum(pos + 1, w).astype(jnp.float32)[None, :, None]
        outs.append((end - start) / cnt - cur[:, :, sl])
    pooled = jnp.concatenate(outs, axis=-1).reshape(B, T, B_GROUPS, B_GROUP_DIM)
    y = jnp.einsum('btgc,gce->btge', pooled, pool_w.astype(jnp.float32)).reshape(B, T, B_WIDTH)
    y = y * pool_scale.astype(jnp.float32)
    return y.astype(p.dtype), full[:, -POOL_HIST:].astype(hist.dtype)

def ab_mixer(h, s_hgrn, pool_hist, pos0, lb, w_in, out_gain, pool_w, pool_scale, w_out):
    B, T, _ = h.shape
    proj = jnp.einsum('btd,de->bte', h, w_in)
    o1 = A_KEY_WIDTH
    o2 = 2 * A_KEY_WIDTH
    o3 = o2 + A_WIDTH
    o4 = o3 + A_WIDTH
    q, fz, i_in, g, p = proj[..., :o1], proj[..., o1:o2], proj[..., o2:o3], proj[..., o3:o4], proj[..., o4:]
    fz = fz.astype(jnp.float32)
    log_f = jnp.logaddexp(jnp.log(lb), jnp.log1p(-lb) + jax.nn.log_sigmoid(fz))
    k = (1.0 - lb) * jax.nn.sigmoid(-fz)
    q = jax.nn.silu(q.astype(jnp.float32)) * (A_EXPAND ** -0.5)
    heads = lambda a, d: a.reshape(B, T, A_HEADS, d)
    o, s_new = hgrn2_recurrence(heads(q, A_EXPAND), heads(k, A_EXPAND), heads(log_f, A_EXPAND),
                                heads(i_in, A_HEAD_DIM), s_hgrn)
    o = rms_norm(o, out_gain) * jax.nn.silu(heads(g, A_HEAD_DIM).astype(jnp.float32))
    o = o.reshape(B, T, A_WIDTH).astype(h.dtype)
    yb, pool_new = multiscale_pool(p, pool_hist, pos0, pool_w, pool_scale)
    mix = jnp.einsum('bte,ed->btd', jnp.concatenate([o, yb], axis=-1), w_out)
    return mix, s_new, pool_new

def chunk_mlp_mixer(h, w_uv, ln_gain, ln_bias, ws, bs, w_out):
    B, T, _ = h.shape
    z = jax.nn.gelu(jnp.einsum('btd,de->bte', h, w_uv), approximate=False)
    u, v = z[..., :C_WIDTH], z[..., C_WIDTH:]
    v = layer_norm(v, ln_gain, ln_bias)
    L = min(C_BLOCK, T)
    n = T // L
    idx = jnp.arange(L)
    mask = (idx[None, :] // CHUNK) <= (idx[:, None] // CHUNK)
    w = jnp.where(mask[None], ws[:, :L, :L], 0.0)
    vc = v.reshape(B, n, L, C_GROUPS, C_GROUP_DIM)
    mixed = (jnp.einsum('gts,bnsgc->bntgc', w, vc)
             + bs[:, :L].T[None, None, :, :, None])
    y = u * mixed.reshape(B, T, C_WIDTH).astype(u.dtype)
    return jnp.einsum('bte,ed->btd', y, w_out), v

def conv_ffn(h, conv_hist, w_in, conv_w, conv_b, w_out):
    T = h.shape[1]
    proj = jnp.einsum('btd,df->btf', h, w_in)
    a, gate = proj[..., :D_FF], proj[..., D_FF:]
    full = jnp.concatenate([conv_hist.astype(a.dtype), a], axis=1)
    conv = conv_b + sum(full[:, j:j + T] * conv_w[j] for j in range(CONV_W))
    y = jnp.einsum('btf,fd->btd', jax.nn.gelu(conv, approximate=False) * gate, w_out)
    return y, full[:, -(CONV_W - 1):].astype(conv_hist.dtype)

def trunk(x, s_hgrn, s_pool, s_conv, pos0, lbs, norm_mix, norm_ffn, norm_final, w_in_ab, hgrn_out_gain,
          pool_w, pool_scale, w_out_ab, w_uv_c, c_ln_gain, c_ln_bias, c_ws, c_bs, w_out_c,
          w_in_ffn, ffn_conv_w, ffn_conv_b, w_out_ffn):
    new_hgrn, new_pool, new_conv, new_cv = [], [], [], []
    for layer in range(DEPTH):
        h = rms_norm(x, norm_mix[layer])
        if layer % 2 == 0:
            e = layer // 2
            mix, sh, sp = ab_mixer(h, s_hgrn[e], s_pool[e], pos0, lbs[e], w_in_ab[e], hgrn_out_gain[e],
                                   pool_w[e], pool_scale[e], w_out_ab[e])
            new_hgrn.append(sh)
            new_pool.append(sp)
        else:
            o = layer // 2
            mix, v = chunk_mlp_mixer(h, w_uv_c[o], c_ln_gain[o], c_ln_bias[o], c_ws[o], c_bs[o], w_out_c[o])
            new_cv.append(v)
        x = x + mix.astype(x.dtype)
        h = rms_norm(x, norm_ffn[layer])
        f, sc = conv_ffn(h, s_conv[layer], w_in_ffn[layer], ffn_conv_w[layer], ffn_conv_b[layer], w_out_ffn[layer])
        new_conv.append(sc)
        x = x + f.astype(x.dtype)
    y = rms_norm(x, norm_final)
    return y, jnp.stack(new_hgrn), jnp.stack(new_pool), jnp.stack(new_conv), jnp.stack(new_cv)

def setup_inputs(seed: int = 0) -> dict:
    key = jax.random.key(seed)
    ks = jax.random.split(key, 24)
    f32 = jnp.float32

    def nrm(k, shape, scale):
        return scale * jax.random.normal(k, shape, f32)

    def gain(k, shape):
        return 1.0 + 0.05 * jax.random.normal(k, shape, f32)

    return {
        "x_prompt": nrm(ks[0], (BATCH, SEQ, D_MODEL), 1.0),
        "x_sample": nrm(ks[1], (DEC_BATCH, DEC_SEQ, D_MODEL), 1.0),
        "state_hgrn": nrm(ks[2], (N_EVEN, DEC_BATCH, A_HEADS, A_EXPAND, A_HEAD_DIM), 0.3),
        "state_pool": nrm(ks[3], (N_EVEN, DEC_BATCH, POOL_HIST, B_WIDTH), 1.0),
        "state_ffn_conv": nrm(ks[4], (DEPTH, DEC_BATCH, CONV_W - 1, D_FF), 1.0),
        "norm_mix": gain(ks[5], (DEPTH, D_MODEL)),
        "norm_ffn": gain(ks[6], (DEPTH, D_MODEL)),
        "norm_final": gain(ks[7], (D_MODEL,)),
        "hgrn_lb_logits": nrm(ks[8], (N_EVEN, A_KEY_WIDTH), 0.5),
        "w_in_ab": nrm(ks[9], (N_EVEN, D_MODEL, AB_IN), D_MODEL ** -0.5),
        "hgrn_out_gain": gain(ks[10], (N_EVEN, A_HEAD_DIM)),
        "pool_w": nrm(ks[11], (N_EVEN, B_GROUPS, B_GROUP_DIM, B_GROUP_DIM), B_GROUP_DIM ** -0.5),
        "pool_scale": gain(ks[12], (N_EVEN, B_WIDTH)),
        "w_out_ab": nrm(ks[13], (N_EVEN, AB_OUT, D_MODEL), AB_OUT ** -0.5),
        "w_uv_c": nrm(ks[14], (N_ODD, D_MODEL, 2 * C_WIDTH), D_MODEL ** -0.5),
        "c_ln_gain": gain(ks[15], (N_ODD, C_WIDTH)),
        "c_ln_bias": nrm(ks[16], (N_ODD, C_WIDTH), 0.02),
        "c_ws": nrm(ks[17], (N_ODD, C_GROUPS, C_BLOCK, C_BLOCK), C_BLOCK ** -0.5),
        "c_bs": gain(ks[18], (N_ODD, C_GROUPS, C_BLOCK)),
        "w_out_c": nrm(ks[19], (N_ODD, C_WIDTH, D_MODEL), C_WIDTH ** -0.5),
        "w_in_ffn": nrm(ks[20], (DEPTH, D_MODEL, 2 * D_FF), D_MODEL ** -0.5),
        "ffn_conv_w": nrm(ks[21], (DEPTH, CONV_W, D_FF), CONV_W ** -0.5),
        "ffn_conv_b": nrm(ks[22], (DEPTH, D_FF), 0.02),
        "w_out_ffn": nrm(ks[23], (DEPTH, D_FF, D_MODEL), D_FF ** -0.5),
    }

def reference(x_prompt, x_sample, state_hgrn, state_pool, state_ffn_conv, norm_mix, norm_ffn, norm_final,
              hgrn_lb_logits, w_in_ab, hgrn_out_gain, pool_w, pool_scale, w_out_ab, w_uv_c, c_ln_gain,
              c_ln_bias, c_ws, c_bs, w_out_c, w_in_ffn, ffn_conv_w, ffn_conv_b, w_out_ffn):
    lbs = hgrn_lower_bounds(hgrn_lb_logits)
    weights = (norm_mix, norm_ffn, norm_final, w_in_ab, hgrn_out_gain, pool_w, pool_scale, w_out_ab,
               w_uv_c, c_ln_gain, c_ln_bias, c_ws, c_bs, w_out_c, w_in_ffn, ffn_conv_w, ffn_conv_b, w_out_ffn)
    bp = x_prompt.shape[0]
    zero_hgrn = jnp.zeros((N_EVEN, bp, A_HEADS, A_EXPAND, A_HEAD_DIM), state_hgrn.dtype)
    zero_pool = jnp.zeros((N_EVEN, bp, POOL_HIST, B_WIDTH), state_pool.dtype)
    zero_conv = jnp.zeros((DEPTH, bp, CONV_W - 1, D_FF), state_ffn_conv.dtype)
    y_prompt, hgrn_prompt, pool_prompt, conv_prompt, _ = trunk(
        x_prompt, zero_hgrn, zero_pool, zero_conv, 0, lbs, *weights)
    y_sample, hgrn_sample, pool_sample, conv_sample, cmlp_v_sample = trunk(
        x_sample, state_hgrn, state_pool, state_ffn_conv, PAST_LEN, lbs, *weights)
    return (y_prompt, y_sample, hgrn_prompt, hgrn_sample, pool_prompt, pool_sample,
            conv_prompt, conv_sample, cmlp_v_sample)


_drawn_inputs = setup_inputs


def setup_inputs(seed=0):
    import zlib

    import numpy as np

    out = dict(_drawn_inputs(seed))
    spreads = {}
    factors = {'state_hgrn': 5.352, 'c_ln_bias': 2.901, 'c_bs': 2.726, 'ffn_conv_b': 4.415}
    for name, (base, spread) in spreads.items():
        noise = np.random.default_rng([zlib.crc32(name.encode()), seed]).standard_normal(out[name].shape)
        drawn = base * np.exp(spread * noise) if base else spread * noise
        out[name] = __import__('jax').numpy.asarray(drawn.astype(out[name].dtype))
    for name, factor in factors.items():
        out[name] = (out[name] * factor).astype(out[name].dtype)
    return out
```

```python
from contextlib import ExitStack

import concourse.bass as bass
from concourse import mybir
from concourse.alu_op_type import AluOpType as ALU

F32 = mybir.dt.float32
F32R = mybir.dt.float32r
U8 = mybir.dt.uint8
ACT = mybir.ActivationFunctionType
ds = bass.ds

P = 128
D = 1024
SEQ = 1024
NS, SL = 8, 16
TOK = SEQ + NS * SL
TB = 384
NTB = TOK // TB
NT = TOK // P
KD = D // P
HEADS = 4
POOLW = (2, 4, 8, 16)
HIST = 15
CW = 2048
CJ = CW // P
DFF = 2816
FJ = DFF // P
STEPS = FJ // 2
EPS = 1e-6
BANKS = 6
RAWS = 4

V_MIX, V_FFN, V_FIN, V_OUTG, V_PSC, V_LNG, V_LNB, NVEC = 0, 16, 32, 40, 41, 45, 61, 77


class Plan:

    def __init__(self):
        self.piece, self.group, self.tick, self.at = 0, 0, 0, {}

    def add(self, name, pieces, groups, ticks):
        self.at[name] = (self.piece, self.group, self.tick)
        self.piece += pieces
        self.group += groups
        self.tick += ticks


PLAN = Plan()
PLAN.add("xin", 0, 24, 24)
PLAN.add("ab", 40, 60, 80)
PLAN.add("abo", 16, 24, 32)
for _l in range(2):
    if _l == 1:
        PLAN.add("v", 32, 96, 112)
        PLAN.add("mix", 0, 48, 48)
        PLAN.add("u0", 4, 6, 8)
        PLAN.add("u", 7 * 8, 7 * 30, 7 * 32)
        PLAN.add("u9", 4, 24, 24)
    PLAN.add(f"f{_l}0", 8, 12, 16)
    PLAN.add(f"f{_l}", 10 * 12, 10 * 36, 10 * 40)
    PLAN.add(f"f{_l}9", 4, 24, 24)
PLAN.add("out", 0, 18, 18)
PIECES = PLAN.piece


def build(nc, A, O):
    ctx = ExitStack()
    with ctx:
        def sem(name):
            return ctx.enter_context(nc.semaphore(name))

        x_loaded = [sem(f"x_loaded{i}") for i in range(NTB)]
        rows_loaded = sem("rows_loaded")
        raw_loaded = [sem(f"raw_loaded{i}") for i in range(RAWS)]
        sin_loaded = sem("sin_loaded")
        hist_loaded = sem("hist_loaded")
        crow_loaded = sem("crow_loaded")
        ws_loaded = sem("ws_loaded")
        bs_loaded = sem("bs_loaded")
        gbc_loaded = sem("gbc_loaded")
        stored = sem("stored")
        tails_stored = sem("tails_stored")
        vout_stored = sem("vout_stored")
        y_stored = [sem(f"y_stored{i}") for i in range(2)]
        w_scaled = sem("w_scaled")
        w_high_ready = sem("w_high_ready")
        w_low_ready = sem("w_low_ready")
        pe_tick = sem("pe_tick")
        acc_free = sem("acc_free")
        xs_init = sem("xs_init")
        xh_ready = sem("xh_ready")
        xl_ready = sem("xl_ready")
        square_ready = sem("square_ready")
        ssq_added = sem("ssq_added")
        norm_mm = sem("norm_mm")
        rms_ready = sem("rms_ready")
        rstd_ready = sem("rstd_ready")
        y_normed = sem("y_normed")
        ident_ready = sem("ident_ready")
        eps_ready = sem("eps_ready")
        setup_done = sem("setup_done")
        setup_chain = sem("setup_chain")
        vec_mm = sem("vec_mm")
        vec_ready = sem("vec_ready")
        carried = sem("carried")
        q_act = sem("q_act")
        q_silu = sem("q_silu")
        g_act = sem("g_act")
        act_prep = sem("act_prep")
        logf_ready = sem("logf_ready")
        logf_used = sem("logf_used")
        k_ready = sem("k_ready")
        reset_ready = sem("reset_ready")
        decay_ready = sem("decay_ready")
        diff_ready = sem("diff_ready")
        exps_ready = sem("exps_ready")
        k_scaled = sem("k_scaled")
        q_scaled = sem("q_scaled")
        scores_mm = sem("scores_mm")
        scores_in = sem("scores_in")
        ic_ready = sem("ic_ready")
        v_mm = sem("v_mm")
        v_ready = sem("v_ready")
        kd_mm = sem("kd_mm")
        kdt_ready = sem("kdt_ready")
        o_mm = sem("o_mm")
        o_out = sem("o_out")
        sd_mm = sem("sd_mm")
        state_decayed = sem("state_decayed")
        state_ready = sem("state_ready")
        vm_ready = sem("vm_ready")
        sstate_decayed = sem("sstate_decayed")
        sstate_ready = sem("sstate_ready")
        osq_ready = sem("osq_ready")
        onorm_mm = sem("onorm_mm")
        onorm_out = sem("onorm_out")
        osqrt = sem("osqrt")
        oinv = sem("oinv")
        o_normed = sem("o_normed")
        o_fin = sem("o_fin")
        hist_mm = sem("hist_mm")
        histt_ready = sem("histt_ready")
        prow_mm = sem("prow_mm")
        prow_ready = sem("prow_ready")
        window_step = sem("window_step")
        sums_ready = sem("sums_ready")
        edge_fixed = sem("edge_fixed")
        pooled_ready = sem("pooled_ready")
        pool_mm = sem("pool_mm")
        yb_ready = sem("yb_ready")
        mh_ready = sem("mh_ready")
        ml_ready = sem("ml_ready")
        convc_mm = sem("convc_mm")
        convc_ready = sem("convc_ready")
        conv_step = [sem(f"conv_step{i}") for i in range(2)]
        gelu_done = [sem(f"gelu_done{i}") for i in range(2)]
        y_formed = [sem(f"y_formed{i}") for i in range(2)]
        yh_ready = sem("yh_ready")
        yl_ready = sem("yl_ready")
        tails_mm = sem("tails_mm")
        trow_ready = sem("trow_ready")
        wsn_zero = sem("wsn_zero")
        wnat_masked = sem("wnat_masked")
        wt_mm = sem("wt_mm")
        wt_ready = sem("wt_ready")
        wsum_mm = sem("wsum_mm")
        wsum_ready = sem("wsum_ready")
        bsb_ready = sem("bsb_ready")
        v_activated = sem("v_activated")
        ln_stats = sem("ln_stats")
        ln_sqrt = sem("ln_sqrt")
        ln_done = sem("ln_done")
        v_out_used = sem("v_out_used")
        vout_ready = sem("vout_ready")
        addend_ready = sem("addend_ready")
        u_activated = sem("u_activated")
        u_gated = sem("u_gated")

        SLOT = TOK * 4
        XH0 = 128
        XL0 = XH0 + KD * SLOT
        W0 = XL0 + KD * SLOT
        RAW0 = W0 + 24 * SLOT
        WH0 = RAW0 + RAWS * 2048
        WL0 = WH0 + 2 * 2048
        RS0 = WL0 + 2 * 2048
        ID0 = RS0 + SLOT
        ON0 = ID0 + 512
        CV0 = ON0 + 512
        E0 = CV0 + 352
        EEND = 229344
        ESIZE = EEND - E0
        used = {}

        def at(name, shape, dt, off):
            size = 1
            for s in shape[1:]:
                size *= s
            size *= 1 if dt == U8 else 4
            assert off + size <= EEND, (name, off + size, EEND)
            used[name] = (off, off + size)
            return nc.alloc_sbuf_tensor_at(name, shape, dt, offset=off)

        def slot(k):
            return W0 + k * SLOT

        xh = at("xh", [P, KD, TOK], F32R, XH0)
        xl = at("xl", [P, KD, TOK], F32R, XL0)
        work = at("work", [P, 24, TOK], F32, W0)
        xs = at("xs", [P, KD, TOK], F32, slot(0))
        raw = at("raw", [P, RAWS, 512], F32, RAW0)
        wh = at("wh", [P, 2, 512], F32R, WH0)
        wl = at("wl", [P, 2, 512], F32R, WL0)
        rstd = at("rstd", [P, TOK], F32, RS0)
        ident = at("ident", [P, P], F32, ID0)
        ones = at("ones", [P, P], F32, ON0)
        vec = at("vec", [P, NVEC + 3], F32, CV0)
        eps_c = vec[:, NVEC:NVEC + 1]
        ssq_e = at("ssq_e", [P, TOK], F32, E0)
        sq_e = at("sq_e", [P, 2, TB], F32, E0 + SLOT)
        xtok = at("xtok", [P, NT, D], F32, slot(8))
        vrow = at("vrow", [NVEC, P], F32, slot(16))
        o = E0
        ediff = at("ediff", [P, 2, HEADS, P], F32, o); o += 4096
        qsc = at("qsc", [P, 2, HEADS, 64], F32, o); o += 2048
        ksc = at("ksc", [P, 2, HEADS, P], F32, o); o += 4096
        sct = at("sct", [P, HEADS, P], F32, o); o += 2048
        vtok = at("vtok", [P, HEADS, P], F32, o); o += 2048
        icp = at("icp", [P, HEADS, P], F32, o); o += 2048
        kdt = at("kdt", [P, HEADS, P], F32, o); o += 2048
        stt = at("stt", [P, HEADS, P], F32, o); o += 2048
        masks = at("masks", [P, 7, 64], U8, o); o += 448
        ebl = at("ebl", [P, HEADS, NS], F32, o); o += 128
        smask = at("smask", [P, NS], F32, o); o += 32
        resetm = at("resetm", [P, TOK], F32, E0)
        maskf = at("maskf", [P, 7, 64], F32, E0 + 8192)
        sin_ = at("sin_", [P, HEADS, TOK], F32, slot(20))
        vms = at("vms", [P, HEADS, TOK], F32, slot(4))
        osq = at("osq", [P, 2, TB], F32, E0)
        orr = at("orr", [P, 2, TB], F32, E0 + 3072)
        pooled = at("pooled", [P, TOK], F32, E0 + 6144)
        hstage = at("hstage", [NS * HIST, 512], F32, E0 + 10752)
        histt = at("histt", [P, HEADS, NS * HIST], F32, E0 + 12800)
        prow = at("prow", [P, 2, 512], F32, E0 + 14720)
        poolw = at("poolw", [P, HEADS, P], F32, E0 + 18816)
        cinv = at("cinv", [P, 16], F32, E0 + 20864)
        PADW = HIST + SEQ + NS * (HIST + SL)
        pada = at("pada", [P, PADW], F32, slot(20))
        padb = at("padb", [P, PADW], F32, slot(20) + 5184)
        padc = at("padc", [P, PADW], F32, slot(20) + 10368)
        mh = at("mh", [P, KD, TOK], F32R, slot(8))
        ml = at("ml", [P, KD, TOK], F32R, slot(16))
        APW = 2 + SEQ + NS * (2 + SL)
        o = slot(8)
        apad = at("apad", [P, 2, APW + 2], F32, o); o += 2 * (APW + 2) * 4
        cv = at("cv", [P, 2, TOK], F32, o); o += 2 * SLOT
        gate = at("gate", [P, 2, TOK], F32, o); o += 2 * SLOT
        convc = at("convc", [P, 20 * FJ], F32, o); o += 1760
        tails = at("tails", [P, 18, FJ], F32, o); o += 1600
        crow = at("crow", [P, 4, P], F32, o); o += 2048
        trow = at("trow", [P, 4, P], F32, o); o += 2048
        ssq_b = at("ssq_b", [P, TOK], F32, o); o += SLOT
        sq_b = at("sq_b", [P, 2, TB], F32, o); o += 3072
        assert o <= slot(24)
        yh = at("yh", [P, 2, TOK], F32R, E0)
        yl = at("yl", [P, 2, TOK], F32R, E0 + 2 * SLOT)
        ut = at("ut", [P, 2, TB], F32, E0 + 4 * SLOT)
        o = slot(0)
        vtmp = at("vtmp", [P, 2, TOK], F32, o); o += 2 * SLOT
        wtp = at("wtp", [P, 8, P], F32, o); o += 4096
        wts = at("wts", [P, 8, P], F32, o); o += 4096
        wsum = at("wsum", [P, 8, 2 * P], F32, o); o += 8192
        bsb = at("bsb", [P, 8, 2 * P], F32, o); o += 8192
        assert o <= slot(8)
        o = E0
        wnat = at("wnat", [P, 8, P], F32, o)
        wsn = at("wsn", [P, 8, P], F32, o + 4096)
        stats = at("stats", [P, NT, CJ, 6], F32, o + 8192)
        mv = at("mv", [P, NT, 2], F32, o + 8192 + 3456)
        lrs = at("lrs", [P, NT], F32, o + 8192 + 3456 + 96)
        adde = at("adde", [P, 2, 2 * P], F32, o + 16384)
        gbc = at("gbc", [P, CJ, P], F32, o)
        bbc = [at(f"bbc{b}", [P, 8, P], F32, o + off) for b, off in ((0, 12288), (1, 18432))]
        otok = at("otok", [P, 2, D], F32, slot(8))

        ps = [ctx.enter_context(nc.psum_tensor(f"bank{b}", [P, 512], F32)) for b in range(8)]
        block = ctx.enter_context(nc.Block())

        def tbs(tb):
            return slice(tb * TB, (tb + 1) * TB)

        wab = A["w_in_ab"][0].rearrange("(h k p) c -> p h k c", h=2, p=P)
        wabo = A["w_out_ab"][0].rearrange("(h k p) c -> p h k c", h=2, p=P)
        wuv = A["w_uv_c"][0].rearrange("(h k p) c -> p h k c", h=2, p=P)
        woc = A["w_out_c"][0].rearrange("(k p) c -> p k c", p=P)
        wfi = [A["w_in_ffn"][l].rearrange("(h k p) c -> p h k c", h=2, p=P) for l in range(2)]
        wfo = [A["w_out_ffn"][l].rearrange("(k p) c -> p k c", p=P) for l in range(2)]

        def loop(eng, n, body):
            with eng.Fori(0, n) as i:
                body(i)

        @block.sync
        def _(sp):
            def load_piece(n, src, s):
                if s is None or s >= RAWS:
                    sp.wait_ge(w_low_ready, n - (RAWS - 1))
                sp.dma_start(raw[:, s % RAWS, :].rearrange("p (k c) -> p k c", k=src.shape[1]), src)\
                    .then_inc(raw_loaded[s % RAWS], 16)

            def up(w, n, s, col):
                for h in range(2):
                    load_piece(n + h, w[:, h, :, ds(col, P)], s + h)

            def down(w, n, s, k0):
                for q in range(4):
                    load_piece(n + q, w[:, ds(k0, 2), q * 256:(q + 1) * 256], s + q)

            xp = A["x_prompt"].rearrange("b (t p) d -> p (b t) d", p=P)
            xsm = A["x_sample"].rearrange("b t d -> (b t) d")
            for t in range(NT):
                sp.dma_start(xtok[:, t, :], xp[:, t, :] if t < NT - 1 else xsm).then_inc(x_loaded[t // 3], 16)
            rows = [(V_MIX, A["norm_mix"].rearrange("l (k p) -> (l k) p", p=P)),
                    (V_FFN, A["norm_ffn"].rearrange("l (k p) -> (l k) p", p=P)),
                    (V_FIN, A["norm_final"].rearrange("(k p) -> k p", p=P)),
                    (V_OUTG, A["hgrn_out_gain"]),
                    (V_PSC, A["pool_scale"].rearrange("l (k p) -> (l k) p", p=P)),
                    (V_LNG, A["c_ln_gain"].rearrange("l (k p) -> (l k) p", p=P)),
                    (V_LNB, A["c_ln_bias"].rearrange("l (k p) -> (l k) p", p=P))]
            for r0, src in rows:
                sp.dma_start(vrow[r0:r0 + src.shape[0], :], src).then_inc(rows_loaded, 16)

            n0, _, _ = PLAN.at["ab"]

            def ab(i):
                for u in range(2):
                    up(wab, n0 + 4 * i + 2 * u, n0 + 2 * u, (2 * i + u) * P)
            ab(0)
            with sp.Fori(1, 10) as i:
                for u in range(2):
                    for h in range(2):
                        s = n0 + 2 * u + h
                        load_piece(4 * i + s, wab[:, h, :, ds((2 * i + u) * P, P)], s + RAWS)

            n0, _, _ = PLAN.at["abo"]
            for u in range(2):
                up(wabo, n0 + 2 * u, n0 + 2 * u, u * P)

            sp.wait_ge(state_ready, NT)
            for h in range(HEADS):
                sp.dma_start(sin_[:, h, 0:SEQ].rearrange("p (q v) -> p q v", q=NS),
                             A["state_hgrn"][0, :, h].rearrange("q k v -> k q v")).then_inc(sin_loaded, 16)
            sp.dma_start(O["hgrn_prompt"][0, 0].rearrange("h k v -> k h v"), stt[:, :, :]).then_inc(stored, 16)
            sp.wait_ge(sstate_ready, HEADS)
            for h in range(HEADS):
                sp.dma_start(O["hgrn_sample"][0, :, h].rearrange("q k v -> k q v"),
                             sin_[:, h, 0:SEQ].rearrange("p (q v) -> p q v", q=NS)).then_inc(stored, 16)
            sp.wait_ge(stored, 16 * 5)
            sp.dma_start(hstage[:, :], A["state_pool"][0].rearrange("q t c -> (q t) c")).then_inc(hist_loaded, 16)
            sp.dma_start(poolw[:, :, :], A["pool_w"][0].rearrange("g c e -> c g e")).then_inc(hist_loaded, 16)
            sp.wait_ge(prow_ready, 2)
            sp.dma_start(O["pool_prompt"][0, 0], prow[P - HIST:P, 0, :]).then_inc(stored, 16)
            for q in range(NS):
                sp.dma_start(O["pool_sample"][0, q], prow[SL * q + 1:SL * (q + 1), 1, :]).then_inc(stored, 16)

            n0, _, _ = PLAN.at["abo"]
            with sp.Fori(1, 4) as i:
                for u in range(2):
                    up(wabo, n0 + 4 * i + 2 * u, n0 + 2 * u, (2 * i + u) * P)

            def ffn(l):
                n0, _, _ = PLAN.at[f"f{l}0"]
                cols = (0, P, DFF, DFF + P)
                for u in range(2):
                    up(wfi[l], n0 + 2 * u, n0 + 2 * u, cols[u])
                sp.wait_ge(rstd_ready, NTB * (2 + 2 * l))
                hist = A["state_ffn_conv"][l].rearrange("q j (f p) -> (q j f) p", p=P)
                taps = A["ffn_conv_w"][l].rearrange("j (f p) -> (j f) p", p=P)
                bias = A["ffn_conv_b"][l].rearrange("(f p) -> f p", p=P)
                for b, src in enumerate((hist[0:128], hist[128:256])):
                    sp.dma_start(crow[:, b, :], src).then_inc(crow_loaded, 16)
                sp.dma_start(crow[0:96, 2, :], hist[256:352]).then_inc(crow_loaded, 16)
                sp.dma_start(crow[96:128, 2, :], taps[0:32]).then_inc(crow_loaded, 16)
                sp.dma_start(crow[0:34, 3, :], taps[32:66]).then_inc(crow_loaded, 16)
                sp.dma_start(crow[34:56, 3, :], bias).then_inc(crow_loaded, 16)
                for u in range(2, 4):
                    up(wfi[l], n0 + 2 * u, n0 + 2 * u, cols[u])
                n0, _, _ = PLAN.at[f"f{l}"]
                with sp.Fori(0, STEPS - 1) as i:
                    for u, col in enumerate(cols):
                        up(wfi[l], n0 + 12 * i + 2 * u, n0 + 2 * u, (i + 1) * 2 * P + col)
                    down(wfo[l], n0 + 12 * i + 8, n0 + 8, 2 * i)
                n0, _, _ = PLAN.at[f"f{l}9"]
                down(wfo[l], n0, n0, FJ - 2)

            def store_tails(l):
                sp.wait_ge(trow_ready, 4 * (l + 1))
                outp = O["conv_prompt"][l, 0].rearrange("j (f p) -> (j f) p", p=P)
                outs = O["conv_sample"][l].rearrange("q j (f p) -> (q j f) p", p=P)
                sp.dma_start(outp, trow[0:44, 0, :]).then_inc(tails_stored, 16)
                sp.dma_start(outs[0:128], trow[:, 1, :]).then_inc(tails_stored, 16)
                sp.dma_start(outs[128:256], trow[:, 2, :]).then_inc(tails_stored, 16)
                sp.dma_start(outs[256:352], trow[0:96, 3, :]).then_inc(tails_stored, 16)

            ffn(0)
            n0, _, _ = PLAN.at["v"]
            up(wuv, n0, n0, CW)
            store_tails(0)
            sp.wait_ge(rstd_ready, NTB * 3)
            sp.wait_ge(wsn_zero, 1)
            sp.dma_start(wnat[:, :, :], A["c_ws"][0].rearrange("g t s -> t g s")).then_inc(ws_loaded, 16)
            for q in range(NS):
                sp.dma_start(wsn[SL * q:SL * (q + 1), :, SL * q:SL * (q + 1)],
                             A["c_ws"][0, :, 0:SL, 0:SL].rearrange("g t s -> t g s")).then_inc(ws_loaded, 16)
            sp.dma_start(bsb[:, :, 0:P], A["c_bs"][0:1].to_broadcast([P, 8, P])).then_inc(bs_loaded, 16)
            sp.wait_ge(wt_ready, 4)
            sp.dma_start(gbc[:, :, :], A["c_ln_gain"].rearrange("o (j c) -> o j c", c=P).to_broadcast([P, CJ, P]))\
                .then_inc(gbc_loaded, 16)
            for b in range(2):
                sp.dma_start(bbc[b][:, :, :], A["c_ln_bias"].rearrange("o (j c) -> o j c", c=P)[:, 8 * b:8 * b + 8]
                             .to_broadcast([P, 8, P])).then_inc(gbc_loaded, 16)
            with sp.Fori(0, 7) as i:
                for u in range(2):
                    up(wuv, n0 + 2 + 4 * i + 2 * u, n0 + 2 + 2 * u, CW + (2 * i + 1 + u) * P)
            up(wuv, n0 + 30, n0 + 30, CW + 15 * P)
            n0, _, _ = PLAN.at["u0"]
            for u in range(2):
                up(wuv, n0 + 2 * u, n0 + 2 * u, u * P)
            sp.wait_ge(vout_ready, 1)
            sp.dma_start(O["cmlp_v"][0].rearrange("q t (j c) -> (q t) j c", c=P), gbc[:, :, :])\
                .then_inc(vout_stored, 16)
            n0, _, _ = PLAN.at["u"]
            with sp.Fori(0, 7) as i:
                for u in range(2):
                    up(wuv, n0 + 8 * i + 2 * u, n0 + 2 * u, (2 * i + 2 + u) * P)
                down(woc, n0 + 8 * i + 4, n0 + 4, 2 * i)
            n0, _, _ = PLAN.at["u9"]
            down(woc, n0, n0, CJ - 2)
            ffn(1)
            store_tails(1)
            yp = O["y_prompt"].rearrange("b (t p) d -> p (b t) d", p=P)
            ysm = O["y_sample"].rearrange("b t d -> (b t) d")
            for t in range(NT):
                sp.wait_ge(acc_free, PLAN.at["out"][1] + 2 * (t + 1))
                sp.dma_start(yp[:, t, :] if t < NT - 1 else ysm, otok[:, t % 2, :])\
                    .then_inc(y_stored[t % 2], 16)
            for par in range(2):
                sp.wait_ge(y_stored[par], 16 * ((NT + 1 - par) // 2))
            sp.wait_ge(stored, 16 * 14)
            sp.wait_ge(tails_stored, 16 * 8)
            sp.wait_ge(vout_stored, 16)


        def some(count):
            return not isinstance(count, int) or count > 0

        LV = 7
        HALF = {True: (64, 32, 16, 8, 4, 2, 1), False: (8, 4, 2, 1)}
        MOFF = {64: 0, 32: 1, 16: 2, 8: 3, 4: 4, 2: 5, 1: 6}

        def tile_cols(t):
            return ds(t * P, P)

        def blocks(ap, b):
            return ap.rearrange("p h (n b) -> p h n b", b=b)

        @block.tensor
        def _(pe):
            def acc_bank(g, s):
                if s is None or s >= BANKS:
                    pe.wait_ge(acc_free, g - (BANKS - 1))
                return ps[s % BANKS]

            def unit(rh, rl, n, g, sn, sg):
                for h in range(2):
                    pe.wait_ge(w_high_ready, n + h + 1)
                    pe.wait_ge(w_low_ready, n + h + 1)
                    place = (sn + h) % 2
                    for k in range(4):
                        kk = 4 * h + k
                        parts = ((wh, rh), (wh, rl), (wl, rh))
                        for c, (w, r) in enumerate(parts):
                            for tb in range(NTB):
                                if kk == 0 and c == 0:
                                    acc_bank(g + tb, sg + tb)
                                mm = pe.matmul(ps[(sg + tb) % BANKS][:, 0:TB], w[:, place, k * P:(k + 1) * P],
                                               r[:, kk, tbs(tb)], start=kk == 0 and c == 0,
                                               stop=kk == KD - 1 and c == 2)
                                if kk == KD - 1 and c == 2:
                                    mm.then_inc(pe_tick, 1)
                    if h == 0:
                        mm.then_inc(pe_tick, 1)

            def down(n, g, sn, sg, steps_done):
                pe.wait_ge(yh_ready, steps_done)
                pe.wait_ge(yl_ready, steps_done)
                for q in range(4):
                    pe.wait_ge(w_high_ready, n + q + 1)
                    pe.wait_ge(w_low_ready, n + q + 1)
                    place = (sn + q) % 2
                    for dd in range(2):
                        g0 = 3 * (2 * q + dd)
                        for k in range(2):
                            for c, (w, r) in enumerate(((wh, yh), (wh, yl), (wl, yh))):
                                for tb in range(NTB):
                                    if k == 0 and c == 0:
                                        acc_bank(g + g0 + tb, sg + g0 + tb)
                                    mm = pe.matmul(ps[(sg + g0 + tb) % BANKS][:, 0:TB],
                                                   w[:, place, k * 256 + dd * P:k * 256 + (dd + 1) * P],
                                                   r[:, k, tbs(tb)], start=k == 0 and c == 0,
                                                   stop=k == 1 and c == 2)
                                    if k == 1 and c == 2:
                                        mm.then_inc(pe_tick, 1)

            def norm(k, ssq):
                pe.wait_ge(ssq_added, 24 * (k + 1))
                for tb in range(NTB):
                    if some(NTB * k + tb - 1):
                        pe.wait_ge(rms_ready, NTB * k + tb - 1)
                    pe.matmul(ps[6 + (NTB * k + tb) % 2][:, 0:TB], ones[:, :], ssq[:, tbs(tb)], start=True, stop=True)\
                        .then_inc(norm_mm, 1)
                if k < 4:
                    pe.wait_ge(xh_ready, 24 * (k + 1))
                    pe.wait_ge(xl_ready, 24 * (k + 1))

            pe.wait_ge(ident_ready, 1)
            pe.wait_ge(rows_loaded, 16 * 7)
            pe.transpose(ps[6][:, 0:NVEC], vrow[:, :], ident[0:NVEC, 0:NVEC]).then_inc(vec_mm, 1)
            for g in range(24):
                tb, d = divmod(g, KD)
                if d == 0:
                    pe.wait_ge(x_loaded[tb], 48)
                bank = acc_bank(g, g)
                for j in range(3):
                    mm = pe.transpose(bank[:, j * P:(j + 1) * P], xtok[:, 3 * tb + j, d * P:(d + 1) * P], ident[:, :])
                mm.then_inc(pe_tick, 1)
            pe.wait_ge(vec_ready, 1)
            norm(0, ssq_e)

            n0, g0, _ = PLAN.at["ab"]

            def ab(i):
                for u in range(2):
                    unit(xh, xl, n0 + 4 * i + 2 * u, g0 + 6 * i + 3 * u, n0 + 2 * u, g0 + 3 * u)
            loop(pe, 10, ab)

            pe.wait_ge(acc_free, 84)

            def tile(t, prompt):
                L = len(HALF[prompt])
                pe.wait_ge(ic_ready, t + 1)
                if some(t):
                    pe.wait_ge(v_ready, t)
                for h in range(HEADS):
                    mm = pe.transpose(ps[0][:, h * P:(h + 1) * P], icp[:, h, :], ident[:, :])
                mm.then_inc(v_mm, 1)
                pe.wait_ge(k_scaled, t * (LV + 2) + 1)
                pe.wait_ge(q_silu, 1)
                if some(t * (LV + 1) - LV):
                    pe.wait_ge(scores_in, t * (LV + 1) - LV)
                for h in range(HEADS):
                    mm = pe.matmul(ps[1][:, h * P:(h + 1) * P], ksc[:, 0, h, :], work[:, h, tile_cols(t)],
                                   start=True, stop=True)
                mm.then_inc(scores_mm, 1)
                for q in range(1, L + 1):
                    pe.wait_ge(q_scaled, t * (LV + 1) + q)
                    pe.wait_ge(k_scaled, t * (LV + 2) + q + 1)
                    if some(t * (LV + 1) + (q - 1 if q > 2 else 0)):
                        pe.wait_ge(scores_in, t * (LV + 1) + (q - 1 if q > 2 else 0))
                    for h in range(HEADS):
                        mm = pe.matmul(ps[6 + q % 2][:, h * 64:(h + 1) * 64], ksc[:, q % 2, h, :], qsc[:, q % 2, h, :],
                                       start=True, stop=True)
                    mm.then_inc(scores_mm, 1)
                pe.wait_ge(k_scaled, t * (LV + 2) + L + 2)
                if some(t):
                    pe.wait_ge(kdt_ready, t)
                for h in range(HEADS):
                    mm = pe.transpose(ps[2][:, h * P:(h + 1) * P], ediff[:, 1, h, :], ident[:, :])
                mm.then_inc(kd_mm, 1)
                pe.wait_ge(scores_in, t * (LV + 1) + L + 1)
                pe.wait_ge(v_ready, t + 1)
                pe.wait_ge(q_scaled, t * (LV + 1) + L + 1)
                pe.wait_ge(state_ready, t + 1)
                if some(t):
                    pe.wait_ge(o_out, t)
                if not prompt:
                    pe.wait_ge(sin_loaded, 16 * HEADS)
                for h in range(HEADS):
                    if prompt:
                        pe.matmul(ps[3][:, h * P:(h + 1) * P], vtok[:, h, :], sct[:, h, :], start=True, stop=False)
                        mm = pe.matmul(ps[3][:, h * P:(h + 1) * P], stt[:, h, :], ediff[:, 0, h, :],
                                       start=False, stop=True)
                    else:
                        for q in range(NS):
                            own = slice(q * SL, (q + 1) * SL)
                            out = ps[3][:, h * P + q * SL:h * P + (q + 1) * SL]
                            pe.matmul(out, vtok[:, h, :], sct[:, h, own], start=True, stop=False)
                            mm = pe.matmul(out, sin_[:, h, q * P:(q + 1) * P], ediff[:, 0, h, own],
                                           start=False, stop=True)
                mm.then_inc(o_mm, 1)
                pe.wait_ge(kdt_ready, t + 1)
                if prompt:
                    for h in range(HEADS):
                        mm = pe.matmul(ps[4][:, h * P:(h + 1) * P], kdt[:, h, :], vtok[:, h, :], start=True, stop=True)
                    mm.then_inc(sd_mm, 1)
                else:
                    for h in range(HEADS):
                        pe.wait_ge(vm_ready, h + 1)
                        if some(h):
                            pe.wait_ge(sstate_ready, h)
                        for c in range(2):
                            mm = pe.matmul(ps[4 + c][:, :], kdt[:, h, :], vms[:, h, c * 512:(c + 1) * 512],
                                           start=True, stop=True)
                        mm.then_inc(sd_mm, 1)

            tile(0, True)
            with pe.Fori(1, NT - 1) as t:
                tile(t, True)
            tile(NT - 1, False)

            pe.wait_ge(hist_loaded, 32)
            for h in range(HEADS):
                mm = pe.transpose(ps[0][:, h * 120:(h + 1) * 120], hstage[:, h * P:(h + 1) * P], ident[0:120, 0:120])
            mm.then_inc(hist_mm, 1)
            for r in range(2):
                for h in range(HEADS):
                    mm = pe.transpose(ps[1 + r][:, h * P:(h + 1) * P],
                                      work[:, 16 + h, (NT - 2 + r) * P:(NT - 1 + r) * P], ident[:, :])
                mm.then_inc(prow_mm, 1)
            for e in range(HEADS * NTB):
                pe.wait_ge(osq_ready, e + 1)
                if some(e - 1):
                    pe.wait_ge(onorm_out, e - 1)
                pe.matmul(ps[6 + e % 2][:, 0:TB], ones[:, :], osq[:, e % 2, :], start=True, stop=True)\
                    .then_inc(onorm_mm, 1)
            for h in range(HEADS):
                pe.wait_ge(pooled_ready, h + 1)
                if some(NTB * h):
                    pe.wait_ge(yb_ready, NTB * h)
                for tb in range(NTB):
                    if h == 0 and tb == 0:
                        pe.wait_ge(o_out, NT)
                        pe.wait_ge(sstate_ready, HEADS)
                    pe.matmul(ps[3 + tb][:, 0:TB], poolw[:, h, :], pooled[:, tbs(tb)], start=True, stop=True)\
                        .then_inc(pool_mm, 1)

            pe.wait_ge(mh_ready, KD)
            pe.wait_ge(ml_ready, KD)
            n0, g0, _ = PLAN.at["abo"]

            def abo(i):
                for u in range(2):
                    unit(mh, ml, n0 + 4 * i + 2 * u, g0 + 6 * i + 3 * u, n0 + 2 * u, g0 + 3 * u)
            loop(pe, 4, abo)
            norm(1, ssq_e)

            def ffn(l):
                pe.wait_ge(crow_loaded, 96 * (l + 1))
                for b in range(4):
                    r = P if b < 3 else 56
                    mm = pe.transpose(ps[7][:, b * P:b * P + r], crow[0:r, b, :], ident[0:r, 0:r])
                mm.then_inc(convc_mm, 1)
                n0, g0, _ = PLAN.at[f"f{l}0"]
                for u in range(4):
                    unit(xh, xl, n0 + 2 * u, g0 + 3 * u, n0 + 2 * u, g0 + 3 * u)
                n1, g1, _ = PLAN.at[f"f{l}"]
                done0 = 2 * (STEPS * l + (8 if l else 0))

                def step(i):
                    for u in range(4):
                        unit(xh, xl, n1 + 12 * i + 2 * u, g1 + 36 * i + 3 * u, n1 + 2 * u, g1 + 3 * u)
                    down(n1 + 12 * i + 8, g1 + 36 * i + 12, n1 + 8, g1 + 12, 2 * i + (done0 + 2))
                loop(pe, STEPS - 1, step)
                n2, g2, _ = PLAN.at[f"f{l}9"]
                down(n2, g2, n2, g2, done0 + 2 * STEPS)
                norm(2 + 2 * l, ssq_b)
                pe.wait_ge(conv_step[l], 9 * FJ)
                pe.wait_ge(rms_ready, NTB * (3 + 2 * l))
                for b, (c0, c1) in enumerate(((0, 44), (44, 172), (172, 300), (300, 396))):
                    flat = tails[:, :, :].rearrange("p r f -> p (r f)")
                    mm = pe.transpose(ps[7][0:c1 - c0, b * P:(b + 1) * P], flat[:, c0:c1], ident[:, :])
                mm.then_inc(tails_mm, 1)

            ffn(0)

            pe.wait_ge(trow_ready, 4)
            pe.wait_ge(wnat_masked, 1)
            pe.wait_ge(ws_loaded, 16 * 9)
            for m, src in enumerate((wnat, wsn)):
                for b in range(2):
                    if some(2 * m + b - 1):
                        pe.wait_ge(wt_ready, 2 * m + b - 1)
                    for j in range(4):
                        mm = pe.transpose(ps[6 + b][:, j * P:(j + 1) * P], src[:, 4 * b + j, :], ident[:, :])
                    mm.then_inc(wt_mm, 1)
            for m, w in enumerate((wtp, wts)):
                for b in range(2):
                    pe.wait_ge(wt_ready, 4)
                    if some(2 * m + b - 1):
                        pe.wait_ge(wsum_ready, 2 * m + b - 1)
                    pe.matmul(ps[6 + b][:, :], ones[:, :], w[:, 4 * b:4 * b + 4, :], start=True, stop=True)\
                        .then_inc(wsum_mm, 1)
            n0, g0, _ = PLAN.at["v"]

            def turn(j, par, g, sg):
                pe.wait_ge(v_activated, j + 1)
                for tb in range(NTB):
                    bank = acc_bank(g + tb, sg + tb)
                    for k in range(3):
                        c = tb * TB + k * P
                        mm = pe.transpose(bank[:, k * P:(k + 1) * P], vtmp[:, par, c:c + P], ident[:, :])
                    mm.then_inc(pe_tick, 1)
            unit(xh, xl, n0, g0, n0, g0)

            def vstep(i):
                for u in range(2):
                    unit(xh, xl, n0 + 2 + 4 * i + 2 * u, g0 + 3 + 12 * i + 6 * u, n0 + 2 + 2 * u, g0 + 3 + 6 * u)
                    turn(2 * i + u, u, g0 + 6 + 12 * i + 6 * u, g0 + 6 + 6 * u)
            loop(pe, 7, vstep)
            unit(xh, xl, n0 + 30, g0 + 87, n0 + 30, g0 + 87)
            turn(14, 0, g0 + 90, g0 + 90)
            turn(15, 1, g0 + 93, g0 + 93)
            _, g0, _ = PLAN.at["mix"]
            pe.wait_ge(ln_done, NT)
            for j in range(CJ):
                for tb in range(NTB):
                    g = g0 + 3 * j + tb
                    bank = acc_bank(g, g)
                    for k in range(3):
                        t = 3 * tb + k
                        w = wtp if t < NT - 1 else wts
                        mm = pe.matmul(bank[:, k * P:(k + 1) * P], work[:, 8 + j, t * P:(t + 1) * P], w[:, j // 2, :],
                                       start=True, stop=True)
                    mm.then_inc(pe_tick, 1)
            n0, g0, _ = PLAN.at["u0"]
            for u in range(2):
                unit(xh, xl, n0 + 2 * u, g0 + 3 * u, n0 + 2 * u, g0 + 3 * u)
            n1, g1, _ = PLAN.at["u"]
            done0 = 2 * STEPS

            def ustep(i):
                for u in range(2):
                    unit(xh, xl, n1 + 8 * i + 2 * u, g1 + 30 * i + 3 * u, n1 + 2 * u, g1 + 3 * u)
                down(n1 + 8 * i + 4, g1 + 30 * i + 6, n1 + 4, g1 + 6, 2 * i + (done0 + 2))
            loop(pe, 7, ustep)
            n2, g2, _ = PLAN.at["u9"]
            down(n2, g2, n2, g2, done0 + CJ)
            norm(3, ssq_b)
            ffn(1)
            _, g0, _ = PLAN.at["out"]
            pe.wait_ge(y_normed, 24)
            for t in range(NT):
                for b in range(2):
                    g = g0 + 2 * t + b
                    bank = acc_bank(g, g)
                    for k in range(4):
                        mm = pe.transpose(bank[:, k * P:(k + 1) * P], xs[:, 4 * b + k, t * P:(t + 1) * P], ident[:, :])
                    mm.then_inc(pe_tick, 1)

        @block.vector
        def _(dve):
            def low(n, s):
                dve.wait_ge(w_high_ready, n + 1)
                dve.tensor_tensor(wl[:, s % 2, :], raw[:, s % RAWS, :], wh[:, s % 2, :].bitcast(F32), ALU.subtract)\
                    .then_inc(w_low_ready, 1)

            def scaled(dst, bank, tb, tick):
                dve.wait_ge(pe_tick, tick)
                dve.tensor_tensor(dst, ps[bank % BANKS][:, 0:TB], rstd[:, tbs(tb)], ALU.mult)\
                    .then_inc(acc_free, 1)

            def add_down(d, tb, g, sg, tick):
                dve.wait_ge(pe_tick, tick)
                dve.wait_ge(acc_free, g - 12)
                dve.tensor_tensor(xs[:, d, tbs(tb)], ps[sg % BANKS][:, 0:TB], xs[:, d, tbs(tb)], ALU.add)\
                    .then_inc(acc_free, 1)

            def x_low(e, d, tb):
                dve.wait_ge(xh_ready, e + 1)
                dve.tensor_tensor(xl[:, d, tbs(tb)], xs[:, d, tbs(tb)], xh[:, d, tbs(tb)].bitcast(F32), ALU.subtract)\
                    .then_inc(xl_ready, 1)

            def inv_rms(k):
                for tb in range(NTB):
                    dve.wait_ge(rms_ready, NTB * k + tb + 1)
                    dve.reciprocal(rstd[:, tbs(tb)], rstd[:, tbs(tb)]).then_inc(rstd_ready, 1)
                dve.wait_ge(rstd_ready, NTB * (k + 1))

            prev = None
            for g in range(24):
                tb, d = divmod(g, KD)
                dve.wait_ge(pe_tick, g + 1)
                dve.tensor_copy(xs[:, d, tbs(tb)], ps[g % BANKS][:, 0:TB]).then_inc(acc_free, 1)
                if prev is not None:
                    x_low(*prev)
                prev = (g, d, tb)
            x_low(*prev)
            inv_rms(0)
            low(0, 0)

            n0, g0, t0 = PLAN.at["ab"]

            def ab(i):
                for u in range(2):
                    low(n0 + 4 * i + 2 * u + 1, n0 + 2 * u + 1)
                    low(n0 + 4 * i + 2 * u + 2, n0 + 2 * u + 2)
                    for tb in range(NTB):
                        scaled(work[:, 2 * i + u, tbs(tb)], g0 + 3 * u + tb, tb, t0 + 8 * i + 4 * u + 2 + tb)
            loop(dve, 10, ab)

            qs, zs, ls = work[:, 0:4, :], work[:, 4:8, :], work[:, 20:24, :]
            dve.memset(stt[:, :, :], 0.0).then_inc(state_ready, 1)
            dve.wait_ge(q_act, 1)
            dve.tensor_scalar(qs, qs, float(P) ** -0.5, None, ALU.mult).then_inc(q_silu, 1)
            dve.wait_ge(act_prep, 3)
            dve.scalar_tensor_tensor(ls, zs, 0.0, ls, ALU.min, ALU.subtract).then_inc(logf_ready, 1)
            dve.wait_ge(logf_used, 1)
            dve.wait_ge(reset_ready, 3)
            for h in range(HEADS):
                dve.tensor_tensor_scan(work[:, 20 + h, :], resetm[:, :], work[:, 20 + h, :], 0.0, ALU.mult, ALU.add)\
                    .then_inc(decay_ready, 1)
            dve.wait_ge(decay_ready, HEADS)
            dve.wait_ge(q_silu, 1)
            dve.wait_ge(setup_done, 1)

            def tile(t, prompt):
                halves = HALF[prompt]
                L = len(halves)
                bt = work[:, 20:24, tile_cols(t)]
                qt = work[:, 0:4, tile_cols(t)]

                def diff(q):
                    b = halves[q - 1]
                    if q == 1:
                        if some(t):
                            dve.wait_ge(kd_mm, t)
                        if some(t * (LV + 2)):
                            dve.wait_ge(k_scaled, t * (LV + 2))
                    elif q == 2:
                        if some(t):
                            dve.wait_ge(o_mm, t)
                    else:
                        dve.wait_ge(k_scaled, t * (LV + 2) + q - 1)
                        dve.wait_ge(q_scaled, t * (LV + 1) + q - 2)
                    bv, ev = blocks(bt, 2 * b), blocks(ediff[:, q % 2], 2 * b)
                    mid = bv[:, :, :, b - 1:b].to_broadcast([P, HEADS, P // (2 * b), b])
                    dve.tensor_tensor(ev[:, :, :, b:], bv[:, :, :, b:], mid, ALU.subtract)
                    dve.tensor_tensor(ev[:, :, :, 0:b], mid, bv[:, :, :, 0:b], ALU.subtract)\
                        .then_inc(diff_ready, 1)

                def take(q):
                    b = halves[q - 1]
                    dve.wait_ge(scores_mm, t * (LV + 1) + q + 1)
                    dve.wait_ge(scores_in, t * (LV + 1) + q)
                    if not isinstance(t, int):
                        dve.sem_inc(carried, 1)
                    m = masks[:, MOFF[b]:MOFF[b] + 1, :].rearrange("p o (n b) -> p o n b", b=b)
                    dve.copy_predicated(blocks(sct[:, :, :], 2 * b)[:, :, :, b:],
                                        m.to_broadcast([P, HEADS, 64 // b, b]),
                                        blocks(ps[6 + q % 2][:, 0:256].rearrange("p (h c) -> p h c", h=HEADS), b))\
                        .then_inc(scores_in, 1)

                diff(1)
                diff(2)
                dve.wait_ge(scores_mm, t * (LV + 1) + 1)
                if some(t):
                    dve.wait_ge(o_mm, t)
                dve.tensor_tensor(sct[:, :, :], ps[1][:, :].rearrange("p (h c) -> p h c", h=HEADS),
                                  ident[:, :].rearrange("p (o c) -> p o c", o=1).to_broadcast([P, HEADS, P]),
                                  ALU.mult).then_inc(scores_in, 1)
                for q in range(1, L + 1):
                    b = halves[q - 1]
                    dve.wait_ge(exps_ready, t * (LV + 3) + q)
                    dve.wait_ge(scores_mm, t * (LV + 1) + max(q - 1, 1))
                    dve.tensor_tensor(blocks(qsc[:, q % 2], b), blocks(qt, 2 * b)[:, :, :, b:],
                                      blocks(ediff[:, q % 2], 2 * b)[:, :, :, b:], ALU.mult)\
                        .then_inc(q_scaled, 1)
                    if q + 2 <= L:
                        diff(q + 2)
                    if q >= 2:
                        take(q - 1)
                odd = L if L % 2 else L - 1
                dve.wait_ge(k_scaled, t * (LV + 2) + odd + 1)
                dve.wait_ge(q_scaled, t * (LV + 1) + odd)
                w = P if prompt else SL
                bv, ev = blocks(bt, w), blocks(ediff[:, 1], w)
                dve.tensor_tensor(ev, bv[:, :, :, w - 1:w].to_broadcast([P, HEADS, P // w, w]), bv, ALU.subtract)\
                    .then_inc(diff_ready, 1)
                take(L)
                dve.wait_ge(exps_ready, t * (LV + 3) + L + 1)
                dve.tensor_tensor(ediff[:, 0], ediff[:, 0], qt, ALU.mult).then_inc(q_scaled, 1)
                if prompt:
                    dve.wait_ge(exps_ready, t * (LV + 3) + L + 3)
                    dve.wait_ge(o_mm, t + 1)
                    dve.wait_ge(state_ready, t + 1)
                    dve.tensor_tensor(stt[:, :, :], stt[:, :, :], ebl[:, :, 0:1].to_broadcast([P, HEADS, P]), ALU.mult)\
                        .then_inc(state_decayed, 1)
                    dve.wait_ge(sd_mm, t + 1)
                    dve.wait_ge(state_decayed, t + 1)
                    dve.tensor_tensor(stt[:, :, :], stt[:, :, :],
                                      ps[4][:, :].rearrange("p (h c) -> p h c", h=HEADS), ALU.add)\
                        .then_inc(state_ready, 1)
                else:
                    dve.wait_ge(v_ready, NT)
                    dve.wait_ge(k_scaled, (NT - 1) * (LV + 2))
                    for h in range(HEADS):
                        dve.tensor_tensor(vms[:, h, 0:SEQ].rearrange("p (q v) -> p q v", q=NS),
                                          vtok[:, h:h + 1, :].to_broadcast([P, NS, P]),
                                          smask[:, :].rearrange("p (q o) -> p q o", o=1).to_broadcast([P, NS, P]),
                                          ALU.mult).then_inc(vm_ready, 1)
                    dve.wait_ge(exps_ready, t * (LV + 3) + L + 3)
                    dve.wait_ge(o_mm, NT)
                    for h in range(HEADS):
                        sv = sin_[:, h, 0:SEQ].rearrange("p (q v) -> p q v", q=NS)
                        dve.tensor_tensor(sv, sv, ebl[:, h, :].rearrange("p (q o) -> p q o", o=1)
                                          .to_broadcast([P, NS, P]), ALU.mult).then_inc(sstate_decayed, 1)
                    for h in range(HEADS):
                        dve.wait_ge(sd_mm, NT + h)
                        dve.wait_ge(sstate_decayed, h + 1)
                        for c in range(2):
                            ins = dve.tensor_tensor(sin_[:, h, c * 512:(c + 1) * 512], ps[4 + c][:, :],
                                                    sin_[:, h, c * 512:(c + 1) * 512], ALU.add)
                        ins.then_inc(sstate_ready, 1)

            tile(0, True)
            with dve.Fori(1, NT - 1) as t:
                tile(t, True)
            tile(NT - 1, False)

            def onorm_in(e):
                if some(e - 1):
                    dve.wait_ge(o_normed, e - 1)
                dve.wait_ge(onorm_mm, e + 1)
                dve.tensor_scalar(orr[:, e % 2, :], ps[6 + e % 2][:, 0:TB], 1.0 / P, EPS, ALU.mult, ALU.add)\
                    .then_inc(onorm_out, 1)

            def onorm(e):
                h, tb = divmod(e, NTB)
                dve.wait_ge(osqrt, e + 1)
                dve.reciprocal(orr[:, e % 2, :], orr[:, e % 2, :]).then_inc(oinv, 1)
                dve.wait_ge(oinv, e + 1)
                o = work[:, h, tbs(tb)]
                dve.scalar_tensor_tensor(o, o, vec[:, V_OUTG:V_OUTG + 1], orr[:, e % 2, :], ALU.mult, ALU.mult)\
                    .then_inc(o_normed, 1)
            for e in range(HEADS * NTB):
                onorm_in(e)
                if e:
                    onorm(e - 1)
            onorm(HEADS * NTB - 1)

            for gi, w in enumerate(POOLW):
                src = (padb, padc)[gi % 2]
                dve.wait_ge(sums_ready, gi + 1)
                if some(NTB * gi):
                    dve.wait_ge(pool_mm, NTB * gi)
                dve.scalar_tensor_tensor(src[:, HIST:HIST + w - 1], src[:, HIST:HIST + w - 1], float(w),
                                         cinv[:, 0:w - 1], ALU.mult, ALU.mult).then_inc(edge_fixed, 1)
                dve.wait_ge(edge_fixed, gi + 1)
                dve.scalar_tensor_tensor(pooled[:, 0:SEQ], src[:, HIST:HIST + SEQ], 1.0 / w, work[:, 16 + gi, 0:SEQ],
                                         ALU.mult, ALU.subtract)
                dve.scalar_tensor_tensor(
                    pooled[:, SEQ:TOK].rearrange("p (q s) -> p q s", q=NS),
                    src[:, HIST + SEQ:PADW].rearrange("p (q s) -> p q s", q=NS)[:, :, HIST:], 1.0 / w,
                    work[:, 16 + gi, SEQ:TOK].rearrange("p (q s) -> p q s", q=NS), ALU.mult, ALU.subtract)\
                    .then_inc(pooled_ready, 1)
                for tb in range(NTB):
                    dve.wait_ge(pool_mm, NTB * gi + tb + 1)
                    dve.tensor_scalar(work[:, 4 + gi, tbs(tb)], ps[3 + tb][:, 0:TB], vec[:, V_PSC + gi:V_PSC + gi + 1],
                                      None, ALU.mult).then_inc(yb_ready, 1)

            for k in range(KD):
                dve.wait_ge(mh_ready, k + 1)
                dve.tensor_tensor(ml[:, k, :], work[:, k, :], mh[:, k, :].bitcast(F32), ALU.subtract)\
                    .then_inc(ml_ready, 1)

            n0, g0, t0 = PLAN.at["abo"]

            def abo(i):
                for u in range(2):
                    low(n0 + 4 * i + 2 * u + 1, n0 + 2 * u + 1)
                    low(n0 + 4 * i + 2 * u + 2, n0 + 2 * u + 2)
                    for tb in range(NTB):
                        add_down(2 * i + u, tb, g0 + 6 * i + 3 * u + tb, g0 + 3 * u + tb, t0 + 8 * i + 4 * u + 2 + tb)
                    for tb in range(NTB):
                        x_low(24 + 6 * i + 3 * u + tb, 2 * i + u, tb)
            dve.wait_ge(xs_init, KD)
            loop(dve, 4, abo)
            inv_rms(1)

            def finish_down(n0, g0, t0, k, last, split=0):
                prev = None
                for q in range(4):
                    if q >= split and n0 + q + 1 < PIECES:
                        low(n0 + q + 1, n0 + q + 1)
                    for m in range(6 * q, 6 * q + 6):
                        d, tb = divmod(m, NTB)
                        add_down(d, tb, g0 + m, g0 + m, t0 + m + 1)
                        if not last:
                            if prev is not None:
                                x_low(*prev)
                            prev = (24 * k + m, d, tb)
                if prev is not None:
                    x_low(*prev)

            def ffn(l):
                c3 = convc[:, :]
                cs = conv_step[l]
                done0 = 2 * (STEPS * l + (8 if l else 0))
                for c in range(2):
                    dve.memset(apad[:, c, 0:2], 0.0)
                dve.wait_ge(convc_ready, 1 + l)

                def conv_unit(c, fc, ch, sg, tick):
                    pad = apad[:, c, :]
                    padp, pads = pad[:, 0:2 + SEQ], pad[:, 2 + SEQ:APW].rearrange("p (q s) -> p q s", q=NS)
                    for tb in range(2):
                        scaled(padp[:, 2 + tb * TB:2 + (tb + 1) * TB], sg + tb, tb, tick + tb)
                    dve.wait_ge(pe_tick, tick + 2)
                    bank = ps[(sg + 2) % BANKS]
                    dve.tensor_tensor(padp[:, 2 + 2 * TB:2 + SEQ], bank[:, 0:256], rstd[:, 2 * TB:SEQ], ALU.mult)
                    dve.tensor_tensor(pads[:, :, 2:], bank[:, 256:TB].rearrange("p (q s) -> p q s", q=NS),
                                      rstd[:, SEQ:TOK].rearrange("p (q s) -> p q s", q=NS), ALU.mult)\
                        .then_inc(acc_free, 1)
                    hist = c3[:, 0:16 * FJ].rearrange("p (q j f) -> p q j f", q=NS, j=2)
                    dve.tensor_scalar(pads[:, :, 0:2], hist[:, :, :, fc].rearrange("p q j o -> p q (j o)"), 1.0, None,
                                      ALU.mult).then_inc(cs, 1)

                def conv_taps(c, fc, ch, g):
                    pad = apad[:, c, :]
                    padp, pads = pad[:, 0:2 + SEQ], pad[:, 2 + SEQ:APW].rearrange("p (q s) -> p q s", q=NS)
                    outp = cv[:, c, 0:SEQ]
                    outs = cv[:, c, SEQ:TOK].rearrange("p (q s) -> p q s", q=NS)
                    col = lambda r: c3[:, ds(fc + r * FJ, 1)]
                    dve.wait_ge(acc_free, g)
                    dve.wait_ge(cs, 9 * ch + 1)
                    if some(ch - 1):
                        dve.wait_ge(y_formed[l], ch - 1)
                    dve.tensor_scalar(outp, padp[:, 0:SEQ], col(16), col(19), ALU.mult, ALU.add).then_inc(cs, 1)
                    dve.tensor_scalar(outs, pads[:, :, 0:SL], col(16), col(19), ALU.mult, ALU.add).then_inc(cs, 1)
                    for j in (1, 2):
                        dve.wait_ge(cs, 9 * ch + 2 * j)
                        dve.scalar_tensor_tensor(outp, padp[:, j:j + SEQ], col(16 + j), outp, ALU.mult, ALU.add)\
                            .then_inc(cs, 1)
                        dve.wait_ge(cs, 9 * ch + 2 * j + 1)
                        dve.scalar_tensor_tensor(outs, pads[:, :, j:j + SL], col(16 + j), outs, ALU.mult, ALU.add)\
                            .then_inc(cs, 1)
                    dve.tensor_scalar(tails[:, 0:2, ds(fc, 1)].rearrange("p r o -> p (r o)"), padp[:, SEQ:SEQ + 2], 1.0,
                                      None, ALU.mult)\
                        .then_inc(cs, 1)
                    dve.tensor_scalar(tails[:, 2:18, ds(fc, 1)].rearrange("p (q j) o -> p q (j o)", q=NS),
                                      pads[:, :, SL:SL + 2], 1.0, None, ALU.mult).then_inc(cs, 1)

                def ups(n, sn, g, sg, tick, s):
                    for u in range(4):
                        low(n + 2 * u + 1, sn + 2 * u + 1)
                        low(n + 2 * u + 2, sn + 2 * u + 2)
                        tk = tick + 4 * u + 2
                        if u < 2:
                            fc = 2 * s + u
                            conv_unit(u, ds(fc, 1), fc, sg + 3 * u, tk)
                            conv_taps(u, fc, fc, g + 3 * u + 3)
                        else:
                            if some(2 * s + done0):
                                dve.wait_ge(yl_ready, 2 * s + done0)
                            for tb in range(NTB):
                                scaled(gate[:, u - 2, tbs(tb)], sg + 3 * u + tb, tb, tk + tb)

                n0, g0, t0 = PLAN.at[f"f{l}0"]
                ups(n0, n0, g0, g0, t0, 0)
                n1, g1, t1 = PLAN.at[f"f{l}"]

                def step(i):
                    ups(n1 + 12 * i, n1, g1 + 36 * i, g1, t1 + 40 * i, i + 1)
                    for q in range(4):
                        low(n1 + 12 * i + 9 + q, n1 + 9 + q)
                        for m in range(6 * q, 6 * q + 6):
                            d, tb = divmod(m, NTB)
                            add_down(d, tb, g1 + 36 * i + 12 + m, g1 + 12 + m, t1 + 40 * i + 17 + m)
                loop(dve, STEPS - 1, step)
                n2, g2, t2 = PLAN.at[f"f{l}9"]
                finish_down(n2, g2, t2, 2 + 2 * l, l == 1)
                inv_rms(2 + 2 * l)

            ffn(0)

            n0, g0, t0 = PLAN.at["v"]
            dve.wait_ge(tails_stored, 64)

            def v_unit(par, n, sn, sg, tick):
                low(n + 1, sn + 1)
                low(n + 2, sn + 2)
                for tb in range(NTB):
                    scaled(vtmp[:, par, tbs(tb)], sg + tb, tb, tick + tb)

            def v_turned(j, sg, tick):
                for tb in range(NTB):
                    bank = ps[(sg + tb) % BANKS]
                    dve.wait_ge(pe_tick, tick + tb)
                    for k in range(3):
                        dve.bn_stats(stats[:, 3 * tb + k, ds(j, 1), :], bank[:, k * P:(k + 1) * P])
                    dve.tensor_scalar(work[:, 8 + j, tbs(tb)], bank[:, 0:TB], 1.0, None, ALU.mult)\
                        .then_inc(acc_free, 1)
            v_unit(0, n0, n0, g0, t0 + 2)

            def vstep(i):
                for u in range(2):
                    v_unit(1 - u, n0 + 2 + 4 * i + 2 * u, n0 + 2 + 2 * u, g0 + 3 + 6 * u, t0 + 14 * i + 6 + 7 * u)
                    v_turned(2 * i + u, g0 + 6 + 6 * u, t0 + 14 * i + 9 + 7 * u)
            loop(dve, 7, vstep)
            te = t0 + 4 + 98
            v_unit(1, n0 + 30, n0 + 30, g0 + 87, te + 2)
            v_turned(14, g0 + 90, te + 5)
            v_turned(15, g0 + 93, te + 8)
            dve.wait_ge(acc_free, g0 + 96)
            for t in range(NT):
                ins = dve.bn_aggr(mv[:, t, :], stats[:, t, :, :].rearrange("p j s -> p (j s)"))
            ins.then_inc(ln_stats, 1)
            dve.wait_ge(ln_sqrt, 1)
            dve.reciprocal(lrs[:, :], lrs[:, :]).then_inc(ln_stats, 1)
            dve.wait_ge(ln_stats, 2)
            for t in [NT - 1] + list(range(NT - 1)):
                v = work[:, 8:24, t * P:(t + 1) * P]
                dve.tensor_scalar(v, v, mv[:, t, 0:1], lrs[:, t:t + 1], ALU.subtract, ALU.mult)\
                    .then_inc(ln_done, 1)

            _, g0, t0 = PLAN.at["mix"]
            dve.wait_ge(wsum_ready, 4)
            dve.wait_ge(bsb_ready, 1)

            def addend(j):
                if j > 1:
                    dve.wait_ge(acc_free, g0 + 3 * (j - 1))
                dve.scalar_tensor_tensor(adde[:, j % 2, :], wsum[:, j // 2, :], vec[:, V_LNB + j:V_LNB + j + 1],
                                         bsb[:, j // 2, :], ALU.mult, ALU.add).then_inc(addend_ready, 1)
            addend(0)
            for j in range(CJ):
                if j + 1 < CJ:
                    addend(j + 1)
                dve.wait_ge(addend_ready, j + 1)
                gain = vec[:, V_LNG + j:V_LNG + j + 1]
                for tb in range(NTB):
                    g = g0 + 3 * j + tb
                    dve.wait_ge(pe_tick, t0 + 3 * j + tb + 1)
                    bank = ps[g % BANKS]
                    if tb == 2 and j == 0:
                        dve.wait_ge(v_out_used, 1)
                    nt = 3 if tb < 2 else 2
                    out = work[:, 8 + j, tb * TB:tb * TB + nt * P].rearrange("p (t c) -> p t c", c=P)
                    ins = dve.scalar_tensor_tensor(
                        out, bank[:, 0:nt * P].rearrange("p (t c) -> p t c", c=P), gain,
                        adde[:, j % 2:j % 2 + 1, 0:P].to_broadcast([P, nt, P]), ALU.mult, ALU.add)
                    if tb == 2:
                        ins = dve.scalar_tensor_tensor(work[:, 8 + j, SEQ:TOK], bank[:, 2 * P:TB], gain,
                                                       adde[:, j % 2, P:2 * P], ALU.mult, ALU.add)
                    ins.then_inc(acc_free, 1)

            def u_groups(s, u, sg, tick, between=None):
                def into(tb):
                    if some(6 * s + 3 * u + tb - 1):
                        dve.wait_ge(u_gated, 6 * s + 3 * u + tb - 1)
                    scaled(ut[:, (3 * u + tb) % 2, :], sg + tb, tb, tick + tb)

                def gated(tb):
                    m = work[:, 8 + 2 * s + u, tbs(tb)]
                    dve.wait_ge(u_activated, 6 * s + 3 * u + tb + 1)
                    dve.tensor_tensor(m, ut[:, (3 * u + tb) % 2, :], m, ALU.mult).then_inc(u_gated, 1)
                into(0)
                into(1)
                if between:
                    between()
                gated(0)
                into(2)
                gated(1)
                gated(2)

            n0, g0, t0 = PLAN.at["u0"]
            done0 = 2 * STEPS
            dve.wait_ge(vout_stored, 16)
            for u in range(2):
                low(n0 + 2 * u + 1, n0 + 2 * u + 1)
                low(n0 + 2 * u + 2, n0 + 2 * u + 2)
                u_groups(0, u, g0 + 3 * u, t0 + 4 * u + 2)
            n1, g1, t1 = PLAN.at["u"]

            def y_low(s):
                for c in range(2):
                    dve.wait_ge(yh_ready, done0 + 2 * s + c + 1)
                    dve.tensor_tensor(yl[:, c, :], work[:, 8 + 2 * s + c, :], yh[:, c, :].bitcast(F32), ALU.subtract)\
                        .then_inc(yl_ready, 1)

            def ustep(i):
                n, t = n1 + 8 * i, t1 + 32 * i
                low(n + 1, n1 + 1)
                low(n + 2, n1 + 2)
                y_low(i)
                u_groups(i + 1, 0, g1, t + 2, lambda: low(n + 3, n1 + 3))
                low(n + 4, n1 + 4)
                u_groups(i + 1, 1, g1 + 3, t + 6, lambda: low(n + 5, n1 + 5))
                for q in range(4):
                    if q:
                        low(n + 5 + q, n1 + 5 + q)
                    for m in range(6 * q, 6 * q + 6):
                        d, tb = divmod(m, NTB)
                        add_down(d, tb, g1 + 30 * i + 6 + m, g1 + 6 + m, t + 9 + m)
            dve.wait_ge(xs_init, 2 * KD)
            loop(dve, 7, ustep)
            n2, g2, t2 = PLAN.at["u9"]
            low(n2 + 1, n2 + 1)
            y_low(7)
            finish_down(n2, g2, t2, 3, False, split=1)
            inv_rms(3)

            ffn(1)
            for k in range(24):
                d, tb = divmod(k, NTB)
                x = xs[:, d, tbs(tb)]
                dve.scalar_tensor_tensor(x, x, vec[:, V_FIN + d:V_FIN + d + 1], rstd[:, tbs(tb)], ALU.mult, ALU.mult)\
                    .then_inc(y_normed, 1)
            _, g0, t0 = PLAN.at["out"]
            for t in range(NT):
                if some(16 * (t // 2)):
                    dve.wait_ge(y_stored[t % 2], 16 * (t // 2))
                for b in range(2):
                    g = g0 + 2 * t + b
                    dve.wait_ge(pe_tick, t0 + 2 * t + b + 1)
                    dve.tensor_copy(otok[:, t % 2, b * 512:(b + 1) * 512], ps[g % BANKS][:, :])\
                        .then_inc(acc_free, 1)

        @block.scalar
        def _(act):
            def high(n, s, tick):
                act.wait_ge(w_scaled, n + 1)
                if some(tick):
                    act.wait_ge(pe_tick, tick)
                act.activation(wh[:, s % 2, :], raw[:, s % RAWS, :], ACT.Copy).then_inc(w_high_ready, 1)

            def finished(e, d, tb, g, sq, need_high=True):
                act.wait_ge(acc_free, g + 1)
                if need_high:
                    act.activation(xh[:, d, tbs(tb)], xs[:, d, tbs(tb)], ACT.Copy).then_inc(xh_ready, 1)
                return e

            def squared(e, par, d, tb, sq):
                if some(e - 1):
                    act.wait_ge(ssq_added, e - 1)
                if not isinstance(e, int):
                    act.sem_inc(carried, 1)
                act.activation(sq[:, par, :], xs[:, d, tbs(tb)], ACT.Square).then_inc(square_ready, 1)

            def rms(k):
                for tb in range(NTB):
                    act.wait_ge(norm_mm, NTB * k + tb + 1)
                    act.activation(rstd[:, tbs(tb)], ps[6 + (NTB * k + tb) % 2][:, 0:TB], ACT.Sqrt,
                                   bias=eps_c, scale=1.0 / D).then_inc(rms_ready, 1)

            act.wait_ge(vec_mm, 1)
            act.activation(vec[:, 0:NVEC], ps[6][:, 0:NVEC], ACT.Copy).then_inc(vec_ready, 1)
            for g in range(24):
                tb, d = divmod(g, KD)
                finished(g, d, tb, g, sq_e)
                squared(g, g % 2, d, tb, sq_e)
            act.wait_ge(eps_ready, 1)
            rms(0)
            high(0, 0, 0)
            n0, g0, t0 = PLAN.at["ab"]
            high(1, 1, 0)

            def ab(i):
                for p, tk in ((2, 1), (3, 4), (4, 5), (5, 8)):
                    high(n0 + 4 * i + p, n0 + p, t0 + 8 * i + tk)
            loop(act, 10, ab)

            act.wait_ge(acc_free, g0 + 60)
            qs, zs, gs, ls = work[:, 0:4, :], work[:, 4:8, :], work[:, 12:16, :], work[:, 20:24, :]
            act.activation(qs, qs, ACT.Silu).then_inc(q_act, 1)
            act.activation(gs, gs, ACT.Silu).then_inc(g_act, 1)
            act.activation(ls, zs, ACT.Abs).then_inc(act_prep, 1)
            act.wait_ge(act_prep, 1)
            act.activation(ls, ls, ACT.Exp, scale=-1.0).then_inc(act_prep, 1)
            act.wait_ge(act_prep, 2)
            act.activation(ls, ls, ACT.Ln, bias=1.0).then_inc(act_prep, 1)
            act.wait_ge(logf_used, 1)
            act.activation(zs, zs, ACT.Exp).then_inc(k_ready, 1)
            act.wait_ge(decay_ready, HEADS)

            def tile(t, prompt):
                L = len(HALF[prompt])
                x0 = t * (LV + 3)
                for q in range(1, L + 1):
                    act.wait_ge(diff_ready, t * (LV + 1) + q)
                    act.activation(ediff[:, q % 2], ediff[:, q % 2], ACT.Exp).then_inc(exps_ready, 1)
                    if q == 1:
                        act.wait_ge(v_mm, t + 1)
                        if some(t):
                            act.wait_ge(sd_mm, t)
                        act.activation(vtok[:, :, :], ps[0][:, :].rearrange("p (h c) -> p h c", h=HEADS), ACT.Copy)\
                            .then_inc(v_ready, 1)
                even = L if L % 2 == 0 else L - 1
                act.wait_ge(q_scaled, t * (LV + 1) + even)
                act.wait_ge(k_scaled, t * (LV + 2) + even + 1)
                act.activation(ediff[:, 0], work[:, 20:24, tile_cols(t)], ACT.Exp).then_inc(exps_ready, 1)
                act.wait_ge(diff_ready, t * (LV + 1) + L + 1)
                act.activation(ediff[:, 1], ediff[:, 1], ACT.Exp).then_inc(exps_ready, 1)
                act.wait_ge(state_ready, t + 1)
                if prompt:
                    last = blocks(work[:, 20:24, tile_cols(t)], P)[:, :, :, P - 1]
                    act.activation(ebl[:, :, 0:1], last, ACT.Exp).then_inc(exps_ready, 1)
                else:
                    last = blocks(work[:, 20:24, tile_cols(t)], SL)[:, :, :, SL - 1]
                    act.activation(ebl[:, :, :], last, ACT.Exp).then_inc(exps_ready, 1)
                act.wait_ge(kd_mm, t + 1)
                act.activation(kdt[:, :, :], ps[2][:, :].rearrange("p (h c) -> p h c", h=HEADS), ACT.Copy)\
                    .then_inc(kdt_ready, 1)
                act.wait_ge(o_mm, t + 1)
                act.activation(work[:, 0:4, tile_cols(t)], ps[3][:, :].rearrange("p (h c) -> p h c", h=HEADS),
                               ACT.Copy).then_inc(o_out, 1)

            tile(0, True)
            with act.Fori(1, NT - 1) as t:
                tile(t, True)
            tile(NT - 1, False)

            act.wait_ge(o_out, NT)
            act.wait_ge(kd_mm, NT)
            act.wait_ge(hist_mm, 1)
            act.activation(histt[:, :, :], ps[0][:, 0:480].rearrange("p (h c) -> p h c", h=HEADS), ACT.Copy)\
                .then_inc(histt_ready, 1)
            for r in range(2):
                act.wait_ge(prow_mm, r + 1)
                act.activation(prow[:, r, :], ps[1 + r][:, :], ACT.Copy).then_inc(prow_ready, 1)

            def osquare(e):
                h, tb = divmod(e, NTB)
                if some(e - 1):
                    act.wait_ge(onorm_mm, e - 1)
                act.activation(osq[:, e % 2, :], work[:, h, tbs(tb)], ACT.Square).then_inc(osq_ready, 1)
            osquare(0)
            for e in range(HEADS * NTB):
                if e + 1 < HEADS * NTB:
                    osquare(e + 1)
                act.wait_ge(onorm_out, e + 1)
                act.activation(orr[:, e % 2, :], orr[:, e % 2, :], ACT.Sqrt).then_inc(osqrt, 1)
            for k in range(KD):
                if k == 0:
                    act.wait_ge(o_fin, HEADS * NTB)
                    act.wait_ge(yb_ready, HEADS * NTB)
                act.activation(mh[:, k, :], work[:, k, :], ACT.Copy).then_inc(mh_ready, 1)

            n0, g0, t0 = PLAN.at["abo"]

            def abo(i):
                for u in range(2):
                    for p, tk in ((2, 1), (3, 4)):
                        high(n0 + 4 * i + 2 * u + p, n0 + 2 * u + p, t0 + 8 * i + 4 * u + tk)
                    for tb in range(NTB):
                        e = 24 + 6 * i + 3 * u + tb
                        finished(e, 2 * i + u, tb, g0 + 6 * i + 3 * u + tb, sq_e)
                        squared(e, (3 * u + tb) % 2, 2 * i + u, tb, sq_e)
            loop(act, 4, abo)
            rms(1)

            def finish_down(n0, g0, t0, k, last):
                for q in range(4):
                    if n0 + q + 2 < PIECES:
                        high(n0 + q + 2, n0 + q + 2, t0 + 6 * (q + 1))
                    for m in range(6 * q, 6 * q + 6):
                        d, tb = divmod(m, NTB)
                        finished(24 * k + m, d, tb, g0 + m, sq_b, not last)
                        squared(24 * k + m, m % 2, d, tb, sq_b)

            def ffn(l):
                done0 = 2 * (STEPS * l + (8 if l else 0))
                cs = conv_step[l]
                act.wait_ge(convc_mm, 1 + l)
                act.activation(convc[:, :], ps[7][:, 0:440], ACT.Copy).then_inc(convc_ready, 1)

                def y_high(s):
                    for c in range(2):
                        act.wait_ge(y_formed[l], 2 * s + c + 1)
                        act.activation(yh[:, c, :], gate[:, c, :], ACT.Copy).then_inc(yh_ready, 1)

                def gelu(c, ch):
                    act.wait_ge(cs, 9 * ch + 7)
                    act.activation(cv[:, c, :], cv[:, c, :], ACT.Gelu).then_inc(gelu_done[l], 1)

                def ups(n, sn, tick, s):
                    for p, tk in ((2, 1), (3, 4), (4, 5), (5, 8), (6, 9), (7, 12), (8, 13), (9, 16)):
                        high(n + p, sn + p, tick + tk)
                        if p == 3:
                            gelu(0, 2 * s)
                        if p == 5:
                            gelu(1, 2 * s + 1)

                n0, g0, t0 = PLAN.at[f"f{l}0"]
                ups(n0, n0, t0, 0)
                n1, g1, t1 = PLAN.at[f"f{l}"]

                def step(i):
                    y_high(i)
                    ups(n1 + 12 * i, n1, t1 + 40 * i, i + 1)
                    for q in range(4):
                        high(n1 + 12 * i + 10 + q, n1 + 10 + q, t1 + 40 * i + 16 + 6 * (q + 1))
                loop(act, STEPS - 1, step)
                n2, g2, t2 = PLAN.at[f"f{l}9"]
                y_high(STEPS - 1)
                finish_down(n2, g2, t2, 2 + 2 * l, l == 1)
                rms(2 + 2 * l)
                for b, (r0, r1) in enumerate(((0, 44), (44, 172), (172, 300), (300, 396))):
                    if b == 0:
                        act.wait_ge(tails_mm, 1 + l)
                    act.activation(trow[0:r1 - r0, b, :], ps[7][0:r1 - r0, b * P:(b + 1) * P], ACT.Copy)\
                        .then_inc(trow_ready, 1)

            ffn(0)

            for m in range(2):
                for b in range(2):
                    act.wait_ge(wt_mm, 2 * m + b + 1)
                    act.activation((wtp, wts)[m][:, 4 * b:4 * b + 4, :],
                                   ps[6 + b][:, :].rearrange("p (j c) -> p j c", c=P), ACT.Copy)\
                        .then_inc(wt_ready, 1)
            for m in range(2):
                for b in range(2):
                    act.wait_ge(wsum_mm, 2 * m + b + 1)
                    act.activation(wsum[:, 4 * b:4 * b + 4, m * P:(m + 1) * P],
                                   ps[6 + b][:, :].rearrange("p (j c) -> p j c", c=P), ACT.Copy)\
                        .then_inc(wsum_ready, 1)

            n0, g0, t0 = PLAN.at["v"]

            def v_gelu(par, g):
                act.wait_ge(acc_free, g)
                act.activation(vtmp[:, par, :], vtmp[:, par, :], ACT.Gelu).then_inc(v_activated, 1)
            high(n0 + 2, n0 + 2, t0 + 1)
            high(n0 + 3, n0 + 3, t0 + 4)
            v_gelu(0, g0 + 3)

            def vstep(i):
                n, t, g = n0 + 2 + 4 * i, t0 + 4 + 14 * i, g0 + 3 + 12 * i
                high(n + 2, n0 + 4, t + 1)
                high(n + 3, n0 + 5, t + 4)
                v_gelu(1, g + 3)
                high(n + 4, n0 + 6, t + 8)
                high(n + 5, n0 + 7, t + 11)
                v_gelu(0, g + 9)
            loop(act, 7, vstep)
            te = t0 + 4 + 98
            high(n0 + 32, n0 + 32, te + 1)
            high(n0 + 33, n0 + 33, te + 4)
            v_gelu(1, g0 + 90)
            act.wait_ge(ln_stats, 1)
            act.activation(lrs[:, :], mv[:, :, 1], ACT.Sqrt, bias=eps_c).then_inc(ln_sqrt, 1)

            n0, g0, t0 = PLAN.at["u0"]
            act.wait_ge(vout_stored, 16)

            def u_gelu(u, g):
                for tb in range(NTB):
                    act.wait_ge(acc_free, g + 3 * u + tb + 1)
                    act.activation(ut[:, (3 * u + tb) % 2, :], ut[:, (3 * u + tb) % 2, :], ACT.Gelu)\
                        .then_inc(u_activated, 1)
            for p, tk in ((2, 1), (3, 4), (4, 5), (5, 8)):
                high(n0 + p, n0 + p, t0 + tk)
                if p in (3, 5):
                    u_gelu((p - 3) // 2, g0)
            n1, g1, t1 = PLAN.at["u"]

            def uy_high(s):
                for c in range(2):
                    act.wait_ge(u_gated, 6 * s + 3 * c + 3)
                    act.activation(yh[:, c, :], work[:, 8 + 2 * s + c, :], ACT.Copy).then_inc(yh_ready, 1)

            def ustep(i):
                uy_high(i)
                for p, tk in ((2, 1), (3, 4), (4, 5), (5, 8)):
                    high(n1 + 8 * i + p, n1 + p, t1 + 32 * i + tk)
                    if p in (3, 5):
                        u_gelu((p - 3) // 2, g1 + 30 * i)
                for q in range(4):
                    high(n1 + 8 * i + 6 + q, n1 + 6 + q, t1 + 32 * i + 8 + 6 * (q + 1))
            loop(act, 7, ustep)
            n2, g2, t2 = PLAN.at["u9"]
            uy_high(7)
            finish_down(n2, g2, t2, 3, False)
            rms(3)
            ffn(1)

        @block.gpsimd
        def _(pool):
            chain = [0]

            def linked(ins):
                chain[0] += 1
                ins.then_inc(setup_chain, 1)
                pool.wait_ge(setup_chain, chain[0])

            def scale_weights(s, i, per, gain):
                n = per * i + s
                pool.wait_ge(raw_loaded[s % RAWS], 16 * (s // RAWS + 1) + (16 * (per // RAWS)) * i)
                if gain is None:
                    pool.wait_ge(w_scaled, n)
                    pool.sem_inc(w_scaled, 1)
                    return
                r = raw[:, s % RAWS, :].rearrange("p (k c) -> p k c", k=4)
                c = gain + 4 * (s % 2)
                g = vec[:, c:c + 4].rearrange("p (k o) -> p k o", o=1).to_broadcast([P, 4, P])
                pool.tensor_tensor(r, r, g, ALU.mult).then_inc(w_scaled, 1)

            def add_square(e, par, tb, sq, ssq):
                pool.wait_ge(square_ready, e + 1)
                if some(e):
                    pool.wait_ge(ssq_added, e)
                pool.tensor_tensor(ssq[:, tbs(tb)], ssq[:, tbs(tb)], sq[:, par, :], ALU.add)\
                    .then_inc(ssq_added, 1)

            linked(pool.memset(ident[:, :], 0.0))
            pool.affine_select(out=ident[:, :], in_=ident[:, :], compare_op=ALU.not_equal, fill=1.0, base=0,
                               pattern=[[-1, P]], channel_multiplier=1).then_inc(ident_ready, 1)
            pool.memset(ones[:, :], 1.0)
            pool.memset(eps_c, EPS).then_inc(eps_ready, 1)
            linked(pool.memset(ssq_e[:, :], 0.0))
            linked(pool.memset(maskf[:, :, :], 1.0))
            for b, off in MOFF.items():
                m = maskf[:, off, :].rearrange("p (n b) -> p n b", b=b)
                linked(pool.affine_select(out=m, in_=m, compare_op=ALU.is_ge, fill=0.0, base=0,
                                          pattern=[[-2 * b, 64 // b], [0, b]], channel_multiplier=1))
                linked(pool.affine_select(out=m, in_=m, compare_op=ALU.is_ge, fill=0.0, base=b - 1,
                                          pattern=[[2 * b, 64 // b], [0, b]], channel_multiplier=-1))
            pool.tensor_copy(masks[:, :, :], maskf[:, :, :])
            linked(pool.memset(smask[:, :], 1.0))
            linked(pool.affine_select(out=smask[:, :], in_=smask[:, :], compare_op=ALU.is_ge, fill=0.0, base=0,
                                      pattern=[[-SL, NS]], channel_multiplier=1))
            pool.affine_select(out=smask[:, :], in_=smask[:, :], compare_op=ALU.is_ge, fill=0.0, base=SL - 1,
                               pattern=[[SL, NS]], channel_multiplier=-1).then_inc(setup_done, 1)
            for g in range(24):
                add_square(g, g % 2, g // KD, sq_e, ssq_e)
            pool.wait_ge(vec_ready, 1)
            n0, _, _ = PLAN.at["ab"]

            def ab(i):
                for p in range(4):
                    scale_weights(n0 + p, i, 4, V_MIX)
            for p in range(4):
                scale_weights(n0 + p, 0, 4, V_MIX)
            pool.wait_ge(rstd_ready, NTB)
            linked(pool.memset(resetm[:, :], 1.0))
            pool.memset(resetm[:, 0:SEQ].rearrange("p (t c) -> p t c", c=P)[:, :, 0:1], 0.0)\
                .then_inc(reset_ready, 1)
            pool.memset(resetm[:, SEQ:TOK].rearrange("p (t c) -> p t c", c=SL)[:, :, 0:1], 0.0)\
                .then_inc(reset_ready, 1)
            pool.memset(ksc[:, 1], 0.0).then_inc(reset_ready, 1)
            with pool.Fori(1, 10) as i:
                ab(i)
            n0, _, _ = PLAN.at["abo"]
            for p in range(4):
                scale_weights(n0 + p, 0, 4, None)
            qs, zs, ls = work[:, 0:4, :], work[:, 4:8, :], work[:, 20:24, :]
            pool.wait_ge(logf_ready, 1)
            pool.tensor_tensor(zs, ls, zs, ALU.subtract).then_inc(logf_used, 1)
            pool.wait_ge(k_ready, 1)
            pool.wait_ge(reset_ready, 3)

            def tile(t, prompt):
                halves = HALF[prompt]
                L = len(halves)
                kt = work[:, 4:8, tile_cols(t)]
                one = ones[:, :].rearrange("p (o c) -> p o c", o=1).to_broadcast([P, HEADS, P])
                if some(t):
                    pool.wait_ge(v_mm, t)
                pool.tensor_tensor(icp[:, :, :], work[:, 8:12, tile_cols(t)], one, ALU.mult).then_inc(ic_ready, 1)
                if some(t * (LV + 1)):
                    pool.wait_ge(scores_mm, t * (LV + 1))
                pool.tensor_tensor(ksc[:, 0], kt, one, ALU.mult).then_inc(k_scaled, 1)
                for q in range(1, L + 1):
                    b = halves[q - 1]
                    if q > 1:
                        pool.wait_ge(scores_mm, t * (LV + 1) + q - 1)
                    pool.wait_ge(exps_ready, t * (LV + 3) + q)
                    if not isinstance(t, int):
                        pool.sem_inc(carried, 1)
                    pool.tensor_tensor(blocks(ksc[:, q % 2], 2 * b)[:, :, :, 0:b], blocks(kt, 2 * b)[:, :, :, 0:b],
                                       blocks(ediff[:, q % 2], 2 * b)[:, :, :, 0:b], ALU.mult)\
                        .then_inc(k_scaled, 1)
                pool.wait_ge(exps_ready, t * (LV + 3) + L + 2)
                if not isinstance(t, int):
                    pool.sem_inc(carried, 1)
                pool.tensor_tensor(ediff[:, 1], ediff[:, 1], kt, ALU.mult).then_inc(k_scaled, 1)

            tile(0, True)
            with pool.Fori(1, NT - 1) as t:
                tile(t, True)
            tile(NT - 1, False)

            pool.wait_ge(hist_loaded, 32)
            pool.wait_ge(histt_ready, 1)
            for c in range(15):
                pool.memset(cinv[:, c:c + 1], 1.0 / (c + 1))
            steps = [0]

            def stepped(ins):
                steps[0] += 1
                ins.then_inc(window_step, 1)
                pool.wait_ge(window_step, steps[0])

            def o_gate(e):
                h, tb = divmod(e, NTB)
                pool.wait_ge(o_normed, e + 1)
                o = work[:, h, tbs(tb)]
                pool.tensor_tensor(o, o, work[:, 12 + h, tbs(tb)], ALU.mult).then_inc(o_fin, 1)
            pool.wait_ge(g_act, 1)
            for gi, w in enumerate(POOLW):
                pads = pada[:, HIST + SEQ:PADW].rearrange("p (q s) -> p q s", q=NS)
                one = ones[:, 0:1]
                pool.memset(pada[:, 0:HIST], 0.0)
                pool.tensor_copy(pada[:, HIST:HIST + SEQ], work[:, 16 + gi, 0:SEQ])
                pool.tensor_copy(pads[:, :, 0:HIST], histt[:, gi, :].rearrange("p (q s) -> p q s", q=NS))
                stepped(pool.tensor_copy(pads[:, :, HIST:], work[:, 16 + gi, SEQ:TOK]
                                         .rearrange("p (q s) -> p q s", q=NS)))
                src, width = pada, 1
                if gi:
                    pool.wait_ge(pooled_ready, gi)
                for k in range(gi + 1):
                    dst = (padb, padc)[k % 2]
                    lo = 2 * width - 1
                    ins = pool.tensor_tensor(dst[:, lo:PADW], src[:, lo:PADW], src[:, lo - width:PADW - width],
                                             ALU.add)
                    stepped(ins)
                    src, width = dst, 2 * width
                pool.sem_inc(sums_ready, 1)
                for e in range(3 * gi, 3 * gi + 3):
                    o_gate(e)
            linked(pool.memset(ssq_e[:, :], 0.0))
            for k in range(KD):
                pool.wait_ge(ml_ready, k + 1)
                pool.tensor_tensor(xs[:, k, :], xh[:, k, :].bitcast(F32), xl[:, k, :].bitcast(F32), ALU.add)\
                    .then_inc(xs_init, 1)
            n0, _, _ = PLAN.at["abo"]

            def abo(i):
                for u in range(2):
                    for tb in range(NTB):
                        add_square(24 + 6 * i + 3 * u + tb, (3 * u + tb) % 2, tb, sq_e, ssq_e)
            with pool.Fori(0, 3) as i:
                for p in range(4, 8):
                    scale_weights(n0 + p, i, 4, None)
                abo(i)
            n0, _, _ = PLAN.at["f00"]
            for p in range(4):
                scale_weights(n0 + p, 0, 4, V_FFN)
            abo(3)

            def finish_down(n0, k, gain):
                for p in (2, 3):
                    scale_weights(n0 + p, 0, 4, None)
                if gain is not None:
                    for p in (4, 5):
                        scale_weights(n0 + p, 0, 4, gain)
                for q in range(4):
                    for m in range(6 * q, 6 * q + 6):
                        add_square(24 * k + m, m % 2, m % NTB, sq_b, ssq_b)

            def ffn(l):
                done0 = 2 * (STEPS * l + (8 if l else 0))
                gain = V_FFN + KD * l

                def y_prod(s):
                    for c in range(2):
                        pool.wait_ge(gelu_done[l], 2 * s + c + 1)
                        pool.wait_ge(acc_free, g_gate(s, c))
                        pool.tensor_tensor(gate[:, c, :], gate[:, c, :], cv[:, c, :], ALU.mult)\
                            .then_inc(y_formed[l], 1)

                def y_low(s):
                    for c in range(2):
                        pool.wait_ge(yh_ready, 2 * s + c + (done0 + 1))
                        pool.tensor_tensor(yl[:, c, :], gate[:, c, :], yh[:, c, :].bitcast(F32), ALU.subtract)\
                            .then_inc(yl_ready, 1)

                g1 = PLAN.at[f"f{l}"][1]

                def g_gate(s, c):
                    return s * 36 + (g1 - 3 + 3 * c)

                n0, _, _ = PLAN.at[f"f{l}0"]
                for p in range(2 if l else 4, 8):
                    scale_weights(n0 + p, 0, 4, gain)
                n1, _, _ = PLAN.at[f"f{l}"]
                with pool.Fori(0, STEPS - 1) as i:
                    for p in range(12):
                        scale_weights(n1 + p, i, 12, gain if p < 8 else None)
                        if p == 2:
                            y_prod(i)
                            y_low(i)
                n2, _, _ = PLAN.at[f"f{l}9"]
                linked(pool.memset(ssq_b[:, :], 0.0))
                scale_weights(n2, 0, 4, None)
                scale_weights(n2 + 1, 0, 4, None)
                y_prod(STEPS - 1)
                y_low(STEPS - 1)
                finish_down(n2, 2 + 2 * l, V_MIX + KD if l == 0 else None)

            ffn(0)
            pool.wait_ge(rstd_ready, NTB * 3)
            pool.memset(wsn[:, :, :], 0.0).then_inc(wsn_zero, 1)
            pool.wait_ge(ws_loaded, 16 * 9)
            pool.memset(wnat[0:64, :, 64:P], 0.0).then_inc(wnat_masked, 1)
            pool.wait_ge(bs_loaded, 16)
            pool.tensor_copy(bsb[:, :, P:2 * P].rearrange("p g (q s) -> p g q s", q=NS),
                             bsb[:, :, 0:SL].rearrange("p g (o s) -> p g o s", o=1)
                             .to_broadcast([P, 8, NS, SL])).then_inc(bsb_ready, 1)
            n0, _, _ = PLAN.at["v"]
            gain = V_MIX + KD
            scale_weights(n0 + 2, 0, 4, gain)
            scale_weights(n0 + 3, 0, 4, gain)
            with pool.Fori(1, 8) as i:
                for p in range(4):
                    scale_weights(n0 + p, i, 4, gain)
            n0, _, _ = PLAN.at["u0"]
            for p in range(4):
                scale_weights(n0 + p, 0, 4, gain)
            pool.wait_ge(gbc_loaded, 48)
            pool.wait_ge(ln_done, 1)
            nv = work[:, 8:24, SEQ:TOK]
            pool.tensor_tensor(gbc[:, :, :], gbc[:, :, :], nv, ALU.mult).then_inc(v_out_used, 1)
            pool.wait_ge(v_out_used, 1)
            for b in range(2):
                gb = gbc[:, 8 * b:8 * b + 8, :]
                ins = pool.tensor_tensor(gb, gb, bbc[b][:, :, :], ALU.add)
            ins.then_inc(vout_ready, 1)
            pool.wait_ge(acc_free, PLAN.at["mix"][1] + 48)
            for k in range(KD):
                pool.tensor_tensor(xs[:, k, :], xh[:, k, :].bitcast(F32), xl[:, k, :].bitcast(F32), ALU.add)\
                    .then_inc(xs_init, 1)
            n1, _, _ = PLAN.at["u"]
            with pool.Fori(0, 7) as i:
                for p in range(8):
                    scale_weights(n1 + p, i, 8, gain if p < 4 else None)
            n2, _, _ = PLAN.at["u9"]
            scale_weights(n2, 0, 4, None)
            scale_weights(n2 + 1, 0, 4, None)
            pool.wait_ge(u_gated, 48)
            pool.wait_ge(yl_ready, 2 * STEPS + CJ)
            linked(pool.memset(ssq_b[:, :], 0.0))
            finish_down(n2, 3, V_FFN + KD)
            ffn(1)


_INS = ["x_prompt", "x_sample", "state_hgrn", "state_pool", "state_ffn_conv", "norm_mix", "norm_ffn", "norm_final",
        "hgrn_lb_logits", "w_in_ab", "hgrn_out_gain", "pool_w", "pool_scale", "w_out_ab", "w_uv_c", "c_ln_gain",
        "c_ln_bias", "c_ws", "c_bs", "w_out_c", "w_in_ffn", "ffn_conv_w", "ffn_conv_b", "w_out_ffn"]
_OUTS = [("y_prompt", (1, SEQ, D)), ("y_sample", (NS, SL, D)), ("hgrn_prompt", (1, 1, HEADS, P, P)),
         ("hgrn_sample", (1, NS, HEADS, P, P)), ("pool_prompt", (1, 1, HIST, 512)),
         ("pool_sample", (1, NS, HIST, 512)), ("conv_prompt", (2, 1, 2, DFF)), ("conv_sample", (2, NS, 2, DFF)),
         ("cmlp_v", (1, NS, SL, CW))]


def kernel(**inputs):
    import numpy as np
    import concourse.bacc as bacc
    from concourse.bass_utils import run_bass_kernel_spmd

    nc = bacc.Bacc("TRN2", target_bir_lowering=False, num_devices=1, dynamic_dma_scratch_size=64)
    arrays, ins, outs = {}, {}, {}
    for name in _INS:
        a = np.ascontiguousarray(inputs[name])
        arrays[f"in_{name}"] = a
        ins[name] = nc.dram_tensor(f"in_{name}", a.shape, mybir.dt.from_np(a.dtype), kind="ExternalInput").ap()
    for name, shape in _OUTS:
        outs[name] = nc.dram_tensor(f"out_{name}", shape, F32, kind="ExternalOutput").ap()
    build(nc, ins, outs)
    r = run_bass_kernel_spmd(nc, [arrays], core_ids=[0])
    return tuple(r.results[0][f"out_{name}"] for name, _ in _OUTS)
```

```python
from contextlib import ExitStack

import concourse.bass as bass
from concourse import mybir
from concourse.alu_op_type import AluOpType as ALU

F32 = mybir.dt.float32
F32R = mybir.dt.float32r
U8 = mybir.dt.uint8
ACT = mybir.ActivationFunctionType
ds = bass.ds

P = 128
D = 1024
SEQ = 1024
NS, SL = 8, 16
TOK = SEQ + NS * SL
TB = 384
NTB = TOK // TB
NT = TOK // P
KD = D // P
HEADS = 4
POOLW = (2, 4, 8, 16)
HIST = 15
CW = 2048
CJ = CW // P
DFF = 2816
FJ = DFF // P
STEPS = FJ // 2
EPS = 1e-6
BANKS = 6
LN_ACT = 4
RAWS = 4

V_MIX, V_FFN, V_FIN, V_OUTG, V_PSC, V_LNG, V_LNB, NVEC = 0, 16, 32, 40, 41, 45, 61, 77


class Plan:

    def __init__(self):
        self.piece, self.group, self.tick, self.at = 0, 0, 0, {}

    def add(self, name, pieces, groups, ticks):
        self.at[name] = (self.piece, self.group, self.tick)
        self.piece += pieces
        self.group += groups
        self.tick += ticks


PLAN = Plan()
PLAN.add("xin", 0, 24, 24)
PLAN.add("ab", 40, 60, 80)
PLAN.add("abo", 16, 24, 32)
for _l in range(2):
    if _l == 1:
        PLAN.add("v", 32, 96, 112)
        PLAN.add("mix", 0, 48, 48)
        PLAN.add("u0", 4, 6, 8)
        PLAN.add("u", 7 * 8, 7 * 30, 7 * 32)
        PLAN.add("u9", 4, 24, 24)
    PLAN.add(f"f{_l}0", 8, 12, 16)
    PLAN.add(f"f{_l}", 10 * 12, 10 * 36, 10 * 40)
    PLAN.add(f"f{_l}9", 4, 24, 24)
PLAN.add("out", 0, 18, 18)
PIECES = PLAN.piece


def build(nc, A, O):
    ctx = ExitStack()
    with ctx:
        def sem(name):
            return ctx.enter_context(nc.semaphore(name))

        x_loaded = [sem(f"x_loaded{i}") for i in range(NTB)]
        rows_loaded = sem("rows_loaded")
        raw_loaded = [sem(f"raw_loaded{i}") for i in range(RAWS)]
        sin_loaded = sem("sin_loaded")
        hist_loaded = sem("hist_loaded")
        crow_loaded = sem("crow_loaded")
        ws_loaded = sem("ws_loaded")
        bs_loaded = sem("bs_loaded")
        gbc_loaded = sem("gbc_loaded")
        states_stored = sem("states_stored")
        stored = sem("stored")
        tails_stored = sem("tails_stored")
        vout_stored = sem("vout_stored")
        y_stored = [sem(f"y_stored{i}") for i in range(2)]
        w_scaled = sem("w_scaled")
        w_high_ready = sem("w_high_ready")
        w_low_ready = sem("w_low_ready")
        pe_tick = sem("pe_tick")
        acc_free = sem("acc_free")
        xs_init = sem("xs_init")
        xh_ready = sem("xh_ready")
        xl_ready = sem("xl_ready")
        square_ready = sem("square_ready")
        ssq_added = sem("ssq_added")
        norm_mm = sem("norm_mm")
        rms_ready = sem("rms_ready")
        rstd_ready = sem("rstd_ready")
        y_out = sem("y_out")
        y_normed = sem("y_normed")
        ident_ready = sem("ident_ready")
        eps_ready = sem("eps_ready")
        setup_done = sem("setup_done")
        setup_chain = sem("setup_chain")
        vec_mm = sem("vec_mm")
        vec_ready = sem("vec_ready")
        carried = sem("carried")
        q_act = sem("q_act")
        q_silu = sem("q_silu")
        g_act = sem("g_act")
        act_prep = sem("act_prep")
        logf_ready = sem("logf_ready")
        logf_used = sem("logf_used")
        k_ready = sem("k_ready")
        reset_ready = sem("reset_ready")
        decay_ready = sem("decay_ready")
        diff_ready = sem("diff_ready")
        exps_ready = sem("exps_ready")
        k_scaled = sem("k_scaled")
        q_scaled = sem("q_scaled")
        scores_mm = sem("scores_mm")
        scores_in = sem("scores_in")
        ic_ready = sem("ic_ready")
        v_mm = sem("v_mm")
        v_ready = sem("v_ready")
        kd_mm = sem("kd_mm")
        kdt_ready = sem("kdt_ready")
        o_mm = sem("o_mm")
        o_out = sem("o_out")
        sd_mm = sem("sd_mm")
        state_decayed = sem("state_decayed")
        state_ready = sem("state_ready")
        vm_ready = sem("vm_ready")
        sstate_decayed = sem("sstate_decayed")
        sstate_ready = sem("sstate_ready")
        osq_ready = sem("osq_ready")
        onorm_mm = sem("onorm_mm")
        onorm_out = sem("onorm_out")
        oinv = sem("oinv")
        o_normed = sem("o_normed")
        o_fin = sem("o_fin")
        hist_mm = sem("hist_mm")
        pad_ready = sem("pad_ready")
        cinv_ready = sem("cinv_ready")
        wide_step = sem("wide_step")
        pad_used = sem("pad_used")
        histt_ready = sem("histt_ready")
        prow_mm = sem("prow_mm")
        prow_ready = sem("prow_ready")
        window_step = sem("window_step")
        sums_ready = sem("sums_ready")
        edge_fixed = sem("edge_fixed")
        pooled_ready = sem("pooled_ready")
        pool_mm = sem("pool_mm")
        yb_ready = sem("yb_ready")
        mh_ready = sem("mh_ready")
        ml_ready = sem("ml_ready")
        convc_mm = sem("convc_mm")
        convc_ready = sem("convc_ready")
        conv_step = [sem(f"conv_step{i}") for i in range(2)]
        gelu_done = [sem(f"gelu_done{i}") for i in range(2)]
        y_formed = [sem(f"y_formed{i}") for i in range(2)]
        yh_ready = sem("yh_ready")
        yl_ready = sem("yl_ready")
        tails_mm = sem("tails_mm")
        trow_ready = sem("trow_ready")
        wsn_zero = sem("wsn_zero")
        wnat_masked = sem("wnat_masked")
        wt_mm = sem("wt_mm")
        wt_ready = sem("wt_ready")
        wsum_mm = sem("wsum_mm")
        wsum_ready = sem("wsum_ready")
        bsb_ready = sem("bsb_ready")
        v_activated = sem("v_activated")
        ln_stats = sem("ln_stats")
        ln_sqrt = sem("ln_sqrt")
        ln_act_done = sem("ln_act_done")
        ln_done = sem("ln_done")
        v_out_used = sem("v_out_used")
        vout_ready = sem("vout_ready")
        addend_ready = sem("addend_ready")
        u_activated = sem("u_activated")
        u_gated = sem("u_gated")

        SLOT = TOK * 4
        XH0 = 128
        XL0 = XH0 + KD * SLOT
        W0 = XL0 + KD * SLOT
        RAW0 = W0 + 24 * SLOT
        WH0 = RAW0 + RAWS * 2048
        WL0 = WH0 + 2 * 2048
        RS0 = WL0 + 2 * 2048
        ID0 = RS0 + SLOT
        ON0 = ID0 + 512
        CV0 = ON0 + 512
        E0 = CV0 + 352
        EEND = 229344
        ESIZE = EEND - E0
        used = {}

        def at(name, shape, dt, off):
            size = 1
            for s in shape[1:]:
                size *= s
            size *= 1 if dt == U8 else 4
            assert off + size <= EEND, (name, off + size, EEND)
            used[name] = (off, off + size)
            return nc.alloc_sbuf_tensor_at(name, shape, dt, offset=off)

        def slot(k):
            return W0 + k * SLOT

        xh = at("xh", [P, KD, TOK], F32R, XH0)
        xl = at("xl", [P, KD, TOK], F32R, XL0)
        work = at("work", [P, 24, TOK], F32, W0)
        xs = at("xs", [P, KD, TOK], F32, slot(0))
        raw = at("raw", [P, RAWS, 512], F32, RAW0)
        wh = at("wh", [P, 2, 512], F32R, WH0)
        wl = at("wl", [P, 2, 512], F32R, WL0)
        rstd = at("rstd", [P, TOK], F32, RS0)
        ident = at("ident", [P, P], F32, ID0)
        ones = at("ones", [P, P], F32, ON0)
        vec = at("vec", [P, NVEC + 3], F32, CV0)
        eps_c = vec[:, NVEC:NVEC + 1]
        ssq_e = at("ssq_e", [P, TOK], F32, E0)
        sq_e = at("sq_e", [P, 2, TB], F32, E0 + SLOT)
        xtok = at("xtok", [P, NT, D], F32, slot(8))
        vrow = at("vrow", [NVEC, P], F32, slot(16))
        o = E0
        ediff = at("ediff", [P, 2, HEADS, P], F32, o); o += 4096
        qsc = at("qsc", [P, 2, HEADS, 64], F32, o); o += 2048
        ksc = at("ksc", [P, 2, HEADS, P], F32, o); o += 4096
        sct = at("sct", [P, HEADS, P], F32, o); o += 2048
        vtok = at("vtok", [P, HEADS, P], F32, o); o += 2048
        icp = at("icp", [P, HEADS, P], F32, o); o += 2048
        kdt = at("kdt", [P, HEADS, P], F32, o); o += 2048
        stt = at("stt", [P, HEADS, P], F32, o); o += 2048
        masks = at("masks", [P, 7, 64], U8, o); o += 448
        ebl = at("ebl", [P, HEADS, NS], F32, o); o += 128
        smask = at("smask", [P, NS], F32, o); o += 32
        resetm = at("resetm", [P, TOK], F32, E0)
        maskf = at("maskf", [P, 7, 64], F32, E0 + 8192)
        sin_ = at("sin_", [P, HEADS, TOK], F32, slot(20))
        vms = at("vms", [P, HEADS, TOK], F32, slot(4))
        osq = [at(f"osq{h}", [P, TOK], F32, off) for h, off in enumerate((E0, E0 + SLOT, slot(6), slot(5)))]
        hstage = at("hstage", [NS * HIST, 512], F32, E0 + 6144)
        histt = at("histt", [P, HEADS, NS * HIST], F32, E0 + 16448)
        poolw = at("poolw", [P, HEADS, P], F32, E0 + 18432)
        cinv = at("cinv", [P, 16], F32, E0 + 20480)
        prow = [at("prow0", [P, 512], F32, slot(20) + 3 * 5184), at("prow1", [P, 512], F32, E0 + 14400)]
        PADW = HIST + SEQ + NS * (HIST + SL)
        pads = [at(f"pad{b}", [P, PADW], F32, slot(20) + b * 5184) for b in range(2)]
        sums = [at("sums0", [P, PADW], F32, slot(20) + 2 * 5184), at("sums1", [P, PADW], F32, E0 + 9216)]
        wide_pad = at("wide_pad", [P, PADW], F32, slot(8))
        wide_sums = [at(f"wide_sums{b}", [P, PADW], F32, slot(8) + (b + 1) * 5184) for b in range(2)]
        POOL_ORDER = (3, 0, 1, 2)
        MIXED_ORDER = (0, 1, 3, 2, 7, 4, 5, 6)
        SUMS_AT = ((0,), (1, 0), (1, 0, 1))
        mh = at("mh", [P, KD, TOK], F32R, slot(8))
        ml = at("ml", [P, KD, TOK], F32R, slot(16))
        APW = 2 + SEQ + NS * (2 + SL)
        o = slot(8)
        apad = at("apad", [P, 2, APW + 2], F32, o); o += 2 * (APW + 2) * 4
        cv = at("cv", [P, 2, TOK], F32, o); o += 2 * SLOT
        gate = at("gate", [P, 2, TOK], F32, o); o += 2 * SLOT
        assert o <= slot(16)
        ssq_b = at("ssq_b", [P, TOK], F32, slot(16))
        sq_b = at("sq_b", [P, 2, TB], F32, slot(17))
        yh2 = at("yh2", [P, 2, TOK], F32R, slot(18))
        yl2 = at("yl2", [P, 2, TOK], F32R, slot(20))
        o = slot(22)
        convc = at("convc", [P, 20 * FJ], F32, o); o += 1760
        tails = at("tails", [P, 18, FJ], F32, o); o += 1600
        trow = at("trow", [P, 4, P], F32, o); o += 2048
        assert o <= slot(24)
        crow = at("crow", [P, 4, P], F32, E0 + 12288)
        yh = at("yh", [P, 2, TOK], F32R, E0)
        yl = at("yl", [P, 2, TOK], F32R, E0 + 2 * SLOT)
        ut = at("ut", [P, 2, TB], F32, E0 + 4 * SLOT)
        yh3 = at("yh3", [P, 2, TOK], F32R, slot(8))
        yl3 = at("yl3", [P, 2, TOK], F32R, slot(10))
        o = slot(0)
        vtmp = at("vtmp", [P, 2, TOK], F32, o); o += 2 * SLOT
        wtp = at("wtp", [P, 8, P], F32, o); o += 4096
        wts = at("wts", [P, 8, P], F32, o); o += 4096
        wsum = at("wsum", [P, 8, 2 * P], F32, o); o += 8192
        bsb = at("bsb", [P, 8, 2 * P], F32, o); o += 8192
        assert o <= slot(8)
        o = E0
        wnat = at("wnat", [P, 8, P], F32, o)
        wsn = at("wsn", [P, 8, P], F32, o + 4096)
        stats = at("stats", [P, NT, CJ, 6], F32, o + 8192)
        mv = at("mv", [P, NT, 2], F32, o + 8192 + 3456)
        lrs = at("lrs", [P, NT], F32, o + 8192 + 3456 + 96)
        lnb = at("lnb", [P, NT], F32, o + 8192 + 3456 + 96 + 64)
        adde = at("adde", [P, 2, 2 * P], F32, o + 16384)
        gbc = at("gbc", [P, CJ, P], F32, o)
        bbc = [at(f"bbc{b}", [P, 8, P], F32, o + off) for b, off in ((0, 12288), (1, 18432))]
        otok = at("otok", [P, 2, D], F32, slot(8))

        ps = [ctx.enter_context(nc.psum_tensor(f"bank{b}", [P, 512], F32)) for b in range(8)]
        block = ctx.enter_context(nc.Block())

        def tbs(tb):
            return slice(tb * TB, (tb + 1) * TB)

        wab = A["w_in_ab"][0].rearrange("(h k p) c -> p h k c", h=2, p=P)
        wabo = A["w_out_ab"][0].rearrange("(h k p) c -> p h k c", h=2, p=P)
        wuv = A["w_uv_c"][0].rearrange("(h k p) c -> p h k c", h=2, p=P)
        woc = A["w_out_c"][0].rearrange("(k p) c -> p k c", p=P)
        wfi = [A["w_in_ffn"][l].rearrange("(h k p) c -> p h k c", h=2, p=P) for l in range(2)]
        wfo = [A["w_out_ffn"][l].rearrange("(k p) c -> p k c", p=P) for l in range(2)]

        def loop(eng, n, body):
            with eng.Fori(0, n) as i:
                body(i)

        @block.sync
        def _(sp):
            def load_piece(n, src, s):
                if s is None or s >= RAWS:
                    sp.wait_ge(w_low_ready, n - (RAWS - 1))
                sp.dma_start(raw[:, s % RAWS, :].rearrange("p (k c) -> p k c", k=src.shape[1]), src)\
                    .then_inc(raw_loaded[s % RAWS], 16)

            def up(w, n, s, col):
                for h in range(2):
                    load_piece(n + h, w[:, h, :, ds(col, P)], s + h)

            def down(w, n, s, k0):
                for q in range(4):
                    load_piece(n + q, w[:, ds(k0, 2), q * 256:(q + 1) * 256], s + q)

            xp = A["x_prompt"].rearrange("b (t p) d -> p (b t) d", p=P)
            xsm = A["x_sample"].rearrange("b t d -> (b t) d")
            for t in range(NT):
                sp.dma_start(xtok[:, t, :], xp[:, t, :] if t < NT - 1 else xsm).then_inc(x_loaded[t // 3], 16)
            rows = [(V_MIX, A["norm_mix"].rearrange("l (k p) -> (l k) p", p=P)),
                    (V_FFN, A["norm_ffn"].rearrange("l (k p) -> (l k) p", p=P)),
                    (V_FIN, A["norm_final"].rearrange("(k p) -> k p", p=P)),
                    (V_OUTG, A["hgrn_out_gain"]),
                    (V_PSC, A["pool_scale"].rearrange("l (k p) -> (l k) p", p=P)),
                    (V_LNG, A["c_ln_gain"].rearrange("l (k p) -> (l k) p", p=P)),
                    (V_LNB, A["c_ln_bias"].rearrange("l (k p) -> (l k) p", p=P))]
            for r0, src in rows:
                sp.dma_start(vrow[r0:r0 + src.shape[0], :], src).then_inc(rows_loaded, 16)

            n0, _, _ = PLAN.at["ab"]

            def ab(i):
                for u in range(2):
                    up(wab, n0 + 4 * i + 2 * u, n0 + 2 * u, (2 * i + u) * P)
            ab(0)
            with sp.Fori(1, 10) as i:
                for u in range(2):
                    for h in range(2):
                        s = n0 + 2 * u + h
                        load_piece(4 * i + s, wab[:, h, :, ds((2 * i + u) * P, P)], s + RAWS)

            n0, _, _ = PLAN.at["abo"]
            for u in range(2):
                up(wabo, n0 + 2 * u, n0 + 2 * u, u * P)

            sp.wait_ge(state_ready, NT)
            for h in range(HEADS):
                sp.dma_start(sin_[:, h, 0:SEQ].rearrange("p (q v) -> p q v", q=NS),
                             A["state_hgrn"][0, :, h].rearrange("q k v -> k q v")).then_inc(sin_loaded, 16)
            sp.dma_start(O["hgrn_prompt"][0, 0].rearrange("h k v -> k h v"), stt[:, :, :])\
                .then_inc(states_stored, 16)
            sp.wait_ge(states_stored, 16)
            sp.wait_ge(o_mm, NT)
            sp.dma_start(hstage[:, :], A["state_pool"][0].rearrange("q t c -> (q t) c")).then_inc(hist_loaded, 16)
            sp.dma_start(poolw[:, :, :], A["pool_w"][0].rearrange("g c e -> c g e")).then_inc(hist_loaded, 16)
            sp.wait_ge(sstate_ready, HEADS)
            for h in range(HEADS):
                sp.dma_start(O["hgrn_sample"][0, :, h].rearrange("q k v -> k q v"),
                             sin_[:, h, 0:SEQ].rearrange("p (q v) -> p q v", q=NS)).then_inc(states_stored, 16)
            sp.wait_ge(prow_ready, 2)
            sp.dma_start(O["pool_prompt"][0, 0], prow[0][P - HIST:P, :]).then_inc(stored, 16)
            for q in range(NS):
                sp.dma_start(O["pool_sample"][0, q], prow[1][SL * q + 1:SL * (q + 1), :]).then_inc(stored, 16)

            n0, _, _ = PLAN.at["abo"]
            with sp.Fori(1, 4) as i:
                for u in range(2):
                    up(wabo, n0 + 4 * i + 2 * u, n0 + 2 * u, (2 * i + u) * P)

            def ffn(l):
                n0, _, _ = PLAN.at[f"f{l}0"]
                cols = (0, P, DFF, DFF + P)
                sp.wait_ge(acc_free, PLAN.at[f"f{l}0"][1] - 24)
                hist = A["state_ffn_conv"][l].rearrange("q j (f p) -> (q j f) p", p=P)
                taps = A["ffn_conv_w"][l].rearrange("j (f p) -> (j f) p", p=P)
                bias = A["ffn_conv_b"][l].rearrange("(f p) -> f p", p=P)
                for b, src in enumerate((hist[0:128], hist[128:256])):
                    sp.dma_start(crow[:, b, :], src).then_inc(crow_loaded, 16)
                sp.dma_start(crow[0:96, 2, :], hist[256:352]).then_inc(crow_loaded, 16)
                sp.dma_start(crow[96:128, 2, :], taps[0:32]).then_inc(crow_loaded, 16)
                sp.dma_start(crow[0:34, 3, :], taps[32:66]).then_inc(crow_loaded, 16)
                sp.dma_start(crow[34:56, 3, :], bias).then_inc(crow_loaded, 16)
                for u in range(2):
                    up(wfi[l], n0 + 2 * u, n0 + 2 * u, cols[u])
                for u in range(2, 4):
                    up(wfi[l], n0 + 2 * u, n0 + 2 * u, cols[u])
                n0, _, _ = PLAN.at[f"f{l}"]
                with sp.Fori(0, STEPS - 1) as i:
                    for u, col in enumerate(cols):
                        up(wfi[l], n0 + 12 * i + 2 * u, n0 + 2 * u, (i + 1) * 2 * P + col)
                    down(wfo[l], n0 + 12 * i + 8, n0 + 8, 2 * i)
                n0, _, _ = PLAN.at[f"f{l}9"]
                down(wfo[l], n0, n0, FJ - 2)

            def store_tails(l):
                sp.wait_ge(trow_ready, 4 * (l + 1))
                outp = O["conv_prompt"][l, 0].rearrange("j (f p) -> (j f) p", p=P)
                outs = O["conv_sample"][l].rearrange("q j (f p) -> (q j f) p", p=P)
                sp.dma_start(outp, trow[0:44, 0, :]).then_inc(tails_stored, 16)
                sp.dma_start(outs[0:128], trow[:, 1, :]).then_inc(tails_stored, 16)
                sp.dma_start(outs[128:256], trow[:, 2, :]).then_inc(tails_stored, 16)
                sp.dma_start(outs[256:352], trow[0:96, 3, :]).then_inc(tails_stored, 16)

            ffn(0)
            n0, _, _ = PLAN.at["v"]
            up(wuv, n0, n0, CW)
            up(wuv, n0 + 2, n0 + 2, CW + P)
            sp.wait_ge(acc_free, PLAN.at["v"][1])
            sp.wait_ge(wsn_zero, 1)
            sp.dma_start(wnat[:, :, :], A["c_ws"][0].rearrange("g t s -> t g s")).then_inc(ws_loaded, 16)
            for q in range(NS):
                sp.dma_start(wsn[SL * q:SL * (q + 1), :, SL * q:SL * (q + 1)],
                             A["c_ws"][0, :, 0:SL, 0:SL].rearrange("g t s -> t g s")).then_inc(ws_loaded, 16)
            sp.dma_start(bsb[:, :, 0:P], A["c_bs"][0:1].to_broadcast([P, 8, P])).then_inc(bs_loaded, 16)
            up(wuv, n0 + 4, n0 + 4, CW + 2 * P)
            with sp.Fori(1, 4) as i:
                for u in range(2):
                    up(wuv, n0 + 2 + 4 * i + 2 * u, n0 + 2 + 2 * u, CW + (2 * i + 1 + u) * P)
            store_tails(0)
            sp.wait_ge(wt_ready, 4)
            sp.dma_start(gbc[:, :, :], A["c_ln_gain"].rearrange("o (j c) -> o j c", c=P).to_broadcast([P, CJ, P]))\
                .then_inc(gbc_loaded, 16)
            for b in range(2):
                sp.dma_start(bbc[b][:, :, :], A["c_ln_bias"].rearrange("o (j c) -> o j c", c=P)[:, 8 * b:8 * b + 8]
                             .to_broadcast([P, 8, P])).then_inc(gbc_loaded, 16)
            with sp.Fori(4, 7) as i:
                for u in range(2):
                    up(wuv, n0 + 2 + 4 * i + 2 * u, n0 + 2 + 2 * u, CW + (2 * i + 1 + u) * P)
            up(wuv, n0 + 30, n0 + 30, CW + 15 * P)
            n0, _, _ = PLAN.at["u0"]
            for u in range(2):
                up(wuv, n0 + 2 * u, n0 + 2 * u, u * P)
            sp.wait_ge(vout_ready, 1)
            sp.dma_start(O["cmlp_v"][0].rearrange("q t (j c) -> (q t) j c", c=P), gbc[:, :, :])\
                .then_inc(vout_stored, 16)
            n0, _, _ = PLAN.at["u"]
            with sp.Fori(0, 7) as i:
                for u in range(2):
                    up(wuv, n0 + 8 * i + 2 * u, n0 + 2 * u, (2 * i + 2 + u) * P)
                down(woc, n0 + 8 * i + 4, n0 + 4, 2 * i)
            n0, _, _ = PLAN.at["u9"]
            down(woc, n0, n0, CJ - 2)
            ffn(1)
            store_tails(1)
            yp = O["y_prompt"].rearrange("b (t p) d -> p (b t) d", p=P)
            ysm = O["y_sample"].rearrange("b t d -> (b t) d")
            for t in range(NT):
                sp.wait_ge(y_out, 2 * (t + 1))
                sp.dma_start(yp[:, t, :] if t < NT - 1 else ysm, otok[:, t % 2, :])\
                    .then_inc(y_stored[t % 2], 16)
            for par in range(2):
                sp.wait_ge(y_stored[par], 16 * ((NT + 1 - par) // 2))
            sp.wait_ge(stored, 16 * (1 + NS))
            sp.wait_ge(states_stored, 16 * (1 + HEADS))
            sp.wait_ge(tails_stored, 16 * 8)
            sp.wait_ge(vout_stored, 16)


        def some(count):
            return not isinstance(count, int) or count > 0

        LV = 7
        HALF = {True: (64, 32, 16, 8, 4, 2, 1), False: (8, 4, 2, 1)}
        MOFF = {64: 0, 32: 1, 16: 2, 8: 3, 4: 4, 2: 5, 1: 6}

        def tile_cols(t):
            return ds(t * P, P)

        def blocks(ap, b):
            return ap.rearrange("p h (n b) -> p h n b", b=b)

        @block.tensor
        def _(pe):
            def acc_bank(g, s):
                if s is None or s >= BANKS:
                    pe.wait_ge(acc_free, g - (BANKS - 1))
                return ps[s % BANKS]

            def unit(rh, rl, n, g, sn, sg, mixed=False):
                for h in range(2):
                    if mixed:
                        pe.wait_ge(mh_ready, 4 * (h + 1))
                        pe.wait_ge(ml_ready, 4 * (h + 1))
                    pe.wait_ge(w_high_ready, n + h + 1)
                    pe.wait_ge(w_low_ready, n + h + 1)
                    place = (sn + h) % 2
                    for k in range(4):
                        kk = 4 * h + k
                        parts = ((wh, rh), (wh, rl), (wl, rh))
                        for c, (w, r) in enumerate(parts):
                            for tb in range(NTB):
                                if kk == 0 and c == 0:
                                    acc_bank(g + tb, sg + tb)
                                mm = pe.matmul(ps[(sg + tb) % BANKS][:, 0:TB], w[:, place, k * P:(k + 1) * P],
                                               r[:, kk, tbs(tb)], start=kk == 0 and c == 0,
                                               stop=kk == KD - 1 and c == 2)
                                if kk == KD - 1 and c == 2:
                                    mm.then_inc(pe_tick, 1)
                    if h == 0:
                        mm.then_inc(pe_tick, 1)

            def down(n, g, sn, sg, steps_done, yh=yh, yl=yl):
                pe.wait_ge(yh_ready, steps_done)
                pe.wait_ge(yl_ready, steps_done)
                for q in range(4):
                    pe.wait_ge(w_high_ready, n + q + 1)
                    pe.wait_ge(w_low_ready, n + q + 1)
                    place = (sn + q) % 2
                    for dd in range(2):
                        g0 = 3 * (2 * q + dd)
                        for k in range(2):
                            for c, (w, r) in enumerate(((wh, yh), (wh, yl), (wl, yh))):
                                for tb in range(NTB):
                                    if k == 0 and c == 0:
                                        acc_bank(g + g0 + tb, sg + g0 + tb)
                                    mm = pe.matmul(ps[(sg + g0 + tb) % BANKS][:, 0:TB],
                                                   w[:, place, k * 256 + dd * P:k * 256 + (dd + 1) * P],
                                                   r[:, k, tbs(tb)], start=k == 0 and c == 0,
                                                   stop=k == 1 and c == 2)
                                    if k == 1 and c == 2:
                                        mm.then_inc(pe_tick, 1)

            def norm(k, ssq):
                pe.wait_ge(ssq_added, 24 * (k + 1))
                for tb in range(NTB):
                    if some(NTB * k + tb - 1):
                        pe.wait_ge(rms_ready, NTB * k + tb - 1)
                    pe.matmul(ps[6 + (NTB * k + tb) % 2][:, 0:TB], ones[:, :], ssq[:, tbs(tb)], start=True, stop=True)\
                        .then_inc(norm_mm, 1)

            def first_unit(k, n, g):
                pe.wait_ge(xh_ready, 24 * (k + 1))
                pe.wait_ge(xl_ready, 24 * (k + 1))
                unit(xh, xl, n, g, n, g)

            pe.wait_ge(ident_ready, 1)
            pe.wait_ge(rows_loaded, 16 * 7)
            pe.transpose(ps[6][:, 0:NVEC], vrow[:, :], ident[0:NVEC, 0:NVEC]).then_inc(vec_mm, 1)
            for g in range(24):
                tb, d = divmod(g, KD)
                if d == 0:
                    pe.wait_ge(x_loaded[tb], 48)
                bank = acc_bank(g, g)
                for j in range(3):
                    mm = pe.transpose(bank[:, j * P:(j + 1) * P], xtok[:, 3 * tb + j, d * P:(d + 1) * P], ident[:, :])
                mm.then_inc(pe_tick, 1)
            pe.wait_ge(vec_ready, 1)

            n0, g0, _ = PLAN.at["ab"]
            first_unit(0, n0, g0)
            norm(0, ssq_e)
            unit(xh, xl, n0 + 2, g0 + 3, n0 + 2, g0 + 3)

            def ab(i):
                for u in range(2):
                    unit(xh, xl, n0 + 4 * i + 2 * u, g0 + 6 * i + 3 * u, n0 + 2 * u, g0 + 3 * u)
            with pe.Fori(1, 10) as i:
                ab(i)

            pe.wait_ge(acc_free, 84)

            def tile(t, prompt):
                L = len(HALF[prompt])
                pe.wait_ge(ic_ready, t + 1)
                if some(t):
                    pe.wait_ge(v_ready, t)
                for h in range(HEADS):
                    mm = pe.transpose(ps[0][:, h * P:(h + 1) * P], icp[:, h, :], ident[:, :])
                mm.then_inc(v_mm, 1)
                pe.wait_ge(k_scaled, t * (LV + 2) + 1)
                pe.wait_ge(q_silu, 2)
                if some(t * (LV + 1) - LV):
                    pe.wait_ge(scores_in, t * (LV + 1) - LV)
                for h in range(HEADS):
                    mm = pe.matmul(ps[1][:, h * P:(h + 1) * P], ksc[:, 0, h, :], work[:, h, tile_cols(t)],
                                   start=True, stop=True)
                mm.then_inc(scores_mm, 1)
                for q in range(1, L + 1):
                    pe.wait_ge(q_scaled, t * (LV + 1) + q)
                    pe.wait_ge(k_scaled, t * (LV + 2) + q + 1)
                    if some(t * (LV + 1) + (q - 1 if q > 2 else 0)):
                        pe.wait_ge(scores_in, t * (LV + 1) + (q - 1 if q > 2 else 0))
                    for h in range(HEADS):
                        mm = pe.matmul(ps[6 + q % 2][:, h * 64:(h + 1) * 64], ksc[:, q % 2, h, :], qsc[:, q % 2, h, :],
                                       start=True, stop=True)
                    mm.then_inc(scores_mm, 1)
                pe.wait_ge(k_scaled, t * (LV + 2) + L + 2)
                if some(t):
                    pe.wait_ge(kdt_ready, t)
                for h in range(HEADS):
                    mm = pe.transpose(ps[2][:, h * P:(h + 1) * P], ediff[:, 1, h, :], ident[:, :])
                mm.then_inc(kd_mm, 1)
                pe.wait_ge(scores_in, t * (LV + 1) + L + 1)
                pe.wait_ge(v_ready, t + 1)
                pe.wait_ge(q_scaled, t * (LV + 1) + L + 1)
                pe.wait_ge(state_ready, t + 1)
                if some(t):
                    pe.wait_ge(o_out, t)
                if not prompt:
                    pe.wait_ge(sin_loaded, 16 * HEADS)
                for h in range(HEADS):
                    if prompt:
                        pe.matmul(ps[3][:, h * P:(h + 1) * P], vtok[:, h, :], sct[:, h, :], start=True, stop=False)
                        mm = pe.matmul(ps[3][:, h * P:(h + 1) * P], stt[:, h, :], ediff[:, 0, h, :],
                                       start=False, stop=True)
                    else:
                        for q in range(NS):
                            own = slice(q * SL, (q + 1) * SL)
                            out = ps[3][:, h * P + q * SL:h * P + (q + 1) * SL]
                            pe.matmul(out, vtok[:, h, :], sct[:, h, own], start=True, stop=False)
                            mm = pe.matmul(out, sin_[:, h, q * P:(q + 1) * P], ediff[:, 0, h, own],
                                           start=False, stop=True)
                mm.then_inc(o_mm, 1)
                pe.wait_ge(kdt_ready, t + 1)
                if prompt:
                    for h in range(HEADS):
                        mm = pe.matmul(ps[4][:, h * P:(h + 1) * P], kdt[:, h, :], vtok[:, h, :], start=True, stop=True)
                    mm.then_inc(sd_mm, 1)
                else:
                    for h in range(HEADS):
                        pe.wait_ge(vm_ready, h + 1)
                        if some(h):
                            pe.wait_ge(sstate_ready, h)
                        for c in range(2):
                            mm = pe.matmul(ps[4 + c][:, :], kdt[:, h, :], vms[:, h, c * 512:(c + 1) * 512],
                                           start=True, stop=True)
                        mm.then_inc(sd_mm, 1)

            tile(0, True)
            with pe.Fori(1, NT - 1) as t:
                tile(t, True)
            tile(NT - 1, False)

            pe.wait_ge(hist_loaded, 32)
            for h in range(HEADS):
                mm = pe.transpose(ps[0][:, h * 120:(h + 1) * 120], hstage[:, h * P:(h + 1) * P], ident[0:120, 0:120])
            mm.then_inc(hist_mm, 1)
            for r in range(2):
                for h in range(HEADS):
                    mm = pe.transpose(ps[1 + r][:, h * P:(h + 1) * P],
                                      work[:, 16 + h, (NT - 2 + r) * P:(NT - 1 + r) * P], ident[:, :])
                mm.then_inc(prow_mm, 1)
            def head_sums(h):
                pe.wait_ge(osq_ready, h + 1)
                if h == 1:
                    pe.wait_ge(histt_ready, 1)
                    pe.wait_ge(prow_ready, 2)
                if h >= 2:
                    pe.wait_ge(onorm_out, NTB * (h - 1))
                for tb in range(NTB):
                    mm = pe.matmul(ps[tb if h % 2 else 5 + tb][:, 0:TB], ones[:, :], osq[h][:, tbs(tb)],
                                   start=True, stop=True)
                mm.then_inc(onorm_mm, 1)

            def pooled_product(n):
                gi = POOL_ORDER[n]
                pe.wait_ge(pooled_ready, n + 1)
                for tb in range(NTB):
                    k = NTB * n + tb
                    if k >= 2:
                        pe.wait_ge(yb_ready, k - 1)
                    else:
                        pe.wait_ge(o_out, NT)
                    pe.matmul(ps[3 + k % 2][:, 0:TB], poolw[:, gi, :], work[:, 16 + gi, tbs(tb)], start=True, stop=True)\
                        .then_inc(pool_mm, 1)
            pe.wait_ge(sstate_ready, HEADS)
            head_sums(0)
            head_sums(1)
            pooled_product(0)
            pooled_product(1)
            head_sums(2)
            head_sums(3)
            pooled_product(2)
            pooled_product(3)

            n0, g0, _ = PLAN.at["abo"]

            def abo(i):
                for u in range(2):
                    unit(mh, ml, n0 + 4 * i + 2 * u, g0 + 6 * i + 3 * u, n0 + 2 * u, g0 + 3 * u)
            unit(mh, ml, n0, g0, n0, g0, mixed=True)
            unit(mh, ml, n0 + 2, g0 + 3, n0 + 2, g0 + 3)
            with pe.Fori(1, 4) as i:
                abo(i)

            def ffn(l):
                n0, g0, _ = PLAN.at[f"f{l}0"]
                first_unit(1 + 2 * l, n0, g0)
                norm(1 + 2 * l, ssq_b if l else ssq_e)
                pe.wait_ge(crow_loaded, 96 * (l + 1))
                pe.wait_ge(rms_ready, NTB * (2 + 2 * l))
                for b in range(4):
                    r = P if b < 3 else 56
                    mm = pe.transpose(ps[7][:, b * P:b * P + r], crow[0:r, b, :], ident[0:r, 0:r])
                mm.then_inc(convc_mm, 1)
                for u in range(1, 4):
                    unit(xh, xl, n0 + 2 * u, g0 + 3 * u, n0 + 2 * u, g0 + 3 * u)
                n1, g1, _ = PLAN.at[f"f{l}"]
                done0 = 2 * (STEPS * l + (8 if l else 0))

                def step(i):
                    for u in range(4):
                        unit(xh, xl, n1 + 12 * i + 2 * u, g1 + 36 * i + 3 * u, n1 + 2 * u, g1 + 3 * u)
                    down(n1 + 12 * i + 8, g1 + 36 * i + 12, n1 + 8, g1 + 12, 2 * i + (done0 + 2))
                loop(pe, STEPS - 1, step)
                n2, g2, _ = PLAN.at[f"f{l}9"]
                down(n2, g2, n2, g2, done0 + 2 * STEPS, yh2, yl2)

            def turn_tails(l):
                pe.wait_ge(conv_step[l], 9 * FJ)
                pe.wait_ge(rms_ready, NTB * (3 + 2 * l))
                for b, (c0, c1) in enumerate(((0, 44), (44, 172), (172, 300), (300, 396))):
                    flat = tails[:, :, :].rearrange("p r f -> p (r f)")
                    mm = pe.transpose(ps[7][0:c1 - c0, b * P:(b + 1) * P], flat[:, c0:c1], ident[:, :])
                mm.then_inc(tails_mm, 1)

            ffn(0)

            n0, g0, _ = PLAN.at["v"]

            def turn(j, par, g, sg):
                pe.wait_ge(v_activated, j + 1)
                for tb in range(NTB):
                    bank = acc_bank(g + tb, sg + tb)
                    for k in range(3):
                        c = tb * TB + k * P
                        mm = pe.transpose(bank[:, k * P:(k + 1) * P], vtmp[:, par, c:c + P], ident[:, :])
                    mm.then_inc(pe_tick, 1)
            first_unit(2, n0, g0)
            norm(2, ssq_b)
            turn_tails(0)

            def mixing_matrix(m):
                if m == 0:
                    pe.wait_ge(trow_ready, 4)
                    pe.wait_ge(wnat_masked, 1)
                    pe.wait_ge(ws_loaded, 16 * 9)
                else:
                    pe.wait_ge(wt_ready, 2)
                for b in range(2):
                    for j in range(4):
                        mm = pe.transpose(ps[6 + b][:, j * P:(j + 1) * P], (wnat, wsn)[m][:, 4 * b + j, :],
                                          ident[:, :])
                    mm.then_inc(wt_mm, 1)

            def mixing_sums(m):
                pe.wait_ge(wt_ready, 4)
                if m == 1:
                    pe.wait_ge(wsum_ready, 2)
                for b in range(2):
                    pe.matmul(ps[6 + b][:, :], ones[:, :], (wtp, wts)[m][:, 4 * b:4 * b + 4, :],
                              start=True, stop=True).then_inc(wsum_mm, 1)

            def vstep(i, between=None):
                for u in range(2):
                    unit(xh, xl, n0 + 2 + 4 * i + 2 * u, g0 + 3 + 12 * i + 6 * u, n0 + 2 + 2 * u, g0 + 3 + 6 * u)
                    if between:
                        between(u)
                    turn(2 * i + u, u, g0 + 6 + 12 * i + 6 * u, g0 + 6 + 6 * u)
            vstep(0)
            vstep(1, mixing_matrix)
            vstep(2, mixing_sums)
            with pe.Fori(3, 7) as i:
                vstep(i)
            unit(xh, xl, n0 + 30, g0 + 87, n0 + 30, g0 + 87)
            turn(14, 0, g0 + 90, g0 + 90)
            turn(15, 1, g0 + 93, g0 + 93)
            _, g0, _ = PLAN.at["mix"]
            pe.wait_ge(ln_done, NT - LN_ACT)
            pe.wait_ge(ln_act_done, LN_ACT)
            for j in range(CJ):
                for tb in range(NTB):
                    g = g0 + 3 * j + tb
                    bank = acc_bank(g, g)
                    for k in range(3):
                        t = 3 * tb + k
                        w = wtp if t < NT - 1 else wts
                        mm = pe.matmul(bank[:, k * P:(k + 1) * P], work[:, 8 + j, t * P:(t + 1) * P], w[:, j // 2, :],
                                       start=True, stop=True)
                    mm.then_inc(pe_tick, 1)
            n0, g0, _ = PLAN.at["u0"]
            for u in range(2):
                unit(xh, xl, n0 + 2 * u, g0 + 3 * u, n0 + 2 * u, g0 + 3 * u)
            n1, g1, _ = PLAN.at["u"]
            done0 = 2 * STEPS

            def ustep(i):
                for u in range(2):
                    unit(xh, xl, n1 + 8 * i + 2 * u, g1 + 30 * i + 3 * u, n1 + 2 * u, g1 + 3 * u)
                down(n1 + 8 * i + 4, g1 + 30 * i + 6, n1 + 4, g1 + 6, 2 * i + (done0 + 2))
            loop(pe, 7, ustep)
            n2, g2, _ = PLAN.at["u9"]
            down(n2, g2, n2, g2, done0 + CJ, yh3, yl3)
            ffn(1)
            norm(4, ssq_b)
            turn_tails(1)
            _, g0, _ = PLAN.at["out"]
            for t in range(NT):
                pe.wait_ge(y_normed, KD * (t // NTB + 1))
                for b in range(2):
                    m = 2 * t + b
                    if m < BANKS:
                        bank = acc_bank(g0 + m, g0 + m)
                    else:
                        pe.wait_ge(y_out, m - (BANKS - 1))
                        bank = ps[(g0 + m) % BANKS]
                    for k in range(4):
                        mm = pe.transpose(bank[:, k * P:(k + 1) * P], xs[:, 4 * b + k, t * P:(t + 1) * P], ident[:, :])
                    mm.then_inc(pe_tick, 1)

        @block.vector
        def _(dve):
            def low(n, s):
                dve.wait_ge(w_high_ready, n + 1)
                dve.tensor_tensor(wl[:, s % 2, :], raw[:, s % RAWS, :], wh[:, s % 2, :].bitcast(F32), ALU.subtract)\
                    .then_inc(w_low_ready, 1)

            def scaled(dst, bank, tb, tick):
                dve.wait_ge(pe_tick, tick)
                dve.tensor_tensor(dst, ps[bank % BANKS][:, 0:TB], rstd[:, tbs(tb)], ALU.mult)\
                    .then_inc(acc_free, 1)

            def add_down(d, tb, g, sg, tick):
                dve.wait_ge(pe_tick, tick)
                dve.wait_ge(acc_free, g - 12)
                dve.tensor_tensor(xs[:, d, tbs(tb)], ps[sg % BANKS][:, 0:TB], xs[:, d, tbs(tb)], ALU.add)\
                    .then_inc(acc_free, 1)

            def x_low(e, d, tb):
                dve.wait_ge(xh_ready, e + 1)
                dve.tensor_tensor(xl[:, d, tbs(tb)], xs[:, d, tbs(tb)], xh[:, d, tbs(tb)].bitcast(F32), ALU.subtract)\
                    .then_inc(xl_ready, 1)

            def inv_rms(k):
                for tb in range(NTB):
                    dve.wait_ge(rms_ready, NTB * k + tb + 1)
                    dve.reciprocal(rstd[:, tbs(tb)], rstd[:, tbs(tb)]).then_inc(rstd_ready, 1)
                dve.wait_ge(rstd_ready, NTB * (k + 1))

            prev = None
            for g in range(24):
                tb, d = divmod(g, KD)
                dve.wait_ge(pe_tick, g + 1)
                dve.tensor_copy(xs[:, d, tbs(tb)], ps[g % BANKS][:, 0:TB]).then_inc(acc_free, 1)
                if prev is not None:
                    x_low(*prev)
                prev = (g, d, tb)
            x_low(*prev)
            low(0, 0)
            low(1, 1)
            low(2, 2)
            low(3, 3)
            inv_rms(0)

            n0, g0, t0 = PLAN.at["ab"]

            def q_scale(c):
                q = work[:, 2 * c:2 * c + 2, :]
                dve.wait_ge(q_act, c + 1)
                dve.tensor_scalar(q, q, float(P) ** -0.5, None, ALU.mult).then_inc(q_silu, 1)

            def logf(c):
                z, f = work[:, 4 + 2 * c:6 + 2 * c, :], work[:, 20 + 2 * c:22 + 2 * c, :]
                dve.wait_ge(act_prep, 5 + c)
                dve.scalar_tensor_tensor(f, z, 0.0, f, ALU.min, ALU.subtract).then_inc(logf_ready, 1)

            def decay(c):
                dve.wait_ge(logf_used, c + 1)
                dve.wait_ge(reset_ready, 3)
                for h in (2 * c, 2 * c + 1):
                    dve.tensor_tensor_scan(work[:, 20 + h, :], resetm[:, :], work[:, 20 + h, :], 0.0,
                                           ALU.mult, ALU.add).then_inc(decay_ready, 1)

            def ab(i, gates=None):
                for u in range(2):
                    first = isinstance(i, int) and i == 0
                    if not first:
                        low(n0 + 4 * i + 2 * u + 1, n0 + 2 * u + 1)
                    if not first or u == 1:
                        low(n0 + 4 * i + 2 * u + 2, n0 + 2 * u + 2)
                    for tb in range(NTB):
                        scaled(work[:, 2 * i + u, tbs(tb)], g0 + 3 * u + tb, tb, t0 + 8 * i + 4 * u + 2 + tb)
                    if gates:
                        gates(u)
            ab(0)
            with dve.Fori(1, 6) as i:
                ab(i)
            ab(6, q_scale)
            ab(7, logf)
            ab(8)
            ab(9, decay)

            dve.memset(stt[:, :, :], 0.0).then_inc(state_ready, 1)
            dve.wait_ge(decay_ready, HEADS)
            dve.wait_ge(q_silu, 2)
            dve.wait_ge(setup_done, 1)

            def tile(t, prompt):
                halves = HALF[prompt]
                L = len(halves)
                bt = work[:, 20:24, tile_cols(t)]
                qt = work[:, 0:4, tile_cols(t)]

                def diff(q):
                    b = halves[q - 1]
                    if q == 1:
                        if some(t):
                            dve.wait_ge(kd_mm, t)
                        if some(t * (LV + 2)):
                            dve.wait_ge(k_scaled, t * (LV + 2))
                    elif q == 2:
                        if some(t):
                            dve.wait_ge(o_mm, t)
                    else:
                        dve.wait_ge(k_scaled, t * (LV + 2) + q - 1)
                        dve.wait_ge(q_scaled, t * (LV + 1) + q - 2)
                    bv, ev = blocks(bt, 2 * b), blocks(ediff[:, q % 2], 2 * b)
                    mid = bv[:, :, :, b - 1:b].to_broadcast([P, HEADS, P // (2 * b), b])
                    dve.tensor_tensor(ev[:, :, :, b:], bv[:, :, :, b:], mid, ALU.subtract)
                    dve.tensor_tensor(ev[:, :, :, 0:b], mid, bv[:, :, :, 0:b], ALU.subtract)\
                        .then_inc(diff_ready, 1)

                def take(q):
                    b = halves[q - 1]
                    dve.wait_ge(scores_mm, t * (LV + 1) + q + 1)
                    dve.wait_ge(scores_in, t * (LV + 1) + q)
                    if not isinstance(t, int):
                        dve.sem_inc(carried, 1)
                    m = masks[:, MOFF[b]:MOFF[b] + 1, :].rearrange("p o (n b) -> p o n b", b=b)
                    dve.copy_predicated(blocks(sct[:, :, :], 2 * b)[:, :, :, b:],
                                        m.to_broadcast([P, HEADS, 64 // b, b]),
                                        blocks(ps[6 + q % 2][:, 0:256].rearrange("p (h c) -> p h c", h=HEADS), b))\
                        .then_inc(scores_in, 1)

                diff(1)
                diff(2)
                if not (isinstance(t, int) and t == 0):
                    dve.wait_ge(exps_ready, t * (LV + 3))
                    dve.wait_ge(state_ready, t)
                    dve.tensor_tensor(stt[:, :, :], stt[:, :, :], ebl[:, :, 0:1].to_broadcast([P, HEADS, P]), ALU.mult)\
                        .then_inc(state_decayed, 1)
                    dve.wait_ge(sd_mm, t)
                    dve.wait_ge(state_decayed, t)
                    dve.tensor_tensor(stt[:, :, :], stt[:, :, :],
                                      ps[4][:, :].rearrange("p (h c) -> p h c", h=HEADS), ALU.add)\
                        .then_inc(state_ready, 1)
                dve.wait_ge(scores_mm, t * (LV + 1) + 1)
                if some(t):
                    dve.wait_ge(o_mm, t)
                dve.tensor_tensor(sct[:, :, :], ps[1][:, :].rearrange("p (h c) -> p h c", h=HEADS),
                                  ident[:, :].rearrange("p (o c) -> p o c", o=1).to_broadcast([P, HEADS, P]),
                                  ALU.mult).then_inc(scores_in, 1)
                for q in range(1, L + 1):
                    b = halves[q - 1]
                    dve.wait_ge(exps_ready, t * (LV + 3) + q)
                    dve.wait_ge(scores_mm, t * (LV + 1) + max(q - 1, 1))
                    dve.tensor_tensor(blocks(qsc[:, q % 2], b), blocks(qt, 2 * b)[:, :, :, b:],
                                      blocks(ediff[:, q % 2], 2 * b)[:, :, :, b:], ALU.mult)\
                        .then_inc(q_scaled, 1)
                    if q + 2 <= L:
                        diff(q + 2)
                    if q >= 2:
                        take(q - 1)
                odd = L if L % 2 else L - 1
                dve.wait_ge(k_scaled, t * (LV + 2) + odd + 1)
                dve.wait_ge(q_scaled, t * (LV + 1) + odd)
                w = P if prompt else SL
                bv, ev = blocks(bt, w), blocks(ediff[:, 1], w)
                dve.tensor_tensor(ev, bv[:, :, :, w - 1:w].to_broadcast([P, HEADS, P // w, w]), bv, ALU.subtract)\
                    .then_inc(diff_ready, 1)
                take(L)
                dve.wait_ge(exps_ready, t * (LV + 3) + L + 1)
                dve.tensor_tensor(ediff[:, 0], ediff[:, 0], qt, ALU.mult).then_inc(q_scaled, 1)
                if not prompt:
                    dve.wait_ge(v_ready, NT)
                    dve.wait_ge(k_scaled, (NT - 1) * (LV + 2))
                    for h in range(HEADS):
                        dve.tensor_tensor(vms[:, h, 0:SEQ].rearrange("p (q v) -> p q v", q=NS),
                                          vtok[:, h:h + 1, :].to_broadcast([P, NS, P]),
                                          smask[:, :].rearrange("p (q o) -> p q o", o=1).to_broadcast([P, NS, P]),
                                          ALU.mult).then_inc(vm_ready, 1)
                    dve.wait_ge(exps_ready, t * (LV + 3) + L + 3)
                    dve.wait_ge(o_mm, NT)
                    for h in range(HEADS):
                        sv = sin_[:, h, 0:SEQ].rearrange("p (q v) -> p q v", q=NS)
                        dve.tensor_tensor(sv, sv, ebl[:, h, :].rearrange("p (q o) -> p q o", o=1)
                                          .to_broadcast([P, NS, P]), ALU.mult).then_inc(sstate_decayed, 1)
                    for h in range(HEADS):
                        dve.wait_ge(sd_mm, NT + h)
                        dve.wait_ge(sstate_decayed, h + 1)
                        for c in range(2):
                            ins = dve.tensor_tensor(sin_[:, h, c * 512:(c + 1) * 512], ps[4 + c][:, :],
                                                    sin_[:, h, c * 512:(c + 1) * 512], ALU.add)
                        ins.then_inc(sstate_ready, 1)

            tile(0, True)
            with dve.Fori(1, NT - 1) as t:
                tile(t, True)
            tile(NT - 1, False)

            def head_out(h):
                o = work[:, h, :]
                dve.wait_ge(oinv, h + 1)
                dve.scalar_tensor_tensor(o, o, vec[:, V_OUTG:V_OUTG + 1], osq[h][:, :], ALU.mult, ALU.mult)\
                    .then_inc(o_normed, 1)
                dve.wait_ge(o_normed, h + 1)
                dve.wait_ge(g_act, 2)
                dve.tensor_tensor(o, o, work[:, 12 + h, :], ALU.mult).then_inc(o_fin, 1)

            def wide_windows():
                src, width = wide_pad, 1
                dve.wait_ge(pad_ready, 1)
                dve.wait_ge(cinv_ready, 1)
                for k in range(4):
                    dst, lo = wide_sums[k % 2], 2 * width - 1
                    if k:
                        dve.wait_ge(wide_step, k)
                    dve.tensor_tensor(dst[:, lo:PADW], src[:, lo:PADW], src[:, lo - width:PADW - width], ALU.add)\
                        .then_inc(wide_step, 1)
                    src, width = dst, 2 * width

            def pool_group(n):
                gi = POOL_ORDER[n]
                w = POOLW[gi]
                if n:
                    src = sums[SUMS_AT[gi][-1]]
                    dve.wait_ge(sums_ready, n)
                else:
                    src = wide_sums[1]
                    dve.wait_ge(wide_step, 4)
                dve.scalar_tensor_tensor(src[:, HIST:HIST + w - 1], src[:, HIST:HIST + w - 1], float(w),
                                         cinv[:, 0:w - 1], ALU.mult, ALU.mult).then_inc(edge_fixed, 1)
                dve.wait_ge(edge_fixed, n + 1)
                dve.wait_ge(prow_mm, 2)
                tok, own = work[:, 16 + gi, 0:SEQ], work[:, 16 + gi, SEQ:TOK].rearrange("p (q s) -> p q s", q=NS)
                dve.scalar_tensor_tensor(tok, src[:, HIST:HIST + SEQ], 1.0 / w, tok, ALU.mult, ALU.subtract)
                dve.scalar_tensor_tensor(own, src[:, HIST + SEQ:PADW].rearrange("p (q s) -> p q s", q=NS)[:, :, HIST:],
                                         1.0 / w, own, ALU.mult, ALU.subtract).then_inc(pooled_ready, 1)
                for tb in range(NTB):
                    k = NTB * n + tb
                    dve.wait_ge(pool_mm, k + 1)
                    dve.tensor_scalar(work[:, 4 + gi, tbs(tb)], ps[3 + k % 2][:, 0:TB],
                                      vec[:, V_PSC + gi:V_PSC + gi + 1], None, ALU.mult).then_inc(yb_ready, 1)

            def mixed_low(n):
                k = MIXED_ORDER[n]
                dve.wait_ge(mh_ready, n + 1)
                dve.tensor_tensor(ml[:, k, :], work[:, k, :], mh[:, k, :].bitcast(F32), ALU.subtract)\
                    .then_inc(ml_ready, 1)
            wide_windows()
            pool_group(0)
            pool_group(1)
            head_out(0)
            head_out(1)
            head_out(2)
            head_out(3)
            pool_group(2)
            for n in range(3):
                mixed_low(n)
            pool_group(3)
            for n in range(3, KD):
                mixed_low(n)

            n0, g0, t0 = PLAN.at["abo"]

            def abo(i):
                for u in range(2):
                    low(n0 + 4 * i + 2 * u + 1, n0 + 2 * u + 1)
                    low(n0 + 4 * i + 2 * u + 2, n0 + 2 * u + 2)
                    dve.wait_ge(xs_init, 2 * i + (u + 1))
                    for tb in range(NTB):
                        add_down(2 * i + u, tb, g0 + 6 * i + 3 * u + tb, g0 + 3 * u + tb, t0 + 8 * i + 4 * u + 2 + tb)
                    for tb in range(NTB):
                        x_low(24 + 6 * i + 3 * u + tb, 2 * i + u, tb)
            loop(dve, 4, abo)

            def finish_down(n0, g0, t0, k, last, split=0):
                prev = None
                for q in range(4):
                    if q >= split and n0 + q + 1 < PIECES:
                        low(n0 + q + 1, n0 + q + 1)
                    for m in range(6 * q, 6 * q + 6):
                        d, tb = divmod(m, NTB)
                        add_down(d, tb, g0 + m, g0 + m, t0 + m + 1)
                        if not last:
                            if prev is not None:
                                x_low(*prev)
                            prev = (24 * k + m, d, tb)
                if prev is not None:
                    x_low(*prev)

            def ffn(l):
                c3 = convc[:, :]
                cs = conv_step[l]
                done0 = 2 * (STEPS * l + (8 if l else 0))
                for c in range(2):
                    dve.memset(apad[:, c, 0:2], 0.0)

                def conv_unit(c, fc, ch, sg, tick):
                    pad = apad[:, c, :]
                    padp, pads = pad[:, 0:2 + SEQ], pad[:, 2 + SEQ:APW].rearrange("p (q s) -> p q s", q=NS)
                    for tb in range(2):
                        scaled(padp[:, 2 + tb * TB:2 + (tb + 1) * TB], sg + tb, tb, tick + tb)
                    dve.wait_ge(pe_tick, tick + 2)
                    bank = ps[(sg + 2) % BANKS]
                    dve.tensor_tensor(padp[:, 2 + 2 * TB:2 + SEQ], bank[:, 0:256], rstd[:, 2 * TB:SEQ], ALU.mult)
                    dve.tensor_tensor(pads[:, :, 2:], bank[:, 256:TB].rearrange("p (q s) -> p q s", q=NS),
                                      rstd[:, SEQ:TOK].rearrange("p (q s) -> p q s", q=NS), ALU.mult)\
                        .then_inc(acc_free, 1)
                    hist = c3[:, 0:16 * FJ].rearrange("p (q j f) -> p q j f", q=NS, j=2)
                    dve.tensor_scalar(pads[:, :, 0:2], hist[:, :, :, fc].rearrange("p q j o -> p q (j o)"), 1.0, None,
                                      ALU.mult).then_inc(cs, 1)

                def conv_taps(c, fc, ch, g):
                    pad = apad[:, c, :]
                    padp, pads = pad[:, 0:2 + SEQ], pad[:, 2 + SEQ:APW].rearrange("p (q s) -> p q s", q=NS)
                    outp = cv[:, c, 0:SEQ]
                    outs = cv[:, c, SEQ:TOK].rearrange("p (q s) -> p q s", q=NS)
                    col = lambda r: c3[:, ds(fc + r * FJ, 1)]
                    dve.wait_ge(acc_free, g)
                    dve.wait_ge(cs, 9 * ch + 1)
                    if some(ch - 1):
                        dve.wait_ge(y_formed[l], ch - 1)
                    dve.tensor_scalar(outp, padp[:, 0:SEQ], col(16), col(19), ALU.mult, ALU.add).then_inc(cs, 1)
                    dve.tensor_scalar(outs, pads[:, :, 0:SL], col(16), col(19), ALU.mult, ALU.add).then_inc(cs, 1)
                    for j in (1, 2):
                        dve.wait_ge(cs, 9 * ch + 2 * j)
                        dve.scalar_tensor_tensor(outp, padp[:, j:j + SEQ], col(16 + j), outp, ALU.mult, ALU.add)\
                            .then_inc(cs, 1)
                        dve.wait_ge(cs, 9 * ch + 2 * j + 1)
                        dve.scalar_tensor_tensor(outs, pads[:, :, j:j + SL], col(16 + j), outs, ALU.mult, ALU.add)\
                            .then_inc(cs, 1)
                    dve.tensor_scalar(tails[:, 0:2, ds(fc, 1)].rearrange("p r o -> p (r o)"), padp[:, SEQ:SEQ + 2], 1.0,
                                      None, ALU.mult)\
                        .then_inc(cs, 1)
                    dve.tensor_scalar(tails[:, 2:18, ds(fc, 1)].rearrange("p (q j) o -> p q (j o)", q=NS),
                                      pads[:, :, SL:SL + 2], 1.0, None, ALU.mult).then_inc(cs, 1)

                def ups(n, sn, g, sg, tick, s):
                    for u in range(4):
                        if not (u == 1 and isinstance(s, int)):
                            low(n + 2 * u + 1, sn + 2 * u + 1)
                        low(n + 2 * u + 2, sn + 2 * u + 2)
                        if u == 0 and isinstance(s, int):
                            low(n + 3, sn + 3)
                        tk = tick + 4 * u + 2
                        if u == 0 and isinstance(s, int):
                            inv_rms(1 + 2 * l)
                            dve.wait_ge(convc_ready, 1 + l)
                        if u < 2:
                            fc = 2 * s + u
                            conv_unit(u, ds(fc, 1), fc, sg + 3 * u, tk)
                            conv_taps(u, fc, fc, g + 3 * u + 3)
                        else:
                            if some(2 * s + done0):
                                dve.wait_ge(yl_ready, 2 * s + done0)
                            for tb in range(NTB):
                                scaled(gate[:, u - 2, tbs(tb)], sg + 3 * u + tb, tb, tk + tb)

                n0, g0, t0 = PLAN.at[f"f{l}0"]
                ups(n0, n0, g0, g0, t0, 0)
                n1, g1, t1 = PLAN.at[f"f{l}"]

                def step(i):
                    ups(n1 + 12 * i, n1, g1 + 36 * i, g1, t1 + 40 * i, i + 1)
                    for q in range(4):
                        low(n1 + 12 * i + 9 + q, n1 + 9 + q)
                        for m in range(6 * q, 6 * q + 6):
                            d, tb = divmod(m, NTB)
                            add_down(d, tb, g1 + 36 * i + 12 + m, g1 + 12 + m, t1 + 40 * i + 17 + m)
                loop(dve, STEPS - 1, step)
                n2, g2, t2 = PLAN.at[f"f{l}9"]
                finish_down(n2, g2, t2, 2 + 2 * l, l == 1)

            ffn(0)

            n0, g0, t0 = PLAN.at["v"]

            def v_unit(par, n, sn, sg, tick, first=False, second=False):
                if not second:
                    low(n + 1, sn + 1)
                low(n + 2, sn + 2)
                if first:
                    low(n + 3, sn + 3)
                    inv_rms(2)
                for tb in range(NTB):
                    scaled(vtmp[:, par, tbs(tb)], sg + tb, tb, tick + tb)

            def v_turned(j, sg, tick):
                for tb in range(NTB):
                    bank = ps[(sg + tb) % BANKS]
                    dve.wait_ge(pe_tick, tick + tb)
                    for k in range(3):
                        dve.bn_stats(stats[:, 3 * tb + k, ds(j, 1), :], bank[:, k * P:(k + 1) * P])
                    dve.tensor_scalar(work[:, 8 + j, tbs(tb)], bank[:, 0:TB], 1.0, None, ALU.mult)\
                        .then_inc(acc_free, 1)
            v_unit(0, n0, n0, g0, t0 + 2, True)

            def vstep(i, first=False):
                for u in range(2):
                    v_unit(1 - u, n0 + 2 + 4 * i + 2 * u, n0 + 2 + 2 * u, g0 + 3 + 6 * u, t0 + 14 * i + 6 + 7 * u,
                           second=first and u == 0)
                    v_turned(2 * i + u, g0 + 6 + 6 * u, t0 + 14 * i + 9 + 7 * u)
            vstep(0, True)
            with dve.Fori(1, 7) as i:
                vstep(i)
            te = t0 + 4 + 98
            v_unit(1, n0 + 30, n0 + 30, g0 + 87, te + 2)
            dve.wait_ge(tails_stored, 64)
            v_turned(14, g0 + 90, te + 5)
            v_turned(15, g0 + 93, te + 8)
            dve.wait_ge(acc_free, g0 + 96)
            for t in range(NT):
                ins = dve.bn_aggr(mv[:, t, :], stats[:, t, :, :].rearrange("p j s -> p (j s)"))
            ins.then_inc(ln_stats, 1)
            dve.wait_ge(ln_sqrt, 1)
            dve.reciprocal(lrs[:, :], lrs[:, :]).then_inc(ln_stats, 1)
            dve.wait_ge(ln_stats, 2)
            dve.scalar_tensor_tensor(lnb[:, :], mv[:, :, 0], -1.0, lrs[:, :], ALU.mult, ALU.mult)\
                .then_inc(ln_stats, 1)
            for t in (NT - 1, *range(NT - 1 - LN_ACT)):
                v = work[:, 8:24, t * P:(t + 1) * P]
                dve.tensor_scalar(v, v, mv[:, t, 0:1], lrs[:, t:t + 1], ALU.subtract, ALU.mult)\
                    .then_inc(ln_done, 1)

            _, g0, t0 = PLAN.at["mix"]
            dve.wait_ge(wsum_ready, 4)
            dve.wait_ge(bsb_ready, 1)

            def addend(j):
                if j > 1:
                    dve.wait_ge(acc_free, g0 + 3 * (j - 1))
                dve.scalar_tensor_tensor(adde[:, j % 2, :], wsum[:, j // 2, :], vec[:, V_LNB + j:V_LNB + j + 1],
                                         bsb[:, j // 2, :], ALU.mult, ALU.add).then_inc(addend_ready, 1)
            addend(0)
            for j in range(CJ):
                if j + 1 < CJ:
                    addend(j + 1)
                dve.wait_ge(addend_ready, j + 1)
                gain = vec[:, V_LNG + j:V_LNG + j + 1]
                for tb in range(NTB):
                    g = g0 + 3 * j + tb
                    dve.wait_ge(pe_tick, t0 + 3 * j + tb + 1)
                    bank = ps[g % BANKS]
                    if tb == 2 and j == 0:
                        dve.wait_ge(v_out_used, 1)
                    nt = 3 if tb < 2 else 2
                    out = work[:, 8 + j, tb * TB:tb * TB + nt * P].rearrange("p (t c) -> p t c", c=P)
                    ins = dve.scalar_tensor_tensor(
                        out, bank[:, 0:nt * P].rearrange("p (t c) -> p t c", c=P), gain,
                        adde[:, j % 2:j % 2 + 1, 0:P].to_broadcast([P, nt, P]), ALU.mult, ALU.add)
                    if tb == 2:
                        ins = dve.scalar_tensor_tensor(work[:, 8 + j, SEQ:TOK], bank[:, 2 * P:TB], gain,
                                                       adde[:, j % 2, P:2 * P], ALU.mult, ALU.add)
                    ins.then_inc(acc_free, 1)

            def u_groups(s, u, sg, tick, between=None):
                def into(tb):
                    if some(6 * s + 3 * u + tb - 1):
                        dve.wait_ge(u_gated, 6 * s + 3 * u + tb - 1)
                    scaled(ut[:, (3 * u + tb) % 2, :], sg + tb, tb, tick + tb)

                def gated(tb):
                    m = work[:, 8 + 2 * s + u, tbs(tb)]
                    dve.wait_ge(u_activated, 6 * s + 3 * u + tb + 1)
                    dve.tensor_tensor(m, ut[:, (3 * u + tb) % 2, :], m, ALU.mult).then_inc(u_gated, 1)
                into(0)
                into(1)
                if between:
                    between()
                gated(0)
                into(2)
                gated(1)
                gated(2)

            n0, g0, t0 = PLAN.at["u0"]
            done0 = 2 * STEPS
            dve.wait_ge(vout_stored, 16)
            for u in range(2):
                low(n0 + 2 * u + 1, n0 + 2 * u + 1)
                low(n0 + 2 * u + 2, n0 + 2 * u + 2)
                u_groups(0, u, g0 + 3 * u, t0 + 4 * u + 2)
            n1, g1, t1 = PLAN.at["u"]

            def y_low(s, yh=yh, yl=yl):
                for c in range(2):
                    dve.wait_ge(yh_ready, done0 + 2 * s + c + 1)
                    dve.tensor_tensor(yl[:, c, :], work[:, 8 + 2 * s + c, :], yh[:, c, :].bitcast(F32), ALU.subtract)\
                        .then_inc(yl_ready, 1)

            def ustep(i):
                n, t = n1 + 8 * i, t1 + 32 * i
                low(n + 1, n1 + 1)
                low(n + 2, n1 + 2)
                y_low(i)
                u_groups(i + 1, 0, g1, t + 2, lambda: low(n + 3, n1 + 3))
                low(n + 4, n1 + 4)
                u_groups(i + 1, 1, g1 + 3, t + 6, lambda: low(n + 5, n1 + 5))
                for q in range(4):
                    if q:
                        low(n + 5 + q, n1 + 5 + q)
                    for m in range(6 * q, 6 * q + 6):
                        d, tb = divmod(m, NTB)
                        add_down(d, tb, g1 + 30 * i + 6 + m, g1 + 6 + m, t + 9 + m)
                    if q == 0 and isinstance(i, int):
                        y_low(i + 1, yh3, yl3)
            dve.wait_ge(xs_init, 2 * KD)
            loop(dve, 6, ustep)
            ustep(6)
            n2, g2, t2 = PLAN.at["u9"]
            low(n2 + 1, n2 + 1)
            finish_down(n2, g2, t2, 3, False, split=1)

            ffn(1)
            for k in range(24):
                tb, d = divmod(k, KD)
                if d == 0:
                    dve.wait_ge(rms_ready, NTB * 4 + tb + 1)
                    dve.reciprocal(rstd[:, tbs(tb)], rstd[:, tbs(tb)]).then_inc(rstd_ready, 1)
                    dve.wait_ge(rstd_ready, NTB * 4 + tb + 1)
                x = xs[:, d, tbs(tb)]
                dve.scalar_tensor_tensor(x, x, vec[:, V_FIN + d:V_FIN + d + 1], rstd[:, tbs(tb)], ALU.mult, ALU.mult)\
                    .then_inc(y_normed, 1)

        @block.scalar
        def _(act):
            def high(n, s, tick):
                act.wait_ge(w_scaled, n + 1)
                if some(tick):
                    act.wait_ge(pe_tick, tick)
                act.activation(wh[:, s % 2, :], raw[:, s % RAWS, :], ACT.Copy).then_inc(w_high_ready, 1)

            def finished(e, d, tb, g, sq, need_high=True):
                act.wait_ge(acc_free, g + 1)
                if need_high:
                    act.activation(xh[:, d, tbs(tb)], xs[:, d, tbs(tb)], ACT.Copy).then_inc(xh_ready, 1)
                return e

            def squared(e, par, d, tb, sq):
                if some(e - 1):
                    act.wait_ge(ssq_added, e - 1)
                if not isinstance(e, int):
                    act.sem_inc(carried, 1)
                act.activation(sq[:, par, :], xs[:, d, tbs(tb)], ACT.Square).then_inc(square_ready, 1)

            def rms(k):
                for tb in range(NTB):
                    act.wait_ge(norm_mm, NTB * k + tb + 1)
                    act.activation(rstd[:, tbs(tb)], ps[6 + (NTB * k + tb) % 2][:, 0:TB], ACT.Sqrt,
                                   bias=eps_c, scale=1.0 / D).then_inc(rms_ready, 1)

            act.wait_ge(vec_mm, 1)
            act.activation(vec[:, 0:NVEC], ps[6][:, 0:NVEC], ACT.Copy).then_inc(vec_ready, 1)
            for g in range(24):
                tb, d = divmod(g, KD)
                finished(g, d, tb, g, sq_e)
                squared(g, g % 2, d, tb, sq_e)
            n0, g0, t0 = PLAN.at["ab"]
            high(0, 0, 0)
            high(1, 1, 0)
            high(2, 2, t0 + 1)
            high(3, 3, t0 + 4)
            act.wait_ge(eps_ready, 1)
            rms(0)
            high(4, 4, t0 + 5)
            high(5, 5, t0 + 8)

            def q_silu_step(c):
                q = work[:, 2 * c:2 * c + 2, :]
                act.wait_ge(acc_free, g0 + 24)
                act.activation(q, q, ACT.Silu).then_inc(q_act, 1)

            def logf_step(k):
                c = k % 2
                z, f = work[:, 4 + 2 * c:6 + 2 * c, :], work[:, 20 + 2 * c:22 + 2 * c, :]
                if k < 2:
                    act.activation(f, z, ACT.Abs).then_inc(act_prep, 1)
                elif k < 4:
                    act.wait_ge(act_prep, k - 1)
                    act.activation(f, f, ACT.Exp, scale=-1.0).then_inc(act_prep, 1)
                else:
                    act.wait_ge(act_prep, k - 1)
                    act.activation(f, f, ACT.Ln, bias=1.0).then_inc(act_prep, 1)

            def g_silu_step(c):
                g = work[:, 12 + 2 * c:14 + 2 * c, :]
                act.wait_ge(acc_free, g0 + 48)
                act.activation(g, g, ACT.Silu).then_inc(g_act, 1)

            def key_step(c):
                z = work[:, 4 + 2 * c:6 + 2 * c, :]
                act.wait_ge(logf_used, c + 1)
                act.activation(z, z, ACT.Exp).then_inc(k_ready, 1)

            def ab(i, steps=None):
                for p, tk in ((2, 1), (3, 4), (4, 5), (5, 8)):
                    high(n0 + 4 * i + p, n0 + p, t0 + 8 * i + tk)
                    if steps and steps[p - 2]:
                        step, k = steps[p - 2]
                        step(k)
            with act.Fori(1, 4) as i:
                ab(i)
            ab(4, ((q_silu_step, 0), (q_silu_step, 1), (logf_step, 0), (logf_step, 1)))
            ab(5, ((logf_step, 2), (logf_step, 3), (logf_step, 4), (logf_step, 5)))
            ab(6)
            ab(7)
            ab(8, ((g_silu_step, 0), (g_silu_step, 1), (key_step, 0), (key_step, 1)))
            ab(9)

            act.wait_ge(decay_ready, HEADS)

            def tile(t, prompt):
                L = len(HALF[prompt])
                x0 = t * (LV + 3)
                for q in range(1, L + 1):
                    act.wait_ge(diff_ready, t * (LV + 1) + q)
                    act.activation(ediff[:, q % 2], ediff[:, q % 2], ACT.Exp).then_inc(exps_ready, 1)
                    if q == 1:
                        act.wait_ge(v_mm, t + 1)
                        if some(t):
                            act.wait_ge(sd_mm, t)
                        act.activation(vtok[:, :, :], ps[0][:, :].rearrange("p (h c) -> p h c", h=HEADS), ACT.Copy)\
                            .then_inc(v_ready, 1)
                even = L if L % 2 == 0 else L - 1
                act.wait_ge(q_scaled, t * (LV + 1) + even)
                act.wait_ge(k_scaled, t * (LV + 2) + even + 1)
                act.activation(ediff[:, 0], work[:, 20:24, tile_cols(t)], ACT.Exp).then_inc(exps_ready, 1)
                act.wait_ge(diff_ready, t * (LV + 1) + L + 1)
                act.activation(ediff[:, 1], ediff[:, 1], ACT.Exp).then_inc(exps_ready, 1)
                act.wait_ge(state_ready, t + 1)
                if prompt:
                    last = blocks(work[:, 20:24, tile_cols(t)], P)[:, :, :, P - 1]
                    act.activation(ebl[:, :, 0:1], last, ACT.Exp).then_inc(exps_ready, 1)
                else:
                    last = blocks(work[:, 20:24, tile_cols(t)], SL)[:, :, :, SL - 1]
                    act.activation(ebl[:, :, :], last, ACT.Exp).then_inc(exps_ready, 1)
                act.wait_ge(kd_mm, t + 1)
                act.activation(kdt[:, :, :], ps[2][:, :].rearrange("p (h c) -> p h c", h=HEADS), ACT.Copy)\
                    .then_inc(kdt_ready, 1)
                act.wait_ge(o_mm, t + 1)
                act.activation(work[:, 0:4, tile_cols(t)], ps[3][:, :].rearrange("p (h c) -> p h c", h=HEADS),
                               ACT.Copy).then_inc(o_out, 1)

            tile(0, True)
            with act.Fori(1, NT - 1) as t:
                tile(t, True)
            tile(NT - 1, False)

            def head_square(h):
                if h == 1:
                    act.wait_ge(hist_mm, 1)
                if h == 2:
                    act.wait_ge(sstate_ready, HEADS)
                act.activation(osq[h][:, :], work[:, h, :], ACT.Square).then_inc(osq_ready, 1)

            def head_log(h):
                act.wait_ge(onorm_mm, h + 1)
                for tb in range(NTB):
                    act.activation(osq[h][:, tbs(tb)], ps[tb if h % 2 else 5 + tb][:, 0:TB], ACT.Ln,
                                   bias=eps_c, scale=1.0 / P).then_inc(onorm_out, 1)

            def head_inverse(h):
                act.wait_ge(onorm_out, NTB * (h + 1))
                act.activation(osq[h][:, :], osq[h][:, :], ACT.Exp, scale=-0.5).then_inc(oinv, 1)

            def padded(gi):
                pad = wide_pad if gi == 3 else pads[gi % 2]
                own = pad[:, HIST + SEQ:PADW].rearrange("p (q s) -> p q s", q=NS)
                if gi == 2:
                    act.wait_ge(pad_used, 1)
                act.activation(pad[:, HIST:HIST + SEQ], work[:, 16 + gi, 0:SEQ], ACT.Copy)
                act.activation(own[:, :, 0:HIST], histt[:, gi, :].rearrange("p (q s) -> p q s", q=NS), ACT.Copy)
                act.activation(own[:, :, HIST:], work[:, 16 + gi, SEQ:TOK].rearrange("p (q s) -> p q s", q=NS),
                               ACT.Copy).then_inc(pad_ready, 1)

            act.wait_ge(o_out, NT)
            head_square(0)
            act.wait_ge(kd_mm, NT)
            act.wait_ge(hist_mm, 1)
            act.activation(histt[:, :, :], ps[0][:, 0:480].rearrange("p (h c) -> p h c", h=HEADS), ACT.Copy)\
                .then_inc(histt_ready, 1)
            act.wait_ge(histt_ready, 1)
            padded(3)
            head_square(1)
            for r in range(2):
                act.wait_ge(prow_mm, r + 1)
                if r == 0:
                    act.wait_ge(states_stored, 16 * (1 + HEADS))
                act.activation(prow[r][:, :], ps[1 + r][:, :], ACT.Copy).then_inc(prow_ready, 1)
            padded(0)
            padded(1)
            head_square(2)
            head_square(3)
            head_log(0)
            head_log(1)
            head_inverse(0)
            head_inverse(1)
            padded(2)
            head_log(2)
            head_log(3)
            head_inverse(2)
            head_inverse(3)
            act.wait_ge(stored, 16 * (1 + NS))
            for k in MIXED_ORDER:
                if k < HEADS:
                    act.wait_ge(o_fin, HEADS)
                else:
                    act.wait_ge(yb_ready, NTB * (POOL_ORDER.index(k - HEADS) + 1))
                act.activation(mh[:, k, :], work[:, k, :], ACT.Copy).then_inc(mh_ready, 1)

            n0, g0, t0 = PLAN.at["abo"]

            def abo(i):
                for u in range(2):
                    for p, tk in ((2, 1), (3, 4)):
                        high(n0 + 4 * i + 2 * u + p, n0 + 2 * u + p, t0 + 8 * i + 4 * u + tk)
                    for tb in range(NTB):
                        e = 24 + 6 * i + 3 * u + tb
                        finished(e, 2 * i + u, tb, g0 + 6 * i + 3 * u + tb, sq_e)
                        squared(e, (3 * u + tb) % 2, 2 * i + u, tb, sq_e)
            loop(act, 4, abo)

            def finish_down(n0, g0, t0, k, last):
                for q in range(4):
                    if n0 + q + 2 < PIECES:
                        high(n0 + q + 2, n0 + q + 2, t0 + 6 * (q + 1))
                    for m in range(6 * q, 6 * q + 6):
                        d, tb = divmod(m, NTB)
                        finished(24 * k + m, d, tb, g0 + m, sq_b, not last)
                        squared(24 * k + m, m % 2, d, tb, sq_b)

            def ffn(l):
                done0 = 2 * (STEPS * l + (8 if l else 0))
                cs = conv_step[l]

                def y_high(s, yh=yh):
                    for c in range(2):
                        act.wait_ge(y_formed[l], 2 * s + c + 1)
                        act.activation(yh[:, c, :], gate[:, c, :], ACT.Copy).then_inc(yh_ready, 1)

                def gelu(c, ch):
                    act.wait_ge(cs, 9 * ch + 7)
                    act.activation(cv[:, c, :], cv[:, c, :], ACT.Gelu).then_inc(gelu_done[l], 1)

                def ups(n, sn, tick, s):
                    for p, tk in ((2, 1), (3, 4), (4, 5), (5, 8), (6, 9), (7, 12), (8, 13), (9, 16)):
                        high(n + p, sn + p, tick + tk)
                        if p == 3 and isinstance(s, int) and s == 0:
                            rms(1 + 2 * l)
                            act.wait_ge(convc_mm, 1 + l)
                            act.activation(convc[:, :], ps[7][:, 0:440], ACT.Copy).then_inc(convc_ready, 1)
                        if p == (4 if isinstance(s, int) and s == 0 else 3):
                            gelu(0, 2 * s)
                        if p == 5:
                            gelu(1, 2 * s + 1)

                n0, g0, t0 = PLAN.at[f"f{l}0"]
                ups(n0, n0, t0, 0)
                n1, g1, t1 = PLAN.at[f"f{l}"]

                def step(i):
                    y_high(i)
                    ups(n1 + 12 * i, n1, t1 + 40 * i, i + 1)
                    for q in range(4):
                        high(n1 + 12 * i + 10 + q, n1 + 10 + q, t1 + 40 * i + 16 + 6 * (q + 1))
                        if q == 0 and isinstance(i, int):
                            y_high(i + 1, yh2)
                loop(act, STEPS - 2, step)
                step(STEPS - 2)
                n2, g2, t2 = PLAN.at[f"f{l}9"]
                finish_down(n2, g2, t2, 2 + 2 * l, l == 1)

            def tail_rows(l):
                for b, (r0, r1) in enumerate(((0, 44), (44, 172), (172, 300), (300, 396))):
                    if b == 0:
                        act.wait_ge(tails_mm, 1 + l)
                    act.activation(trow[0:r1 - r0, b, :], ps[7][0:r1 - r0, b * P:(b + 1) * P], ACT.Copy)\
                        .then_inc(trow_ready, 1)

            ffn(0)

            n0, g0, t0 = PLAN.at["v"]

            def v_gelu(par, g):
                act.wait_ge(acc_free, g)
                act.activation(vtmp[:, par, :], vtmp[:, par, :], ACT.Gelu).then_inc(v_activated, 1)
            high(n0 + 2, n0 + 2, t0 + 1)
            high(n0 + 3, n0 + 3, t0 + 4)
            rms(2)
            tail_rows(0)
            v_gelu(0, g0 + 3)

            def mixing_matrix(m):
                for b in range(2):
                    act.wait_ge(wt_mm, 2 * m + b + 1)
                    act.activation((wtp, wts)[m][:, 4 * b:4 * b + 4, :],
                                   ps[6 + b][:, :].rearrange("p (j c) -> p j c", c=P), ACT.Copy)\
                        .then_inc(wt_ready, 1)

            def mixing_sums(m):
                for b in range(2):
                    act.wait_ge(wsum_mm, 2 * m + b + 1)
                    act.activation(wsum[:, 4 * b:4 * b + 4, m * P:(m + 1) * P],
                                   ps[6 + b][:, :].rearrange("p (j c) -> p j c", c=P), ACT.Copy)\
                        .then_inc(wsum_ready, 1)

            def vstep(i, between=None):
                n, t, g = n0 + 2 + 4 * i, t0 + 4 + 14 * i, g0 + 3 + 12 * i
                high(n + 2, n0 + 4, t + 1)
                high(n + 3, n0 + 5, t + 4)
                if between:
                    between(0)
                v_gelu(1, g + 3)
                high(n + 4, n0 + 6, t + 8)
                high(n + 5, n0 + 7, t + 11)
                if between:
                    between(1)
                v_gelu(0, g + 9)
            vstep(0)
            vstep(1, mixing_matrix)
            vstep(2, mixing_sums)
            with act.Fori(3, 7) as i:
                vstep(i)
            te = t0 + 4 + 98
            high(n0 + 32, n0 + 32, te + 1)
            high(n0 + 33, n0 + 33, te + 4)
            v_gelu(1, g0 + 90)
            act.wait_ge(ln_stats, 1)
            act.activation(lrs[:, :], mv[:, :, 1], ACT.Sqrt, bias=eps_c).then_inc(ln_sqrt, 1)
            act.wait_ge(ln_stats, 3)
            for t in range(NT - 1 - LN_ACT, NT - 1):
                v = work[:, 8:24, t * P:(t + 1) * P]
                act.activation(v, v, ACT.Identity, bias=lnb[:, t:t + 1], scale=lrs[:, t:t + 1])\
                    .then_inc(ln_act_done, 1)

            n0, g0, t0 = PLAN.at["u0"]
            act.wait_ge(vout_stored, 16)

            def u_gelu(u, g):
                for tb in range(NTB):
                    act.wait_ge(acc_free, g + 3 * u + tb + 1)
                    act.activation(ut[:, (3 * u + tb) % 2, :], ut[:, (3 * u + tb) % 2, :], ACT.Gelu)\
                        .then_inc(u_activated, 1)
            for p, tk in ((2, 1), (3, 4), (4, 5), (5, 8)):
                high(n0 + p, n0 + p, t0 + tk)
                if p in (3, 5):
                    u_gelu((p - 3) // 2, g0)
            n1, g1, t1 = PLAN.at["u"]

            def uy_high(s, yh=yh):
                for c in range(2):
                    act.wait_ge(u_gated, 6 * s + 3 * c + 3)
                    act.activation(yh[:, c, :], work[:, 8 + 2 * s + c, :], ACT.Copy).then_inc(yh_ready, 1)

            def ustep(i):
                uy_high(i)
                for p, tk in ((2, 1), (3, 4), (4, 5), (5, 8)):
                    high(n1 + 8 * i + p, n1 + p, t1 + 32 * i + tk)
                    if p in (3, 5):
                        u_gelu((p - 3) // 2, g1 + 30 * i)
                for q in range(4):
                    high(n1 + 8 * i + 6 + q, n1 + 6 + q, t1 + 32 * i + 8 + 6 * (q + 1))
                    if q == 0 and isinstance(i, int):
                        uy_high(i + 1, yh3)
            loop(act, 6, ustep)
            ustep(6)
            n2, g2, t2 = PLAN.at["u9"]
            finish_down(n2, g2, t2, 3, False)
            ffn(1)
            rms(4)
            tail_rows(1)
            _, g0, t0 = PLAN.at["out"]
            for t in range(NT):
                if t >= 2:
                    act.wait_ge(y_stored[t % 2], 16 * (t // 2))
                for b in range(2):
                    m = 2 * t + b
                    act.wait_ge(pe_tick, t0 + m + 1)
                    act.activation(otok[:, t % 2, b * 512:(b + 1) * 512], ps[(g0 + m) % BANKS][:, :], ACT.Copy)\
                        .then_inc(y_out, 1)

        @block.gpsimd
        def _(pool):
            chain = [0]

            def linked(ins):
                chain[0] += 1
                ins.then_inc(setup_chain, 1)
                pool.wait_ge(setup_chain, chain[0])

            def scale_weights(s, i, per, gain):
                n = per * i + s
                pool.wait_ge(raw_loaded[s % RAWS], 16 * (s // RAWS + 1) + (16 * (per // RAWS)) * i)
                if gain is None:
                    pool.wait_ge(w_scaled, n)
                    pool.sem_inc(w_scaled, 1)
                    return
                r = raw[:, s % RAWS, :].rearrange("p (k c) -> p k c", k=4)
                c = gain + 4 * (s % 2)
                g = vec[:, c:c + 4].rearrange("p (k o) -> p k o", o=1).to_broadcast([P, 4, P])
                pool.tensor_tensor(r, r, g, ALU.mult).then_inc(w_scaled, 1)

            def add_square(e, par, tb, sq, ssq):
                pool.wait_ge(square_ready, e + 1)
                if some(e):
                    pool.wait_ge(ssq_added, e)
                pool.tensor_tensor(ssq[:, tbs(tb)], ssq[:, tbs(tb)], sq[:, par, :], ALU.add)\
                    .then_inc(ssq_added, 1)

            linked(pool.memset(ident[:, :], 0.0))
            pool.affine_select(out=ident[:, :], in_=ident[:, :], compare_op=ALU.not_equal, fill=1.0, base=0,
                               pattern=[[-1, P]], channel_multiplier=1).then_inc(ident_ready, 1)
            pool.memset(ones[:, :], 1.0)
            pool.memset(eps_c, EPS).then_inc(eps_ready, 1)
            linked(pool.memset(ssq_e[:, :], 0.0))
            linked(pool.memset(maskf[:, :, :], 1.0))
            for b, off in MOFF.items():
                m = maskf[:, off, :].rearrange("p (n b) -> p n b", b=b)
                linked(pool.affine_select(out=m, in_=m, compare_op=ALU.is_ge, fill=0.0, base=0,
                                          pattern=[[-2 * b, 64 // b], [0, b]], channel_multiplier=1))
                linked(pool.affine_select(out=m, in_=m, compare_op=ALU.is_ge, fill=0.0, base=b - 1,
                                          pattern=[[2 * b, 64 // b], [0, b]], channel_multiplier=-1))
            pool.tensor_copy(masks[:, :, :], maskf[:, :, :])
            linked(pool.memset(smask[:, :], 1.0))
            linked(pool.affine_select(out=smask[:, :], in_=smask[:, :], compare_op=ALU.is_ge, fill=0.0, base=0,
                                      pattern=[[-SL, NS]], channel_multiplier=1))
            pool.affine_select(out=smask[:, :], in_=smask[:, :], compare_op=ALU.is_ge, fill=0.0, base=SL - 1,
                               pattern=[[SL, NS]], channel_multiplier=-1).then_inc(setup_done, 1)
            n0, _, _ = PLAN.at["ab"]
            for g in range(24):
                add_square(g, g % 2, g // KD, sq_e, ssq_e)
                if g == 15:
                    pool.wait_ge(vec_ready, 1)
                    for p in range(4):
                        scale_weights(n0 + p, 0, 4, V_MIX)

            def ab(i):
                for p in range(4):
                    scale_weights(n0 + p, i, 4, V_MIX)
            pool.wait_ge(rstd_ready, NTB)
            linked(pool.memset(resetm[:, :], 1.0))
            pool.memset(resetm[:, 0:SEQ].rearrange("p (t c) -> p t c", c=P)[:, :, 0:1], 0.0)\
                .then_inc(reset_ready, 1)
            pool.memset(resetm[:, SEQ:TOK].rearrange("p (t c) -> p t c", c=SL)[:, :, 0:1], 0.0)\
                .then_inc(reset_ready, 1)
            pool.memset(ksc[:, 1], 0.0).then_inc(reset_ready, 1)
            with pool.Fori(1, 8) as i:
                ab(i)

            def log_keys(c):
                z, f = work[:, 4 + 2 * c:6 + 2 * c, :], work[:, 20 + 2 * c:22 + 2 * c, :]
                pool.wait_ge(logf_ready, c + 1)
                pool.tensor_tensor(z, f, z, ALU.subtract).then_inc(logf_used, 1)
            for p in range(4):
                scale_weights(n0 + p, 8, 4, V_MIX)
            log_keys(0)
            log_keys(1)
            for p in range(4):
                scale_weights(n0 + p, 9, 4, V_MIX)
            n0, _, _ = PLAN.at["abo"]
            for p in range(4):
                scale_weights(n0 + p, 0, 4, None)
            pool.wait_ge(k_ready, 2)
            pool.wait_ge(reset_ready, 3)

            def tile(t, prompt):
                halves = HALF[prompt]
                L = len(halves)
                kt = work[:, 4:8, tile_cols(t)]
                one = ones[:, :].rearrange("p (o c) -> p o c", o=1).to_broadcast([P, HEADS, P])
                if some(t):
                    pool.wait_ge(v_mm, t)
                pool.tensor_tensor(icp[:, :, :], work[:, 8:12, tile_cols(t)], one, ALU.mult).then_inc(ic_ready, 1)
                if some(t * (LV + 1)):
                    pool.wait_ge(scores_mm, t * (LV + 1))
                pool.tensor_tensor(ksc[:, 0], kt, one, ALU.mult).then_inc(k_scaled, 1)
                for q in range(1, L + 1):
                    b = halves[q - 1]
                    if q > 1:
                        pool.wait_ge(scores_mm, t * (LV + 1) + q - 1)
                    pool.wait_ge(exps_ready, t * (LV + 3) + q)
                    if not isinstance(t, int):
                        pool.sem_inc(carried, 1)
                    pool.tensor_tensor(blocks(ksc[:, q % 2], 2 * b)[:, :, :, 0:b], blocks(kt, 2 * b)[:, :, :, 0:b],
                                       blocks(ediff[:, q % 2], 2 * b)[:, :, :, 0:b], ALU.mult)\
                        .then_inc(k_scaled, 1)
                pool.wait_ge(exps_ready, t * (LV + 3) + L + 2)
                if not isinstance(t, int):
                    pool.sem_inc(carried, 1)
                pool.tensor_tensor(ediff[:, 1], ediff[:, 1], kt, ALU.mult).then_inc(k_scaled, 1)

            tile(0, True)
            with pool.Fori(1, NT - 1) as t:
                tile(t, True)
            tile(NT - 1, False)

            pool.wait_ge(histt_ready, 1)
            linked(pool.memset(wide_pad[:, 0:HIST], 0.0))
            for c in range(15):
                ins = pool.memset(cinv[:, c:c + 1], 1.0 / (c + 1))
            ins.then_inc(cinv_ready, 1)
            pool.wait_ge(states_stored, 16 * (1 + HEADS))
            for pad in pads:
                linked(pool.memset(pad[:, 0:HIST], 0.0))
            steps = 0
            for gi in range(3):
                pool.wait_ge(pad_ready, gi + 2)
                src, width = pads[gi % 2], 1
                for k, place in enumerate(SUMS_AT[gi]):
                    dst = sums[place]
                    lo = 2 * width - 1
                    if k == 1 and gi:
                        pool.wait_ge(pooled_ready, gi + 1)
                    pool.tensor_tensor(dst[:, lo:PADW], src[:, lo:PADW], src[:, lo - width:PADW - width], ALU.add)\
                        .then_inc(window_step, 1)
                    steps += 1
                    pool.wait_ge(window_step, steps)
                    if k == 0:
                        pool.sem_inc(pad_used, 1)
                    src, width = dst, 2 * width
                pool.sem_inc(sums_ready, 1)
            linked(pool.memset(ssq_e[:, :], 0.0))
            for k in range(KD):
                pool.wait_ge(ml_ready, (1, 2, 4, 4)[k] if k < 4 else KD)
                pool.tensor_tensor(xs[:, k, :], xh[:, k, :].bitcast(F32), xl[:, k, :].bitcast(F32), ALU.add)\
                    .then_inc(xs_init, 1)
            n0, _, _ = PLAN.at["abo"]

            def abo(i):
                for u in range(2):
                    for tb in range(NTB):
                        add_square(24 + 6 * i + 3 * u + tb, (3 * u + tb) % 2, tb, sq_e, ssq_e)
            with pool.Fori(0, 3) as i:
                for p in range(4, 8):
                    scale_weights(n0 + p, i, 4, None)
                abo(i)
            n0, _, _ = PLAN.at["f00"]
            for p in range(4):
                scale_weights(n0 + p, 0, 4, V_FFN)
            abo(3)

            def finish_down(n0, k, gain):
                for p in (2, 3):
                    scale_weights(n0 + p, 0, 4, None)
                if gain is not None:
                    for p in (4, 5):
                        scale_weights(n0 + p, 0, 4, gain)
                for q in range(4):
                    for m in range(6 * q, 6 * q + 6):
                        add_square(24 * k + m, m % 2, m % NTB, sq_b, ssq_b)

            def ffn(l):
                done0 = 2 * (STEPS * l + (8 if l else 0))
                gain = V_FFN + KD * l

                def y_prod(s):
                    for c in range(2):
                        pool.wait_ge(gelu_done[l], 2 * s + c + 1)
                        pool.wait_ge(acc_free, g_gate(s, c))
                        pool.tensor_tensor(gate[:, c, :], gate[:, c, :], cv[:, c, :], ALU.mult)\
                            .then_inc(y_formed[l], 1)

                def y_low(s, yh=yh, yl=yl):
                    for c in range(2):
                        pool.wait_ge(yh_ready, 2 * s + c + (done0 + 1))
                        pool.tensor_tensor(yl[:, c, :], gate[:, c, :], yh[:, c, :].bitcast(F32), ALU.subtract)\
                            .then_inc(yl_ready, 1)

                g1 = PLAN.at[f"f{l}"][1]

                def g_gate(s, c):
                    if isinstance(s, int):
                        return PLAN.at[f"f{l}9"][1] - 24 - 3 + 3 * c
                    return s * 36 + (g1 - 3 + 3 * c)

                n0, _, _ = PLAN.at[f"f{l}0"]
                for p in range(2 if l else 4, 8):
                    scale_weights(n0 + p, 0, 4, gain)
                n1, _, _ = PLAN.at[f"f{l}"]
                with pool.Fori(0, STEPS - 1) as i:
                    for p in range(12):
                        scale_weights(n1 + p, i, 12, gain if p < 8 else None)
                        if p == 2:
                            y_prod(i)
                            y_low(i)
                n2, _, _ = PLAN.at[f"f{l}9"]
                y_prod(STEPS - 1)
                y_low(STEPS - 1, yh2, yl2)
                linked(pool.memset(ssq_b[:, :], 0.0))
                scale_weights(n2, 0, 4, None)
                scale_weights(n2 + 1, 0, 4, None)
                finish_down(n2, 2 + 2 * l, V_MIX + KD if l == 0 else None)

            ffn(0)
            n0, _, _ = PLAN.at["v"]
            gain = V_MIX + KD
            scale_weights(n0 + 2, 0, 4, gain)
            scale_weights(n0 + 3, 0, 4, gain)
            pool.wait_ge(acc_free, PLAN.at["v"][1])
            pool.memset(wsn[:, :, :], 0.0).then_inc(wsn_zero, 1)
            pool.wait_ge(ws_loaded, 16 * 9)
            pool.memset(wnat[0:64, :, 64:P], 0.0).then_inc(wnat_masked, 1)
            pool.wait_ge(bs_loaded, 16)
            pool.tensor_copy(bsb[:, :, P:2 * P].rearrange("p g (q s) -> p g q s", q=NS),
                             bsb[:, :, 0:SL].rearrange("p g (o s) -> p g o s", o=1)
                             .to_broadcast([P, 8, NS, SL])).then_inc(bsb_ready, 1)
            with pool.Fori(1, 8) as i:
                for p in range(4):
                    scale_weights(n0 + p, i, 4, gain)
            n0, _, _ = PLAN.at["u0"]
            for p in range(4):
                scale_weights(n0 + p, 0, 4, gain)
            pool.wait_ge(gbc_loaded, 48)
            pool.wait_ge(ln_done, 1)
            nv = work[:, 8:24, SEQ:TOK]
            pool.tensor_tensor(gbc[:, :, :], gbc[:, :, :], nv, ALU.mult).then_inc(v_out_used, 1)
            pool.wait_ge(v_out_used, 1)
            for b in range(2):
                gb = gbc[:, 8 * b:8 * b + 8, :]
                ins = pool.tensor_tensor(gb, gb, bbc[b][:, :, :], ALU.add)
            ins.then_inc(vout_ready, 1)
            pool.wait_ge(acc_free, PLAN.at["mix"][1] + 48)
            for k in range(KD):
                pool.tensor_tensor(xs[:, k, :], xh[:, k, :].bitcast(F32), xl[:, k, :].bitcast(F32), ALU.add)\
                    .then_inc(xs_init, 1)
            n1, _, _ = PLAN.at["u"]
            with pool.Fori(0, 7) as i:
                for p in range(8):
                    scale_weights(n1 + p, i, 8, gain if p < 4 else None)
            n2, _, _ = PLAN.at["u9"]
            scale_weights(n2, 0, 4, None)
            scale_weights(n2 + 1, 0, 4, None)
            pool.wait_ge(u_gated, 48)
            pool.wait_ge(yl_ready, 2 * STEPS + CJ)
            linked(pool.memset(ssq_b[:, :], 0.0))
            finish_down(n2, 3, V_FFN + KD)
            ffn(1)


_INS = ["x_prompt", "x_sample", "state_hgrn", "state_pool", "state_ffn_conv", "norm_mix", "norm_ffn", "norm_final",
        "hgrn_lb_logits", "w_in_ab", "hgrn_out_gain", "pool_w", "pool_scale", "w_out_ab", "w_uv_c", "c_ln_gain",
        "c_ln_bias", "c_ws", "c_bs", "w_out_c", "w_in_ffn", "ffn_conv_w", "ffn_conv_b", "w_out_ffn"]
_OUTS = [("y_prompt", (1, SEQ, D)), ("y_sample", (NS, SL, D)), ("hgrn_prompt", (1, 1, HEADS, P, P)),
         ("hgrn_sample", (1, NS, HEADS, P, P)), ("pool_prompt", (1, 1, HIST, 512)),
         ("pool_sample", (1, NS, HIST, 512)), ("conv_prompt", (2, 1, 2, DFF)), ("conv_sample", (2, NS, 2, DFF)),
         ("cmlp_v", (1, NS, SL, CW))]


def kernel(**inputs):
    import numpy as np
    import concourse.bacc as bacc
    from concourse.bass_utils import run_bass_kernel_spmd

    nc = bacc.Bacc("TRN2", target_bir_lowering=False, num_devices=1, dynamic_dma_scratch_size=64)
    arrays, ins, outs = {}, {}, {}
    for name in _INS:
        a = np.ascontiguousarray(inputs[name])
        arrays[f"in_{name}"] = a
        ins[name] = nc.dram_tensor(f"in_{name}", a.shape, mybir.dt.from_np(a.dtype), kind="ExternalInput").ap()
    for name, shape in _OUTS:
        outs[name] = nc.dram_tensor(f"out_{name}", shape, F32, kind="ExternalOutput").ap()
    build(nc, ins, outs)
    r = run_bass_kernel_spmd(nc, [arrays], core_ids=[0])
    return tuple(r.results[0][f"out_{name}"] for name, _ in _OUTS)
```
